# Optimizing a Trainium2 kernel written in Bass

```python
import math
import numpy as np
import jax
import jax.numpy as jnp
from jax import lax
import jax, jax.numpy as jnp

D_MODEL = 2048
BATCH = 1
SEQ = 256
DEPTH = 1

D_MIX = D_MODEL
SSD_WIDTH = D_MIX // 2
ATT_WIDTH = D_MIX - SSD_WIDTH

SSD_HEAD_DIM = 64
SSD_HEADS = SSD_WIDTH // SSD_HEAD_DIM
SSD_GROUPS = 2
SSD_STATE = 128
SSD_CHUNK = 128
CONV_WIDTH = 4
CONV_CH = SSD_WIDTH + 2 * SSD_GROUPS * SSD_STATE

ATT_HEAD_DIM = 64
ATT_HEADS = ATT_WIDTH // ATT_HEAD_DIM
ATT_KV_HEADS = 4
ATT_GROUP = ATT_HEADS // ATT_KV_HEADS
KV_WIDTH = ATT_KV_HEADS * ATT_HEAD_DIM
CMP_BLOCK = 32
CMP_STRIDE = 16
CMP_HIDDEN = 256
SEL_BLOCK = 64
N_SELECT = 16
WINDOW = 512
Q_BLOCK = 128
N_BRANCH = 3

ROPE_THETA = 500000.0
ROPE_DIM = ATT_HEAD_DIM // 4

D_FF = -((-8 * D_MODEL) // (3 * 256)) * 256

NORM_EPS = 1e-6
NEG_INF = -1e30
FORCE_SCORE = 1e4

IN_WIDTHS = (SSD_WIDTH, CONV_CH, SSD_HEADS, ATT_WIDTH, KV_WIDTH, KV_WIDTH, KV_WIDTH, KV_WIDTH, KV_WIDTH, KV_WIDTH, ATT_HEADS * N_BRANCH)
D_IN = sum(IN_WIDTHS)


def rmsnorm(x, w):
    xf = x.astype(jnp.float32)
    xf = xf * lax.rsqrt(jnp.mean(xf * xf, axis=-1, keepdims=True) + NORM_EPS)
    return xf.astype(x.dtype) * w

def rope_tables(seq, dtype):
    inv = 1.0 / (ROPE_THETA ** (jnp.arange(0, ROPE_DIM, 2, dtype=jnp.float32) / ROPE_DIM))
    ang = jnp.arange(seq, dtype=jnp.float32)[:, None] * inv[None, :]
    return jnp.cos(ang).astype(dtype), jnp.sin(ang).astype(dtype)

def partial_rope(x, cos, sin):
    half = ROPE_DIM // 2
    c = cos[None, :, None, :]
    s = sin[None, :, None, :]
    x1 = x[..., :half]
    x2 = x[..., half:ROPE_DIM]
    return jnp.concatenate([x1 * c - x2 * s, x2 * c + x1 * s, x[..., ROPE_DIM:]], axis=-1)

def causal_depthwise_conv(u, w, b):
    y = lax.conv_general_dilated(u, w[:, None, :].astype(u.dtype), window_strides=(1,), padding=((CONV_WIDTH - 1, 0),), dimension_numbers=('NWC', 'WIO', 'NWC'), feature_group_count=u.shape[-1])
    return y + b

def ssd_chunked(xdt, adt, bm, cm):
    bsz, seq = xdt.shape[:2]
    nc = seq // SSD_CHUNK
    hg = SSD_HEADS // SSD_GROUPS
    x = xdt.reshape(bsz, nc, SSD_CHUNK, SSD_GROUPS, hg, SSD_HEAD_DIM)
    a = adt.reshape(bsz, nc, SSD_CHUNK, SSD_GROUPS, hg)
    b = bm.reshape(bsz, nc, SSD_CHUNK, SSD_GROUPS, SSD_STATE)
    c = cm.reshape(bsz, nc, SSD_CHUNK, SSD_GROUPS, SSD_STATE)
    a_cum = jnp.cumsum(a, axis=2)
    causal = jnp.tril(jnp.ones((SSD_CHUNK, SSD_CHUNK), dtype=bool))[:, :, None, None]
    seg = a_cum[:, :, :, None] - a_cum[:, :, None, :]
    decay = jnp.exp(jnp.where(causal, seg, -jnp.inf))
    cb = jnp.einsum('bclgn,bcsgn->bclsg', c, b)
    y_diag = jnp.einsum('bclsgh,bcsghp->bclghp', cb[..., None] * decay, x)
    decay_states = jnp.exp(a_cum[:, :, -1:] - a_cum)
    states = jnp.einsum('bclgn,bclghp->bcghpn', b, x * decay_states[..., None])
    chunk_decay = jnp.exp(a_cum[:, :, -1])

    def step(h, inp):
        st, dec = inp
        return h * dec[..., None, None] + st, h

    h0 = jnp.zeros_like(states[:, 0])
    _, prev = lax.scan(step, h0, (jnp.moveaxis(states, 1, 0), jnp.moveaxis(chunk_decay, 1, 0)))
    prev = jnp.moveaxis(prev, 0, 1)
    y_off = jnp.einsum('bclgn,bcghpn->bclghp', c, prev) * jnp.exp(a_cum)[..., None]
    return (y_diag + y_off).reshape(bsz, seq, SSD_HEADS, SSD_HEAD_DIM)

def ssd_mixer(z, xbc, dt_raw, conv_w, conv_b, dt_bias, a_log, d_skip, norm_w):
    bsz, seq = z.shape[:2]
    xbc = jax.nn.silu(causal_depthwise_conv(xbc, conv_w, conv_b))
    xs, bm, cm = jnp.split(xbc, [SSD_WIDTH, SSD_WIDTH + SSD_GROUPS * SSD_STATE], axis=-1)
    xh = xs.reshape(bsz, seq, SSD_HEADS, SSD_HEAD_DIM)
    dt = jax.nn.softplus(dt_raw.astype(jnp.float32) + dt_bias.astype(jnp.float32))
    a = -jnp.exp(a_log.astype(jnp.float32))
    y = ssd_chunked(xh * dt[..., None], a * dt, bm.reshape(bsz, seq, SSD_GROUPS, SSD_STATE), cm.reshape(bsz, seq, SSD_GROUPS, SSD_STATE))
    y = y + d_skip[:, None] * xh
    y = y.reshape(bsz, seq, SSD_WIDTH).astype(z.dtype)
    return rmsnorm(y * jax.nn.silu(z), norm_w)

def selection_overlap(n_cmp, n_sel):
    cs = np.arange(n_cmp)[:, None] * CMP_STRIDE
    ce = cs + CMP_BLOCK
    ss = np.arange(n_sel)[None, :] * SEL_BLOCK
    se = ss + SEL_BLOCK
    ov = np.clip(np.minimum(ce, se) - np.maximum(cs, ss), 0, None)
    return (ov / CMP_BLOCK).astype(np.float32)

def compress_tokens(kv, w1, w2, pe):
    bsz, seq = kv.shape[:2]
    n_cmp = (seq - CMP_BLOCK) // CMP_STRIDE + 1
    idx = np.arange(n_cmp)[:, None] * CMP_STRIDE + np.arange(CMP_BLOCK)[None, :]
    blocks = kv[:, idx] + pe[None, None, :, None, :]
    flat = jnp.swapaxes(blocks, 2, 3).reshape(bsz, n_cmp, ATT_KV_HEADS, CMP_BLOCK * ATT_HEAD_DIM)
    return jax.nn.silu(flat @ w1) @ w2

def nsa_mixer(q, kc, vc, ks, vs, kw, vw, gate_raw, cmp_w1_k, cmp_w2_k, cmp_w1_v, cmp_w2_v, cmp_pe_k, cmp_pe_v, cos, sin):
    bsz, seq = q.shape[:2]
    hd = ATT_HEAD_DIM
    scale = hd ** -0.5
    q = q.reshape(bsz, seq, ATT_HEADS, hd)
    kc, vc, ks, vs, kw, vw = [t.reshape(bsz, seq, ATT_KV_HEADS, hd) for t in (kc, vc, ks, vs, kw, vw)]
    q_grp = q.reshape(bsz, seq, ATT_KV_HEADS, ATT_GROUP, hd)
    q_rot = partial_rope(q, cos, sin).reshape(bsz, seq, ATT_KV_HEADS, ATT_GROUP, hd)
    ks = partial_rope(ks, cos, sin)
    kw = partial_rope(kw, cos, sin)
    t_pos = jnp.arange(seq)

    k_cmp = compress_tokens(kc, cmp_w1_k, cmp_w2_k, cmp_pe_k)
    v_cmp = compress_tokens(vc, cmp_w1_v, cmp_w2_v, cmp_pe_v)
    n_cmp = k_cmp.shape[1]
    cmp_end = jnp.arange(n_cmp) * CMP_STRIDE + CMP_BLOCK - 1
    cmp_mask = cmp_end[None, :] <= t_pos[:, None]
    s_cmp = jnp.einsum('bshgd,bihd->bhgsi', q_grp, k_cmp).astype(jnp.float32) * scale
    p_cmp = jax.nn.softmax(jnp.where(cmp_mask, s_cmp, NEG_INF), axis=-1) * cmp_mask
    o_cmp = jnp.einsum('bhgsi,bihd->bshgd', p_cmp.astype(v_cmp.dtype), v_cmp)

    n_sel = seq // SEL_BLOCK
    k_top = min(N_SELECT, n_sel)
    overlap = jnp.asarray(selection_overlap(n_cmp, n_sel))
    imp = jnp.einsum('bhgsi,ij->bhsj', p_cmp, overlap)
    blk = jnp.arange(n_sel)[None, :]
    cur = (t_pos // SEL_BLOCK)[:, None]
    imp = jnp.where((blk == 0) | (blk == cur) | (blk == cur - 1), FORCE_SCORE, imp)
    imp = jnp.where(blk <= cur, imp, -1.0)
    top_val, top_idx = lax.top_k(imp, k_top)
    top_valid = top_val >= 0.0

    ks_blocks = ks.reshape(bsz, n_sel, SEL_BLOCK, ATT_KV_HEADS, hd).transpose(0, 3, 1, 2, 4)
    vs_blocks = vs.reshape(bsz, n_sel, SEL_BLOCK, ATT_KV_HEADS, hd).transpose(0, 3, 1, 2, 4)
    kw_pad = jnp.pad(kw, ((0, 0), (WINDOW, 0), (0, 0), (0, 0)))
    vw_pad = jnp.pad(vw, ((0, 0), (WINDOW, 0), (0, 0), (0, 0)))
    gather_blocks = jax.vmap(jax.vmap(lambda blocks, ix: blocks[ix]))
    q_offs = jnp.arange(Q_BLOCK)
    w_offs = jnp.arange(WINDOW + Q_BLOCK)
    s_offs = jnp.arange(SEL_BLOCK)

    def query_block(qb):
        s0 = qb * Q_BLOCK
        tq = s0 + q_offs
        qblk = lax.dynamic_slice_in_dim(q_rot, s0, Q_BLOCK, axis=1)
        ib = lax.dynamic_slice_in_dim(top_idx, s0, Q_BLOCK, axis=2)
        vb = lax.dynamic_slice_in_dim(top_valid, s0, Q_BLOCK, axis=2)
        kg = gather_blocks(ks_blocks, ib)
        vg = gather_blocks(vs_blocks, ib)
        kpos = ib[..., None] * SEL_BLOCK + s_offs
        m_sel = (kpos <= tq[:, None, None]) & vb[..., None]
        s_sel = jnp.einsum('bqhgd,bhqjkd->bhgqjk', qblk, kg).astype(jnp.float32) * scale
        s_sel = jnp.where(m_sel[:, :, None], s_sel, NEG_INF).reshape(bsz, ATT_KV_HEADS, ATT_GROUP, Q_BLOCK, k_top * SEL_BLOCK)
        p_sel = jax.nn.softmax(s_sel, axis=-1).astype(vg.dtype)
        o_sel = jnp.einsum('bhgqn,bhqnd->bqhgd', p_sel, vg.reshape(bsz, ATT_KV_HEADS, Q_BLOCK, k_top * SEL_BLOCK, hd))
        kwb = lax.dynamic_slice_in_dim(kw_pad, s0, WINDOW + Q_BLOCK, axis=1)
        vwb = lax.dynamic_slice_in_dim(vw_pad, s0, WINDOW + Q_BLOCK, axis=1)
        kp = s0 - WINDOW + w_offs
        dist = tq[:, None] - kp[None, :]
        m_win = (dist >= 0) & (dist < WINDOW) & (kp[None, :] >= 0)
        s_win = jnp.einsum('bqhgd,bkhd->bhgqk', qblk, kwb).astype(jnp.float32) * scale
        p_win = jax.nn.softmax(jnp.where(m_win, s_win, NEG_INF), axis=-1).astype(vwb.dtype)
        o_win = jnp.einsum('bhgqk,bkhd->bqhgd', p_win, vwb)
        return o_sel, o_win

    o_sel, o_win = lax.map(query_block, jnp.arange(seq // Q_BLOCK))
    o_sel = jnp.moveaxis(o_sel, 0, 1).reshape(bsz, seq, ATT_KV_HEADS, ATT_GROUP, hd)
    o_win = jnp.moveaxis(o_win, 0, 1).reshape(bsz, seq, ATT_KV_HEADS, ATT_GROUP, hd)
    g = jax.nn.sigmoid(gate_raw.astype(jnp.float32)).reshape(bsz, seq, ATT_KV_HEADS, ATT_GROUP, N_BRANCH, 1).astype(q.dtype)
    o = g[..., 0, :] * o_cmp + g[..., 1, :] * o_sel + g[..., 2, :] * o_win
    return o.reshape(bsz, seq, ATT_WIDTH)

def first_inputs(seed: int = 0) -> dict:
    key = jax.random.key(seed)
    k = jax.random.split(key, 24)
    f32 = jnp.float32
    L = DEPTH

    def dense(kk, shape, fan_in):
        return jax.random.normal(kk, shape, f32) * fan_in ** -0.5

    def gain(kk, shape):
        return 1.0 + 0.05 * jax.random.normal(kk, shape, f32)

    dt = jnp.exp(jax.random.uniform(k[5], (L, SSD_HEADS), f32, math.log(1e-3), math.log(1e-1)))
    return {
        'x': jax.random.normal(k[0], (BATCH, SEQ, D_MODEL), f32),
        'attn_norm_w': gain(k[1], (L, D_MODEL)),
        'w_in': dense(k[2], (L, D_MODEL, D_IN), D_MODEL),
        'conv_w': dense(k[3], (L, CONV_WIDTH, CONV_CH), CONV_WIDTH),
        'conv_b': 0.01 * jax.random.normal(k[4], (L, CONV_CH), f32),
        'dt_bias': dt + jnp.log(-jnp.expm1(-dt)),
        'a_log': jnp.log(jax.random.uniform(k[6], (L, SSD_HEADS), f32, 1.0, 16.0)),
        'd_skip': 1.0 + 0.1 * jax.random.normal(k[7], (L, SSD_HEADS), f32),
        'ssd_norm_w': gain(k[8], (L, SSD_WIDTH)),
        'cmp_w1_k': dense(k[9], (L, CMP_BLOCK * ATT_HEAD_DIM, CMP_HIDDEN), CMP_BLOCK * ATT_HEAD_DIM),
        'cmp_w2_k': dense(k[10], (L, CMP_HIDDEN, ATT_HEAD_DIM), CMP_HIDDEN),
        'cmp_w1_v': dense(k[11], (L, CMP_BLOCK * ATT_HEAD_DIM, CMP_HIDDEN), CMP_BLOCK * ATT_HEAD_DIM),
        'cmp_w2_v': dense(k[12], (L, CMP_HIDDEN, ATT_HEAD_DIM), CMP_HIDDEN),
        'cmp_pe_k': 0.1 * jax.random.normal(k[13], (L, CMP_BLOCK, ATT_HEAD_DIM), f32),
        'cmp_pe_v': 0.1 * jax.random.normal(k[14], (L, CMP_BLOCK, ATT_HEAD_DIM), f32),
        'w_out': dense(k[15], (L, D_MIX, D_MODEL), D_MIX),
        'ffn_norm_w': gain(k[16], (L, D_MODEL)),
        'w_gate': dense(k[17], (L, D_MODEL, D_FF), D_MODEL),
        'w_up': dense(k[18], (L, D_MODEL, D_FF), D_MODEL),
        'w_down': dense(k[19], (L, D_FF, D_MODEL), D_FF),
        'final_norm_w': gain(k[20], (D_MODEL,)),
    }

def first_block(x, attn_norm_w, w_in, conv_w, conv_b, dt_bias, a_log, d_skip, ssd_norm_w, cmp_w1_k, cmp_w2_k, cmp_w1_v, cmp_w2_v, cmp_pe_k, cmp_pe_v, w_out, ffn_norm_w, w_gate, w_up, w_down, final_norm_w):
    cos, sin = rope_tables(x.shape[1], x.dtype)
    split_at = np.cumsum(IN_WIDTHS)[:-1].tolist()
    h = x
    for l in range(DEPTH):
        u = rmsnorm(h, attn_norm_w[l])
        z, xbc, dt_raw, q, kc, vc, ks, vs, kw, vw, gate_raw = jnp.split(u @ w_in[l], split_at, axis=-1)
        y_ssd = ssd_mixer(z, xbc, dt_raw, conv_w[l], conv_b[l], dt_bias[l], a_log[l], d_skip[l], ssd_norm_w[l])
        y_att = nsa_mixer(q, kc, vc, ks, vs, kw, vw, gate_raw, cmp_w1_k[l], cmp_w2_k[l], cmp_w1_v[l], cmp_w2_v[l], cmp_pe_k[l], cmp_pe_v[l], cos, sin)
        mixed = jnp.concatenate([y_ssd.astype(h.dtype), y_att.astype(h.dtype)], axis=-1)
        h = h + mixed @ w_out[l]
        v = rmsnorm(h, ffn_norm_w[l])
        h = h + (jax.nn.silu(v @ w_gate[l]) * (v @ w_up[l])) @ w_down[l]
    return rmsnorm(h, final_norm_w)


A_HEAD_DIM = 128
A_WIDTH = D_MODEL // 2
A_HEADS = A_WIDTH // A_HEAD_DIM
A_CHUNK = 64
B_HEAD_DIM = 128
B_WIDTH = D_MODEL // 2
B_HEADS = B_WIDTH // B_HEAD_DIM
D_FF_2 = -(-(8 * D_MODEL) // (3 * 256)) * 256
N_IN = 4 * A_WIDTH + 3 * B_WIDTH + B_HEADS + 2 * D_MODEL
RMS_EPS = 1e-6


def _in_split_points():
    sizes = [A_WIDTH] * 4 + [B_WIDTH] * 3 + [B_HEADS, D_MODEL, D_MODEL]
    return [int(v) for v in np.cumsum(sizes)[:-1]]

def rms_norm(x, w):
    xf = x.astype(jnp.float32)
    y = xf * lax.rsqrt(jnp.mean(xf * xf, axis=-1, keepdims=True) + RMS_EPS)
    return (y * w.astype(jnp.float32)).astype(x.dtype)

def hgrn2_mixer(q, f_logit, i, g, lb, norm_w):
    B, S, _ = q.shape
    H, D, C = A_HEADS, A_HEAD_DIM, A_CHUNK
    z = f_logit.astype(jnp.float32)
    lb = lb.astype(jnp.float32)
    log_f = jnp.log(lb + (1.0 - lb) * jax.nn.sigmoid(z))
    k = (1.0 - lb) * jax.nn.sigmoid(-z)

    def to_chunks(t):
        return t.astype(jnp.float32).reshape(B, S // C, C, H, D).transpose(1, 0, 3, 2, 4)

    causal = jnp.tril(jnp.ones((C, C), dtype=bool))[None, None, :, :, None]

    def step(state, inp):
        qc, kc, vc, gc = inp
        b = jnp.cumsum(gc, axis=2)
        o_inter = jnp.einsum('bhtk,bhkv->bhtv', qc * jnp.exp(b), state)
        diff = jnp.where(causal, b[:, :, :, None, :] - b[:, :, None, :, :], -jnp.inf)
        scores = jnp.einsum('bhtsk,bhsk->bhts', qc[:, :, :, None, :] * jnp.exp(diff), kc)
        o_intra = jnp.einsum('bhts,bhsv->bhtv', scores, vc)
        b_last = b[:, :, -1:, :]
        k_dec = kc * jnp.exp(b_last - b)
        new_state = jnp.exp(b_last[:, :, 0, :])[..., None] * state + jnp.einsum('bhsk,bhsv->bhkv', k_dec, vc)
        return new_state, o_inter + o_intra

    state0 = jnp.zeros((B, H, D, D), jnp.float32)
    _, o = lax.scan(step, state0, (to_chunks(q), to_chunks(k), to_chunks(i), to_chunks(log_f)))
    o = o.transpose(1, 0, 3, 2, 4).reshape(B, S, H, D)
    o = rms_norm(o, norm_w) * jax.nn.silu(g.astype(jnp.float32).reshape(B, S, H, D))
    return o.reshape(B, S, A_WIDTH).astype(q.dtype)

def fox_mixer(q, k, v, f_logit):
    B, S, _ = q.shape
    H, D, Qb = B_HEADS, B_HEAD_DIM, Q_BLOCK
    n_blk = S // Qb
    qh = q.reshape(B, S, H, D).transpose(0, 2, 1, 3) * (D ** -0.5)
    kh = k.reshape(B, S, H, D).transpose(0, 2, 1, 3)
    vh = v.reshape(B, S, H, D).transpose(0, 2, 1, 3)
    cum = jnp.cumsum(jax.nn.log_sigmoid(f_logit.astype(jnp.float32)), axis=1).transpose(0, 2, 1)
    q_blocks = qh.reshape(B, H, n_blk, Qb, D).transpose(2, 0, 1, 3, 4)
    c_blocks = cum.reshape(B, H, n_blk, Qb).transpose(2, 0, 1, 3)
    pos_k = jnp.arange(S)

    def block(args):
        idx, q_blk, c_blk = args
        pos_q = idx * Qb + jnp.arange(Qb)
        s = jnp.einsum('bhqd,bhkd->bhqk', q_blk, kh).astype(jnp.float32)
        s = s + c_blk[..., None] - cum[:, :, None, :]
        s = jnp.where((pos_q[:, None] >= pos_k[None, :])[None, None], s, -jnp.inf)
        p = jax.nn.softmax(s, axis=-1)
        return jnp.einsum('bhqk,bhkd->bhqd', p.astype(vh.dtype), vh)

    out = lax.map(block, (jnp.arange(n_blk), q_blocks, c_blocks))
    return out.transpose(1, 0, 3, 2, 4).reshape(B, S, B_WIDTH)

def second_inputs(seed: int = 0) -> dict:
    key = jax.random.key(seed)
    ks = jax.random.split(key, 14)
    f32 = jnp.float32

    def dense(k, fan_in, fan_out):
        return jax.random.normal(k, (DEPTH, fan_in, fan_out), f32) * fan_in ** -0.5

    def gain(k, n):
        return 1.0 + 0.02 * jax.random.normal(k, (DEPTH, n), f32)

    return {
        "x": jax.random.normal(ks[0], (BATCH, SEQ, D_MODEL), f32),
        "w_in": dense(ks[1], D_MODEL, N_IN),
        "b_fox_f": 0.1 * jax.random.normal(ks[2], (DEPTH, B_HEADS), f32),
        "hgrn_lb_logits": jax.random.normal(ks[3], (DEPTH + 1, A_WIDTH), f32),
        "hgrn_norm_w": gain(ks[4], A_HEAD_DIM),
        "w_up_a": dense(ks[5], A_WIDTH, D_MODEL),
        "w_up_b": dense(ks[6], B_WIDTH, D_MODEL),
        "w_o": dense(ks[7], D_MODEL, D_MODEL),
        "norm_mix_pre": gain(ks[8], D_MODEL),
        "norm_mix_post": gain(ks[9], D_MODEL),
        "norm_ffn_pre": gain(ks[10], D_MODEL),
        "norm_ffn_post": gain(ks[11], D_MODEL),
        "w_ffn_in": dense(ks[12], D_MODEL, 2 * D_FF_2),
        "w_ffn_down": dense(ks[13], D_FF_2, D_MODEL),
    }

def second_block(x, w_in, b_fox_f, hgrn_lb_logits, hgrn_norm_w, w_up_a, w_up_b, w_o,
              norm_mix_pre, norm_mix_post, norm_ffn_pre, norm_ffn_post, w_ffn_in, w_ffn_down):
    split_points = _in_split_points()
    lb_table = jnp.cumsum(jax.nn.softmax(hgrn_lb_logits.astype(jnp.float32), axis=0), axis=0)
    for l in range(DEPTH):
        h = rms_norm(x, norm_mix_pre[l])
        proj = h @ w_in[l]
        a_q, a_f, a_i, a_g, b_q, b_k, b_v, b_f, g_a, g_b = jnp.split(proj, split_points, axis=-1)
        y_a = hgrn2_mixer(a_q, a_f, a_i, a_g, lb_table[l], hgrn_norm_w[l]) @ w_up_a[l]
        y_b = fox_mixer(b_q, b_k, b_v, b_f + b_fox_f[l]) @ w_up_b[l]
        merged = jax.nn.sigmoid(g_a) * y_a + jax.nn.sigmoid(g_b) * y_b
        x = x + rms_norm(merged @ w_o[l], norm_mix_post[l])
        h = rms_norm(x, norm_ffn_pre[l])
        gate, up = jnp.split(h @ w_ffn_in[l], 2, axis=-1)
        x = x + rms_norm((jax.nn.silu(gate) * up) @ w_ffn_down[l], norm_ffn_post[l])
    return x


def setup_inputs(seed=0):
    out = dict(first_inputs(seed))
    for name, value in second_inputs(seed + 1).items():
        if name != "x":
            out[name + "_2"] = value
    return out


def reference(
    x, attn_norm_w, w_in, conv_w, conv_b, dt_bias, a_log, d_skip, ssd_norm_w, cmp_w1_k,
    cmp_w2_k, cmp_w1_v, cmp_w2_v, cmp_pe_k, cmp_pe_v, w_out, ffn_norm_w, w_gate, w_up, w_down,
    final_norm_w, w_in_2, b_fox_f_2, hgrn_lb_logits_2, hgrn_norm_w_2, w_up_a_2, w_up_b_2, w_o_2,
    norm_mix_pre_2, norm_mix_post_2, norm_ffn_pre_2, norm_ffn_post_2, w_ffn_in_2, w_ffn_down_2,
):
    x = first_block(
        x, attn_norm_w, w_in, conv_w, conv_b, dt_bias, a_log, d_skip, ssd_norm_w, cmp_w1_k,
        cmp_w2_k, cmp_w1_v, cmp_w2_v, cmp_pe_k, cmp_pe_v, w_out, ffn_norm_w, w_gate, w_up,
        w_down, final_norm_w,
    )
    return second_block(
        x, w_in_2, b_fox_f_2, hgrn_lb_logits_2, hgrn_norm_w_2, w_up_a_2, w_up_b_2, w_o_2,
        norm_mix_pre_2, norm_mix_post_2, norm_ffn_pre_2, norm_ffn_post_2, w_ffn_in_2,
        w_ffn_down_2,
    )


_drawn_inputs = setup_inputs


def setup_inputs(seed=0):
    import zlib

    import numpy as np

    out = dict(_drawn_inputs(seed))
    spreads = {}
    factors = {'conv_b': 3.892,
     'cmp_pe_k': 8.0,
     'b_fox_f_2': 6.386,
     'hgrn_norm_w_2': 6.011,
     'norm_mix_post_2': 3.464,
     'norm_ffn_pre_2': 3.327,
     'norm_ffn_post_2': 4.973}
    for name, (base, spread) in spreads.items():
        noise = np.random.default_rng([zlib.crc32(name.encode()), seed]).standard_normal(out[name].shape)
        drawn = base * np.exp(spread * noise) if base else spread * noise
        out[name] = jnp.asarray(drawn.astype(out[name].dtype))
    for name, factor in factors.items():
        out[name] = (out[name] * factor).astype(out[name].dtype)
    return out
```

```python
import numpy as np

import concourse.bass as bass
from concourse import mybir
from contextlib import ExitStack

P = 128
D = 2048
T = 256
KT = D // P
CH = 512
FF = 5632
NCH = FF // CH
GROUPS = [(0, 4), (4, 8), (8, 11)]
NRAW = 6
NSPL = 4
EPS = 1e-6
NEG = -8e30
LEVELS = [64, 32, 16, 8, 4, 2, 1]

_CONST = [("ident", 128), ("U", 128), ("OS", 256), ("perm", 128), ("cm", 256), ("lev", 1024),
          ("cos", 256), ("sin", 256), ("cadd", 30), ("cmul", 30), ("bd", 8)]
_PARAM = [("anw", 16), ("fnw", 16), ("snw", 8), ("convw", 48), ("convb", 12), ("pek", 32), ("pev", 32),
          ("nmp", 16), ("nfp", 16), ("lb0", 8), ("lb1", 8), ("hnw", 1), ("dtb", 16), ("alog", 16),
          ("dsk", 16), ("bfox", 8), ("w2k", 256), ("w2v", 128)]
OFF = {}
_at = 0
for _n, _w in _CONST + _PARAM:
    OFF[_n] = (_at, _w)
    _at += _w
NCST = _at + _at % 2


class Engine:

    def __init__(self, sem):
        self.sem, self.n, self.queue, self.seen = sem, 0, [], {}

    def do(self, fn, inc=True):
        self.n += inc
        self.queue.append((fn, inc))
        return (self.sem, self.n)

    def wait(self, *marks):
        for m in marks:
            if m is not None and self.seen.get(m[0].name, 0) < m[1]:
                self.seen[m[0].name] = m[1]
                self.queue.append((m, None))

    def last(self):
        return (self.sem, self.n) if self.n else None

    def play(self, eng):
        for fn, inc in self.queue:
            if inc is None:
                eng.wait_ge(fn[0], fn[1])
            else:
                ins = fn(eng)
                if inc:
                    ins.then_inc(self.sem, 1)


def build(nc, ins, out, tap=None):
    F = mybir.dt.float32
    R = mybir.dt.float32r
    I32 = mybir.dt.int32
    ALU = mybir.AluOpType
    ACT = mybir.ActivationFunctionType
    AX = mybir.AxisListType.X
    MUL, ADD, SUB, MAX, MIN = ALU.mult, ALU.add, ALU.subtract, ALU.max, ALU.min

    ctx = ExitStack()
    with ctx:
        def sb(name, shape, dt=F):
            return ctx.enter_context(nc.sbuf_tensor(name, shape, dt))

        def sem(name):
            return ctx.enter_context(nc.semaphore(name))

        raw = sb("raw", [P, NRAW, 1024])
        whi = sb("whi", [P, NSPL, 1024], R)
        wlo = sb("wlo", [P, NSPL, 1024], R)
        xhi = sb("xhi", [P, KT, T], R)
        xlo = sb("xlo", [P, KT, T], R)
        h = sb("h", [P, 2, D])
        scr = sb("scr", [P, 2, D])
        cst = sb("cst", [P, NCST])
        sm = sb("sm", [P, 1024])
        WN = (nc.sbuf_bytes_remaining // 4 - 64) // 2 * 2
        with nc.sbuf_tensor("W", [P, WN], F) as Wt:
            W = Wt
        hhi = sb("hhi", [P, KT, T], R)
        hlo = sb("hlo", [P, KT, T], R)
        ps = ctx.enter_context(nc.psum_tensor("ps", [P, 8, 512], F))

        def C(name, rows=P):
            o, w = OFF[name]
            return cst[0:rows, o:o + w]

        V = Engine(sem("s_dve"))
        A = Engine(sem("s_act"))
        E = Engine(sem("s_pe"))
        S = Engine(sem("s_sp"))
        s_raw = [sem(f"s_raw{i}") for i in range(NRAW)]
        s_x = sem("s_x")
        s_c = sem("s_c")
        s_bc = sem("s_bc")
        s_out = sem("s_out")
        s_pool = sem("s_pool")

        def W_(o, *shape):
            n = int(np.prod(shape))
            ap = W[:, o:o + n]
            if len(shape) == 2:
                return ap.rearrange("p (a b) -> p a b", a=shape[0])
            if len(shape) == 3:
                return ap.rearrange("p (a b c) -> p a b c", a=shape[0], b=shape[1])
            if len(shape) == 4:
                return ap.rearrange("p (a b c d) -> p a b c d", a=shape[0], b=shape[1], c=shape[2])
            return ap

        sm_at = [0]

        def small(*shape):
            n = int(np.prod(shape))
            o = sm_at[0]
            sm_at[0] += n
            ap = sm[:, o:o + n]
            if len(shape) == 2:
                return ap.rearrange("p (a b) -> p a b", a=shape[0])
            return ap

        def bc(ap, axis, shape):
            return ap.unsqueeze(axis).to_broadcast(shape)

        def act(o, i, f=ACT.Copy, w=(), own=True, **kw):
            A.wait(*w)
            if own:
                A.wait(A.last())
            return A.do(lambda e: e.activation(o, i, f, **kw))

        def tt(o, a, b, op, w=(), own=True):
            V.wait(*w)
            if own:
                V.wait(V.last())
            return V.do(lambda e: e.tensor_tensor(o, a, b, op))

        def ts(o, a, s1, s2, op0, op1=None, w=()):
            V.wait(*w, V.last())
            if op1 is None:
                return V.do(lambda e: e.tensor_scalar(o, a, s1, None, op0))
            return V.do(lambda e: e.tensor_scalar(o, a, s1, s2, op0, op1))

        def stt(o, a, s, b, op0, op1, w=()):
            V.wait(*w, V.last())
            return V.do(lambda e: e.scalar_tensor_tensor(out=o, in0=a, scalar=s, in1=b, op0=op0, op1=op1))

        def vdo(fn, w=()):
            V.wait(*w, V.last())
            return V.do(fn)

        def vcopy(o, a, w=()):
            V.wait(*w, V.last())
            return V.do(lambda e: e.tensor_copy(o, a))

        def mm(o, l, r, start=True, stop=True, inc=False, w=(), skip=False):
            E.wait(*w)
            return E.do(lambda e: e.matmul(o, l, r, start=start, stop=stop, skip_group_check=skip), inc)

        def tp(o, i, inc=False, w=()):
            E.wait(*w)
            k = i.shape[0]
            return E.do(lambda e: e.transpose(o, i, C("ident")[0:k, 0:k]), inc)

        class Banks:
            def __init__(self):
                self.free, self.busy, self.at = [[] for _ in range(4)], [False] * 4, 0

            def get(self):
                for _ in range(4):
                    i = self.at
                    self.at = (self.at + 1) % 4
                    if not self.busy[i]:
                        break
                else:
                    raise AssertionError("no bank")
                self.busy[i] = True
                E.wait(*self.free[i])
                return i

            def ap(self, i):
                return ps[:, 4 + i, :]

            def put(self, i, *marks):
                self.busy[i] = False
                self.free[i] = list(marks)

        B = Banks()

        def fence():
            marks = [V.last(), A.last(), E.last()]
            for e in (V, A, E):
                e.wait(*marks)

        items = []

        def item(name, src, kind, ks, ncols, opnd="x", rawonly=False):
            items.append(dict(name=name, src=src, kind=kind, ks=ks, nc=ncols, op=opnd, raw=rawonly))

        def kpairs(a, b):
            return [[k, k + 1] for k in range(a, b, 2)]

        w_in1, w_n1, cmp1, w_outd, gu1, dn1 = (ins[n] for n in ("w_in1", "w_n1", "cmp1", "w_out1", "gu1", "dn1"))
        names = ["k", "q0", "q1", "v", "c", "x0", "x1", "x2", "z0", "z1"]
        kinds = dict(k="feat", q="feat", v="tok", c="feat", x="feat", z="tok")
        for n, nm in enumerate(names):
            item("1" + nm, w_in1[n], kinds[nm[0]], kpairs(0, KT), CH)
            if nm == "v":
                item("1g", w_n1, "tok", [list(range(KT))], 64)
            if nm == "c":
                item("1mk", cmp1[0], "cmp", [list(range(4 * u, 4 * u + 4)) for u in range(4)], 256, rawonly=True)
                item("1mv", cmp1[1], "cmp", [list(range(4 * u, 4 * u + 4)) for u in range(4)], 256, rawonly=True)
        for c in range(4):
            item(f"1o{c}", w_outd[c], "tok", kpairs(0, KT), CH)

        def ffn_items(b, gu, dn):
            for g, (c0, c1) in enumerate(GROUPS):
                for c in range(c0, c1):
                    item(f"{b}fg{c}", gu[0][c], "tok", kpairs(0, KT), CH)
                    item(f"{b}fu{c}", gu[1][c], "tok", kpairs(0, KT), CH)
                for c in range(4):
                    item(f"{b}fd{g}_{c}", dn[c][2 * c0:2 * c1], "tok", kpairs(0, 4 * (c1 - c0)), CH, "h")

        ffn_items(1, gu1, dn1)
        w_in2 = ins["w_in2"]
        names = (["af0", "af1", "aq0", "aq1", "ai0", "ai1", "ag0", "ag1"] + [f"ga{c}" for c in range(4)]
                 + ["bq0", "bq1", "bk0", "bk1", "bv0", "bv1"] + [f"gb{c}" for c in range(4)])
        for n, nm in enumerate(names):
            item("2" + nm, w_in2[n], "feat" if nm[:2] in ("af", "aq", "bq", "bk") else "tok", kpairs(0, KT), CH)
            if nm == "bv1":
                item("2bf", ins["w_n2"], "tok", [list(range(KT))], 8)
        for c in range(4):
            item(f"2ua{c}", ins["w_up"][0][c], "tok", kpairs(0, 8), CH)
            item(f"2ub{c}", ins["w_up"][1][c], "tok", kpairs(8, 16), CH)
        for c in range(4):
            item(f"2o{c}", ins["w_o"][c], "tok", kpairs(0, KT), CH, "h")
        ffn_items(2, ins["gu2"], ins["dn2"])

        units = []
        for it in items:
            it["first"] = len(units)
            for u, ks in enumerate(it["ks"]):
                units.append(dict(item=it, u=u, ks=ks, src=it["src"][u], n=len(ks) * it["nc"]))

        state = dict(dma=0, split=0, nraw={})

        def pump_dma():
            while state["dma"] < len(units):
                j = state["dma"]
                if j >= NRAW:
                    old = units[j - NRAW]
                    if "freed" not in old:
                        return
                    S.wait(*old["freed"])
                u = units[j]
                slot = j % NRAW
                S.queue.append((lambda e, u=u, slot=slot: e.dma_start(raw[:, slot, 0:u["n"]], u["src"]).then_inc(s_raw[slot], 16), False))
                u["landed"] = (s_raw[slot], 16 * (j // NRAW + 1))
                state["dma"] += 1

        split_free = [None] * NSPL

        def pump_split(upto):
            while state["split"] <= min(upto, len(units) - 1):
                j = state["split"]
                state["split"] += 1
                u = units[j]
                if u["item"]["raw"]:
                    continue
                pump_dma()
                s = state["nraw"].setdefault("n", 0) % NSPL
                state["nraw"]["n"] += 1
                u["slot"] = s
                n, r = u["n"], j % NRAW
                hi = act(whi[:, s, 0:n], raw[:, r, 0:n], w=(u["landed"], split_free[s]), own=False)
                lo = tt(wlo[:, s, 0:n], raw[:, r, 0:n], whi[:, s, 0:n].bitcast(F), SUB, w=(hi, split_free[s]), own=False)
                u["hi"], u["lo"] = hi, lo
                split_free[s] = None
                u["freed"] = (hi, lo)
                pump_dma()

        pair_free = [[], []]
        opnd_ready = {"x": [None] * KT, "h": [None] * KT}
        opnds = {"x": (xhi, xlo), "h": (hhi, hlo)}
        later = []

        def due(n):
            for t in [t for t in later if t[0] <= n]:
                later.remove(t)
                t[1]()

        pe_units = [0]
        pair_at = [0]

        def run_item(it, evac):
            pair = pair_at[0] % 2
            pair_at[0] += 1
            banks = [ps[:, 2 * pair, :], ps[:, 2 * pair + 1, :]]
            hi_t, lo_t = opnds[it["op"]]
            nU = len(it["ks"])
            ncol = it["nc"]
            for ui in range(nU):
                gi = it["first"] + ui
                u = units[gi]
                pump_split(gi + NSPL - 1)
                pump_dma()
                if ui == 0:
                    E.wait(*pair_free[pair])
                if it["raw"]:
                    E.wait(u["landed"])
                    w4 = raw[:, gi % NRAW, 0:u["n"]].rearrange("p (k n) -> p k n", n=ncol)
                    kv = 0 if it["name"] == "1mk" else 1
                    for kk, k in enumerate(u["ks"]):
                        for ht in range(2):
                            last = mm(banks[0][:, ht * 60:ht * 60 + 60], w4[:, kk, ht * 128:ht * 128 + 128],
                                      flat[:, kv, k, :], start=(k == 0 and ht == 0), stop=(k == 15),
                                      inc=(kk == len(u["ks"]) - 1 and ht == 1), skip=True,
                                      w=flat_ready if kk == 0 else ())
                    u["freed"] = (last,)
                    pump_dma()
                else:
                    E.wait(u["hi"])
                    s = u["slot"]
                    wh = whi[:, s, 0:u["n"]].rearrange("p (k n) -> p k n", n=ncol)
                    wl = wlo[:, s, 0:u["n"]].rearrange("p (k n) -> p k n", n=ncol)
                    nk = len(u["ks"])
                    for kk, k in enumerate(u["ks"]):
                        E.wait(*(opnd_ready[it["op"]][k] or ()))
                        f0 = ui == 0 and kk == 0
                        l0 = ui == nU - 1 and kk == nk - 1
                        if it["kind"] == "tok":
                            for tb in range(2):
                                o = banks[tb][:, 0:ncol]
                                xh_ = hi_t[:, k, tb * 128:tb * 128 + 128]
                                xl_ = lo_t[:, k, tb * 128:tb * 128 + 128]
                                mm(o, xl_, wh[:, kk, :], start=f0, stop=False)
                                mm(o, xh_, wh[:, kk, :], start=False, stop=False)
                                last = mm(o, xh_, wl[:, kk, :], start=False, stop=l0, w=(u["lo"],),
                                          inc=(kk == nk - 1 and tb == 1))
                        else:
                            for ct in range(4):
                                o = banks[ct // 2][:, (ct % 2) * 256:(ct % 2) * 256 + 256]
                                wh_ = wh[:, kk, ct * 128:ct * 128 + 128]
                                wl_ = wl[:, kk, ct * 128:ct * 128 + 128]
                                mm(o, wh_, hi_t[:, k, :], start=(f0 and ct % 2 == 0), stop=False, skip=True)
                                mm(o, wh_, lo_t[:, k, :], start=False, stop=False, skip=True)
                                last = mm(o, wl_, hi_t[:, k, :], start=False, stop=l0, skip=True, w=(u["lo"],),
                                          inc=(kk == nk - 1 and ct == 3))
                    split_free[s] = last
                pe_units[0] += 1
                if ui == nU - 1:
                    pair_free[pair] = list(evac(it, banks, last))
                due(pe_units[0])
                yield

        item_at = [0]

        def run(names, evac, side=None, ratio=1):
            for nm in names:
                it = items[item_at[0]]
                item_at[0] += 1
                assert it["name"] == nm, (it["name"], nm)
                for _ in run_item(it, evac):
                    for _ in range(ratio):
                        if side is not None:
                            next(side, None)

        def flush():
            for t in list(later):
                later.remove(t)
                t[1]()

        def chain(*gens):
            for g in gens:
                yield from g

        ss = small(2)
        rs = small(2)
        epsc = small(1)

        def rstd(src_of, width, marks, junk):
            A.wait(*marks)
            for tb in range(2):
                act(junk(tb), src_of(tb), ACT.Square, accum_out=ss[:, tb:tb + 1])
            m = ts(rs, ss, 1.0 / width, EPS, MUL, ADD, w=(A.last(), V.last()))
            m = act(rs, rs, ACT.Sqrt, w=(m,))
            V.wait(m)
            return vdo(lambda e: e.reciprocal(rs, rs))

        def to_T(dst, src, wcols, marks):
            hi_t, lo_t = opnds[dst]
            prior = E.last()
            E.wait(*marks)
            for k in range(0, KT, 2):
                b = B.get()
                pb = B.ap(b)
                for j in range(2):
                    for tb in range(2):
                        m = tp(pb[:, j * 256 + tb * 128:j * 256 + tb * 128 + 128], src[:, tb, (k + j) * 128:(k + j) * 128 + 128],
                               inc=(j == 1 and tb == 1))
                evac_split(dst, k, pb, m, wcols, prior)
                B.put(b, A.last(), V.last())

        def evac_split(dst, k, pb, m, wcols, prior):
            hi_t, lo_t = opnds[dst]
            A.wait(prior)
            V.wait(prior)
            if wcols(k) is None:
                pv = pb.rearrange("p (a b) -> p a b", a=2)
                hi = act(hi_t[:, k:k + 2, :], pv, w=(m,))
                lo = tt(lo_t[:, k:k + 2, :], pv, hi_t[:, k:k + 2, :].bitcast(F), SUB, w=(hi,))
            else:
                for j in range(2):
                    hi = act(hi_t[:, k + j, :], pb[:, j * 256:j * 256 + 256], w=(m,), scale=wcols(k + j))
                for j in range(2):
                    lo = stt(lo_t[:, k + j, :], pb[:, j * 256:j * 256 + 256], wcols(k + j), hi_t[:, k + j, :].bitcast(F), MUL, SUB, w=(hi,))
            opnd_ready[dst][k] = opnd_ready[dst][k + 1] = (hi, lo)

        def norm_to_T(dst, wname, marks):
            m = rstd(lambda tb: h[:, tb, :], D, [*marks, E.last()], lambda tb: scr[:, tb, :])
            ms = []
            for tb in range(2):
                ms.append(ts(scr[:, tb, :], h[:, tb, :], rs[:, tb:tb + 1], None, MUL, w=(m, A.last(), E.last())))
            to_T(dst, scr, lambda k: C(wname)[:, k:k + 1], ms)

        G = W_(8192, 2, CH)
        Hb = W_(8192 + 1024, 2, CH)
        bcw = W_(8192 + 2048, D)
        bc_n = [0]

        def load_bcw(i, marks):
            S.wait(*marks)
            bc_n[0] += 1
            S.queue.append((lambda e: e.dma_start(bcw, ins["wb"][i]).then_inc(s_bc, 16), False))
            return (s_bc, 16 * bc_n[0])

        fst = {}

        def ffn(b, acc_first):
            dst = h if b == 1 else scr

            def ev_gate(it, banks, last):
                ms = []
                for tb in range(2):
                    ms.append(act(G[:, tb, :], banks[tb], ACT.Silu, w=(last, fst.get("g_free"))))
                fst["g"] = ms[-1]
                return ms

            def ev_up(it, banks, last):
                c = int(it["name"][3:])
                ms = []
                for tb in range(2):
                    ms.append(tt(Hb[:, tb, :], G[:, tb, :], banks[tb], MUL, w=(last, fst["g"], fst.get("h_free"))))
                fst["g_free"] = ms[-1]
                g0 = [a for a, z in GROUPS if a <= c < z][0]

                def transposes():
                    prior = fst.get("down")
                    for j in range(0, 4, 2):
                        bb = B.get()
                        pb = B.ap(bb)
                        for jj in range(2):
                            for tb in range(2):
                                m = tp(pb[:, jj * 256 + tb * 128:jj * 256 + tb * 128 + 128],
                                       Hb[:, tb, (j + jj) * 128:(j + jj) * 128 + 128], inc=(jj == 1 and tb == 1), w=(ms[-1],))
                        evac_split("h", 4 * (c - g0) + j, pb, m, lambda k: None, prior)
                        B.put(bb, A.last(), V.last())
                    fst["h_free"] = m

                later.append((pe_units[0] + 2, transposes))
                return ms

            def ev_down(it, banks, last):
                c = int(it["name"].split("_")[1])
                g = int(it["name"][3])
                fst["down"] = last
                ms = []
                for tb in range(2):
                    o = dst[:, tb, c * CH:c * CH + CH]
                    if g == 0 and not acc_first:
                        ms.append(act(o, banks[tb], w=(last,)))
                    else:
                        ms.append(tt(o, o, banks[tb], ADD, w=(last, A.last() if g == 1 and not acc_first else None)))
                return ms

            for g, (c0, c1) in enumerate(GROUPS):
                for c in range(c0, c1):
                    run([f"{b}fg{c}"], ev_gate)
                    run([f"{b}fu{c}"], ev_up)
                run([f"{b}fd{g}_{c}" for c in range(4)], ev_down)

        qf = W_(0, 8, T)
        qr = W_(2048, 8, T)
        kr = W_(4096, 4, T)
        vt = W_(5120, 2, CH)
        xT = W_(6144, 12, T)
        sz = W_(9216, 2, 1024)
        kraw = W_(11264, 4, T)
        ckv = W_(12288, 4, T)
        flat = W_(13312, 2, 16, 60)
        hid = W_(15232, 2, 2, 60)
        hrep = W_(15472, 2, 240)
        BD = W_(15952, 2, CH)
        SX = W_(16976, 1024)
        PM = W_(18000, 1024)
        PT = W_(19024, 1024)
        RT = W_(20048, 1024)
        kcT = W_(21072, 60)
        assert 21132 <= WN, WN
        flat_ready = []
        gs = small(2, 48)
        dt = small(2, 16)
        aa = small(2, 16)
        zsum = small(4, 8)
        mnx = small(16)
        wgt = small(16)
        t16a = small(16)
        sp = [small(32) for _ in range(4)]
        ec = small(48)
        R1 = {}

        def cp_banks(dst, ct0):
            def ev(it, banks, last):
                n = int(it["name"][-1]) if it["name"][-1].isdigit() else 0
                ms = []
                for b in range(2):
                    o = dst[:, n * 4 + 2 * b:n * 4 + 2 * b + 2, :]
                    ms.append(act(o, banks[b].rearrange("p (a b) -> p a b", a=2), w=(last,)))
                R1[it["name"]] = ms[-1]
                return ms
            return ev

        def softplus(o, x, n, w, neg=False):
            e, u, z, r = (s[:, 0:n] for s in sp)
            m = ts(u, x, -1.0, None, MUL, w=w)
            m = tt(e, x, u, MAX, w=(m,))
            m = act(e, e, ACT.Exp, scale=-1.0, w=(m,))
            m = ts(u, e, 1.0, None, ADD, w=(m,))
            l = act(r, u, ACT.Ln, w=(m,))
            m = ts(u, u, -1.0, None, ADD, w=(l,))
            m = ts(z, u, 0.0, None, ALU.is_equal, w=(m,))
            m = tt(r, r, z, ADD, w=(m,))
            m2 = tt(u, u, z, ADD, w=(m,))
            V.wait(m2)
            m = vdo(lambda e_: e_.reciprocal(u, u))
            m = tt(r, r, e, MUL, w=(m,))
            m = tt(r, r, u, MUL, w=(m,))
            if neg:
                return stt(o, x, 0.0, r, MIN, SUB, w=(m,))
            return stt(o, x, 0.0, r, MAX, ADD, w=(m,))

        def rope(src, dst, ntile, ready):
            for t in range(0, ntile, 2):
                b = B.get()
                pb = B.ap(b)
                m = mm(pb, C("perm"), src[:, t:t + 2, :].rearrange("p a b -> p (a b)"), inc=True, w=ready)
                c = tt(dst[:, t:t + 2, :], src[:, t:t + 2, :], bc(C("cos"), 1, [P, 2, T]), MUL, w=ready)
                m = tt(RT[:, 0:512].rearrange("p (a b) -> p a b", a=2), pb.rearrange("p (a b) -> p a b", a=2), bc(C("sin"), 1, [P, 2, T]), MUL, w=(m,))
                B.put(b, m)
                m = tt(dst[:, t:t + 2, :], dst[:, t:t + 2, :], RT[:, 0:512].rearrange("p (a b) -> p a b", a=2), ADD, w=(m, c))
                R1["rope"] = m
                yield

        def softmax_scores(S_of, nh, Kn, scale, scores, zout, ready):
            per = 512 // Kn
            banks = [B.get() for _ in range((nh + per - 1) // per)]
            m = None
            for r in range(nh):
                pb = B.ap(banks[r // per])[:, (r % per) * Kn:(r % per) * Kn + Kn]
                m = scores(r, pb)
            mk = C("cm")[:, 256 - Kn:256]
            for r in range(nh):
                pb = B.ap(banks[r // per])[:, (r % per) * Kn:(r % per) * Kn + Kn]
                V.wait(m, R1.get("sx_free"))
                o = SX[:, r * Kn:r * Kn + Kn]
                vdo(lambda e, o=o, pb=pb, r=r: e.tensor_tensor_reduce(
                    out=o, in0=pb, in1=mk, scale=-scale, scalar=3e38, op0=ADD, op1=MIN, accum_out=mnx[:, r:r + 1]))
            for b in banks:
                B.put(b, V.last())
            for r in range(nh):
                o = PM[:, r * Kn:r * Kn + Kn]
                act(o, SX[:, r * Kn:r * Kn + Kn], ACT.Exp, scale=-1.0, bias=mnx[:, r:r + 1],
                    accum_out=zout(r), w=(V.last(), R1.get("pm_free")))
            R1["sx_free"] = A.last()
            R1["pm"] = A.last()

        def transpose_P(nh, Kn):
            nblk = nh * (Kn // 128)
            for q in range(0, nblk, 4):
                b = B.get()
                pb = B.ap(b)
                for j in range(4):
                    m = tp(pb[:, j * 128:j * 128 + 128], PM[:, (q + j) * 128:(q + j) * 128 + 128], inc=(j == 3), w=(R1["pm"],))
                a = act(PT[:, q * 128:q * 128 + 512], pb, w=(m, R1.get("pt_free")))
                B.put(b, a)
            R1["pm_free"] = m
            R1["pt"] = a

        def att_o(tb, hh):
            return scr[:, tb, 1024 + hh * 512:1024 + hh * 512 + 512].rearrange("p (h d) -> p h d", h=8)

        def attention1():
            yield from rope(kraw, kr, 4, (R1["1k"],))
            yield from rope(qf, qr, 8, (R1["1q1"],))
            E.wait(R1["rope"], R1["1v"])
            for tb in range(2):
                Kn = 128 * (tb + 1)
                for br in range(2):
                    for hh in range(2):
                        ob = None
                        for gg in range(2):
                            g = 2 * hh + gg
                            p0 = (g % 2) * 64

                            def scores(r, pb):
                                return mm(pb, qr[p0:p0 + 64, (g // 2) * 4 + r, tb * 128:tb * 128 + 128],
                                          kr[p0:p0 + 64, br * 2 + g // 2, 0:Kn], inc=(r == 3))

                            softmax_scores(None, 4, Kn, 0.125, scores, lambda r: zsum[:, br, 4 * gg + r:4 * gg + r + 1], ())
                            yield
                            transpose_P(4, Kn)
                            yield
                            if ob is None:
                                ob = B.get()
                            po = B.ap(ob)
                            for r in range(4):
                                for kb in range(tb + 1):
                                    q = r * (tb + 1) + kb
                                    m = mm(po[:, (4 * gg + r) * 64:(4 * gg + r) * 64 + 64], PT[:, q * 128:q * 128 + 128],
                                           vt[:, kb, br * 256 + g * 64:br * 256 + g * 64 + 64], start=(kb == 0), stop=(kb == tb),
                                           inc=(r == 3 and kb == tb), w=(R1["pt"],))
                            R1["pt_free"] = m
                            yield
                        V.wait(R1["pm"], R1["1g"])
                        w8 = wgt[:, 0:8]
                        z8 = zsum[:, br, :]
                        vdo(lambda e, z8=z8: e.reciprocal(w8, z8))
                        gv = gs[:, tb, :].rearrange("p (h b) -> p h b", b=3)[:, 8 * hh:8 * hh + 8, br + 1]
                        m2 = tt(w8, w8, gv, MUL, w=(V.last(),))
                        o = att_o(tb, hh)
                        pv = po.rearrange("p (h d) -> p h d", h=8)
                        if br == 0:
                            m2 = tt(o, pv, bc(w8, 2, [P, 8, 64]), MUL, w=(m, m2))
                        else:
                            rt = RT[:, 0:512].rearrange("p (h d) -> p h d", h=8)
                            m2 = tt(rt, pv, bc(w8, 2, [P, 8, 64]), MUL, w=(m, m2))
                            tt(o, o, rt, ADD, w=(m2,))
                        B.put(ob, m2)
                        A.wait(V.last())
                        yield

        def compressed():
            hs = [R1["1mk"], R1["1mv"]]
            b = B.get()
            pb = B.ap(b)
            w2k = C("w2k").rearrange("p (a b) -> p a b", a=2)
            w2v = C("w2v").rearrange("p (a b) -> p a b", a=2)
            for ht in range(2):
                m = mm(pb[:, 0:60], w2k[:, ht, :], hid[:, 0, ht, :], start=(ht == 0), stop=(ht == 1), inc=(ht == 1), w=hs)
            a = act(kcT, pb[:, 0:60], w=(m,))
            B.put(b, a)
            for ht in range(2):
                vcopy(hrep[:, ht, :].rearrange("p (g r i) -> p g r i", g=4, r=4),
                      hid[:, 1, ht, :].rearrange("p (g i) -> p g i", g=4).unsqueeze(2).to_broadcast([P, 4, 4, 15]), w=hs)
            mh = V.last()
            for gp in range(2):
                b = B.get()
                pb = B.ap(b)
                for ht in range(2):
                    m = mm(pb[0:120, 0:64], hrep[:, ht, gp * 120:gp * 120 + 120], w2v[:, ht, :],
                           start=(ht == 0), stop=(ht == 1), inc=(ht == 1), w=(mh,))
                m = tt(BD[0:120, gp, :].rearrange("p (c d) -> p c d", c=8), bc(pb[0:120, 0:64], 1, [120, 8, 64]),
                       bc(C("bd", 120), 2, [120, 8, 64]), MUL, w=(m,))
                B.put(b, m)
            mbd = m
            yield
            for tb in range(2):
                bs = [B.get(), B.get()]
                for par in range(2):
                    for g2 in range(2):
                        for r in range(4):
                            p0, g = par * 64, 2 * g2 + par
                            m = mm(B.ap(bs[par])[:, (4 * g2 + r) * 15:(4 * g2 + r) * 15 + 15], qf[p0:p0 + 64, g2 * 4 + r, tb * 128:tb * 128 + 128],
                                   kcT[p0:p0 + 64, g * 15:g * 15 + 15], inc=(g2 == 1 and r == 3), w=(a,))
                yield
                s = SX[:, 0:240].rearrange("p (h i) -> p h i", i=15)
                s4 = SX[:, 0:240].rearrange("p (a b c) -> p a b c", a=2, b=2)
                e = PM[:, 0:240].rearrange("p (h i) -> p h i", i=15)
                cadd = C("cadd")[:, tb * 15:tb * 15 + 15]
                cmul = C("cmul")[:, tb * 15:tb * 15 + 15]
                for par in range(2):
                    ml = act(s4[:, :, par, :], B.ap(bs[par])[:, 0:120].rearrange("p (a c) -> p a c", a=2), w=(m, R1.get("sx_free")), scale=0.125)
                    B.put(bs[par], ml)
                m = tt(s, s, bc(cadd, 1, [P, 16, 15]), ADD, w=(ml,))
                m = vdo(lambda e_: e_.reduce_max(mnx[:, 0:16], s, AX))
                m = tt(s, s, bc(mnx[:, 0:16], 2, [P, 16, 15]), SUB, w=(m,))
                m = act(e, s, ACT.Exp, w=(m, R1.get("pm_free")))
                R1["sx_free"] = m
                V.wait(m)
                m = vdo(lambda e_: e_.reduce_sum(t16a[:, 0:16], e, AX))
                V.wait(m)
                m = vdo(lambda e_: e_.reciprocal(t16a, t16a))
                gv = gs[:, tb, :].rearrange("p (h b) -> p h b", b=3)[:, :, 0]
                mw = tt(t16a, t16a, gv, MUL, w=(m, R1["1g"]))
                m = tt(e, e, bc(cmul, 1, [P, 16, 15]), MUL, w=(m,))
                yield
                b = B.get()
                pb = B.ap(b)
                for gp in range(2):
                    mt = tp(pb[0:120, gp * 128:gp * 128 + 128], PM[:, gp * 120:gp * 120 + 120], inc=(gp == 1), w=(m,))
                R1["pm_free"] = mt
                m = act(PT[0:120, 0:256], pb[0:120, 0:256], w=(mt, R1.get("pt_free")))
                B.put(b, m)
                yield
                for gp in range(2):
                    b = B.get()
                    pb = B.ap(b)
                    mo = mm(pb, PT[0:120, gp * 128:gp * 128 + 128], BD[0:120, gp, :], inc=True, w=(m, mbd))
                    rt = RT[:, 0:512].rearrange("p (h d) -> p h d", h=8)
                    m2 = tt(rt, pb.rearrange("p (h d) -> p h d", h=8), bc(t16a[:, 8 * gp:8 * gp + 8], 2, [P, 8, 64]), MUL, w=(mo, mw))
                    B.put(b, m2)
                    tt(att_o(tb, gp), att_o(tb, gp), rt, ADD, w=(m2,))
                R1["pt_free"] = mo
                yield

        def flatten():
            pes = [C("pek"), C("pev")]
            m0 = R1["1c"]
            for kv in range(2):
                for hh in range(4):
                    p0 = (hh % 2) * 64
                    src = ckv[p0:p0 + 64, kv * 2 + hh // 2, :].rearrange("p (i j) -> p i j", j=16)
                    for jp in range(2):
                        for q in range(2):
                            o = flat[jp * 64:jp * 64 + 64, kv, 8 * q:8 * q + 8, hh * 15:hh * 15 + 15]
                            i_ = src[:, q:q + 15, jp:16:2].rearrange("p i j -> p j i")
                            pe = pes[kv][p0:p0 + 64, 16 * q + jp:16 * q + 16:2].unsqueeze(2).to_broadcast([64, 8, 15])
                            tt(o, i_, pe, ADD, w=(m0,))
            flat_ready.append(V.last())

        def ev_cmp(it, banks, last):
            kv = 0 if it["name"] == "1mk" else 1
            m = act(hid[:, kv, :, :], banks[0][:, 0:120].rearrange("p (a b) -> p a b", a=2), ACT.Silu, w=(last,))
            R1[it["name"]] = m
            return [m]

        def ev_v(it, banks, last):
            ms = [act(vt[:, tb, :], banks[tb], w=(last,)) for tb in range(2)]
            R1[it["name"]] = ms[-1]
            return ms

        def ev_g1(it, banks, last):
            ms = []
            for tb in range(2):
                m = act(gs[:, tb, :], banks[tb][:, 16:64], ACT.Sigmoid, w=(last,))
                ms.append(tt(dt[:, tb, :], banks[tb][:, 0:16], C("dtb"), ADD, w=(m,)))
            d32 = dt.rearrange("p a b -> p (a b)")
            m = softplus(d32, d32, 32, w=(V.last(),))
            e = act(ec[:, 0:16], C("alog"), ACT.Exp)
            m = ts(ec[:, 0:16], ec[:, 0:16], -1.0, None, MUL, w=(e,))
            tt(aa, dt, bc(ec[:, 0:16], 1, [P, 2, 16]), MUL, w=(m,))
            R1["1g"] = V.last()
            R1["1ga"] = A.last()
            return ms

        def ev_conv(it, banks, last):
            n = int(it["name"][-1])
            ms = []
            cw = C("convw")
            taps = []
            for ct in range(4):
                t = n * 4 + ct
                src = banks[ct // 2][:, (ct % 2) * 256:(ct % 2) * 256 + 256]
                taps.append(act(xT[:, t, :], src, ACT.Identity, scale=cw[:, t * 4 + 3:t * 4 + 4], bias=C("convb")[:, t:t + 1], w=(last,)))
            for ct in range(4):
                t = n * 4 + ct
                src = banks[ct // 2][:, (ct % 2) * 256:(ct % 2) * 256 + 256]
                o = xT[:, t, :]
                m = taps[ct | 1]
                for s in range(1, 4):
                    m = stt(o[:, s:T], src[:, 0:T - s], cw[:, t * 4 + 3 - s:t * 4 + 4 - s], o[:, s:T], MUL, ADD, w=(m,))
                ms.append(m)
            for ct in range(0, 4, 2):
                t = n * 4 + ct
                act(xT[:, t:t + 2, :], xT[:, t:t + 2, :], ACT.Silu, w=(ms[ct + 1],))
            R1[it["name"]] = A.last()
            return ms

        def ev_z(it, banks, last):
            n = int(it["name"][-1])
            ms = [act(sz[:, tb, n * 512:n * 512 + 512], banks[tb], ACT.Silu, w=(last,)) for tb in range(2)]
            R1[it["name"]] = ms[-1]
            return ms

        xs = W_(0, 2, 1024)
        xd = W_(2048, 2, 1024)
        Bt = W_(4096, 256)
        xe = W_(5120, 1024)
        ys = W_(11264, 2, 1024)
        st = W_(13312, 2, 512)
        cbm = W_(14336, 4, 128)
        UA = W_(16976, 4, 128)
        EE = W_(18000, 4, 128)
        MM = W_(19024, 4, 128)

        def ssd():
            fence()
            for tb in range(2):
                for q in range(2):
                    b = B.get()
                    pb = B.ap(b)
                    for j in range(4):
                        m = tp(pb[:, j * 128:j * 128 + 128], xT[:, 4 * q + j, tb * 128:tb * 128 + 128], inc=(j == 3), w=(R1["1x2"],))
                    a = act(xs[:, tb, q * 512:q * 512 + 512], pb, w=(m,))
                    B.put(b, a)
                yield
            b = B.get()
            pb = B.ap(b)
            for g in range(2):
                m = tp(pb[:, g * 128:g * 128 + 128], xT[:, 8 + g, 0:128], inc=(g == 1))
            mb = act(Bt, pb[:, 0:256], w=(m,))
            B.put(b, mb)
            for tb in range(2):
                mx = tt(xd[:, tb, :].rearrange("p (h d) -> p h d", h=16), xs[:, tb, :].rearrange("p (h d) -> p h d", h=16),
                        bc(dt[:, tb, :], 2, [P, 16, 64]), MUL, w=(a,))
            b = B.get()
            pb = B.ap(b)
            mm(pb[:, 0:16], C("OS")[:, 128:256], aa[:, 0, :], w=(R1["1g"],))
            m = mm(pb[:, 16:32], C("U"), aa[:, 1, :], inc=True)
            m = act(ec[:, 16:48], pb[:, 0:32], ACT.Exp, w=(m,))
            B.put(b, m)
            yield
            mxe = tt(xe.rearrange("p (h d) -> p h d", h=16), xd[:, 0, :].rearrange("p (h d) -> p h d", h=16),
                     bc(ec[:, 16:32], 2, [P, 16, 64]), MUL, w=(m, mx))
            for g in range(2):
                b = B.get()
                pb = B.ap(b)
                m = mm(pb, Bt[:, g * 128:g * 128 + 128], xe[:, g * 512:g * 512 + 512], inc=True, w=(mxe, mb))
                a = act(st[:, g, :], pb, w=(m,))
                B.put(b, a)
            yield
            for g in range(2):
                b = B.get()
                pb = B.ap(b)
                m = mm(pb, xT[:, 10 + g, 128:256], st[:, g, :], inc=True, w=(a,))
                m = tt(ys[:, 1, g * 512:g * 512 + 512].rearrange("p (h d) -> p h d", h=8), pb.rearrange("p (h d) -> p h d", h=8),
                       bc(ec[:, 32 + 8 * g:40 + 8 * g], 2, [P, 8, 64]), MUL, w=(m,))
                B.put(b, m)
            b = B.get()
            pb = B.ap(b)
            for c in range(2):
                for g in range(2):
                    m = mm(pb[:, (2 * c + g) * 128:(2 * c + g) * 128 + 128], xT[:, 8 + g, c * 128:c * 128 + 128],
                           xT[:, 10 + g, c * 128:c * 128 + 128], inc=(c == 1 and g == 1))
            mcb = tt(cbm, pb.rearrange("p (a b) -> p a b", a=4), bc(C("U"), 1, [P, 4, 128]), MUL, w=(m,))
            B.put(b, mcb)
            yield
            seg_free = m_free = None
            for c in range(2):
                for g in range(2):
                    ob = B.get()
                    po = B.ap(ob)
                    for hq in range(2):
                        h0 = 8 * g + 4 * hq
                        mu = tt(UA, bc(C("U"), 1, [P, 4, 128]), bc(aa[:, c, h0:h0 + 4], 2, [P, 4, 128]), MUL, w=(seg_free,))
                        b = B.get()
                        pb = B.ap(b)
                        seg_free = mm(pb, C("OS")[:, 128:256], UA.rearrange("p a b -> p (a b)"), inc=True, w=(mu,))
                        me = act(EE, pb.rearrange("p (a b) -> p a b", a=4), ACT.Exp, w=(seg_free, V.last()))
                        B.put(b, me)
                        mk = tt(MM, EE, bc(cbm[:, 2 * c + g, :], 1, [P, 4, 128]), MUL, w=(me, m_free, mcb))
                        yield
                        for r in range(4):
                            hd = h0 + r
                            m_free = mm(po[:, (4 * hq + r) * 64:(4 * hq + r) * 64 + 64], MM[:, r, :], xd[:, c, hd * 64:hd * 64 + 64],
                                        inc=(r == 3), w=(mk, mx))
                        yield
                    yv = ys[:, c, g * 512:g * 512 + 512]
                    if c == 0:
                        m = vcopy(yv, po, w=(m_free,))
                    else:
                        m = tt(yv, yv, po, ADD, w=(m_free, V.last()))
                    B.put(ob, m)
            for tb in range(2):
                m = tt(xs[:, tb, :].rearrange("p (h d) -> p h d", h=16), xs[:, tb, :].rearrange("p (h d) -> p h d", h=16),
                       bc(C("dsk"), 2, [P, 16, 64]), MUL, w=(mx,))
                m = tt(ys[:, tb, :], ys[:, tb, :], xs[:, tb, :], ADD, w=(m,))
                R1[f"y{tb}"] = m
            yield

        def ssd_finish():
            for tb in range(2):
                m = tt(ys[:, tb, :], ys[:, tb, :], sz[:, tb, :], MUL, w=(R1[f"y{tb}"], R1["1z1"]))
            m = rstd(lambda tb: ys[:, tb, :], 1024, [m, E.last()], lambda tb: xs[:, tb, :])
            ms = []
            for tb in range(2):
                ms.append(ts(scr[:, tb, 0:1024], ys[:, tb, :], rs[:, tb:tb + 1], None, MUL, w=(m,)))
            return ms

        S0 = 8192
        aq = W_(S0, 8, T)
        ab = W_(S0 + 2048, 8, T)
        ak = W_(S0 + 4096, 8, T)
        ai = W_(S0 + 6144, 2, 1024)
        AM = W_(S0 + 8192, 8, 128)
        A2 = W_(S0 + 9216, 4, 128)
        DD = W_(S0 + 9728, 4, T)
        QE = W_(S0 + 10752, 4, T)
        KE = W_(S0 + 11776, 4, T)
        assert S0 + 12800 <= WN, WN
        sg = W_(0, 4, 4, CH)
        lbt = small(3, 8)

        def lower_bounds():
            l0, l1 = C("lb0"), C("lb1")
            m = tt(lbt[:, 0, :], l0, l1, MAX)
            a = tt(lbt[:, 1, :], l0, lbt[:, 0, :], SUB, w=(m,))
            b = tt(lbt[:, 2, :], l1, lbt[:, 0, :], SUB, w=(m,))
            a = act(lbt[:, 1:3, :], lbt[:, 1:3, :], ACT.Exp, w=(b,))
            m = tt(lbt[:, 2, :], lbt[:, 1, :], lbt[:, 2, :], ADD, w=(a,))
            V.wait(m)
            m = vdo(lambda e: e.reciprocal(lbt[:, 2, :], lbt[:, 2, :]))
            m = tt(lbt[:, 0, :], lbt[:, 1, :], lbt[:, 2, :], MUL, w=(m,))
            m = ts(lbt[:, 1, :], lbt[:, 0, :], -1.0, 1.0, MUL, ADD, w=(m,))
            A.wait(m)

        def ev_af(it, banks, last):
            n = int(it["name"][-1])
            ms = []
            for b in range(2):
                t = n * 4 + 2 * b
                pv = banks[b].rearrange("p (a b) -> p a b", a=2)
                act(ab[:, t:t + 2, :], pv, ACT.Sigmoid, w=(last,))
                ms.append(act(ak[:, t:t + 2, :], pv, ACT.Sigmoid, scale=-1.0))
            mk = ms[-1]
            for t in range(n * 4, n * 4 + 4):
                ts(ak[:, t, :], ak[:, t, :], lbt[:, 1, t:t + 1], None, MUL, w=(mk,))
                act(ab[:, t, :], ab[:, t, :], ACT.Ln, scale=lbt[:, 1, t:t + 1], bias=lbt[:, 0, t:t + 1], w=(mk,))
                V.wait(A.last())
                vdo(lambda e, t=t: e.tensor_tensor_scan(ab[:, t, :], ones256, ab[:, t, :], 0.0, MUL, ADD))
            R1[it["name"]] = V.last()
            return ms

        ones256 = None

        def ev_t1024(dst, func=ACT.Copy):
            def ev(it, banks, last):
                n = int(it["name"][-1])
                ms = [act(dst[:, tb, n * 512:n * 512 + 512], banks[tb], func, w=(last,)) for tb in range(2)]
                R1[it["name"]] = ms[-1]
                return ms
            return ev

        def ev_ga(which):
            def ev(it, banks, last):
                n = int(it["name"][-1])
                ms = []
                for tb in range(2):
                    o = W[:, which * 4096 + n * 1024 + tb * 512:which * 4096 + n * 1024 + tb * 512 + 512]
                    ms.append(act(o, banks[tb], ACT.Sigmoid, w=(last,)))
                R1[it["name"]] = ms[-1]
                return ms
            return ev

        gsil = scr[:, :, 1024:2048]

        def hgrn():
            E.wait(R1["2ai1"])
            mz = vdo(lambda e: e.memset(AM, 0.0))
            V.wait(mz)
            o_free = None
            for hg in range(2):
                h0 = 4 * hg
                V.wait(E.last())
                vdo(lambda e: e.memset(AM, 0.0))
                vdo(lambda e: e.memset(QE, 0.0))
                mz = vdo(lambda e: e.memset(KE, 0.0))
                qe_free = None
                for li, m_ in enumerate([0, 128] + LEVELS):
                    if m_ == 0:
                        ql, kl, me = aq[:, h0:h0 + 4, :], ak[:, h0:h0 + 4, :], R1["2aq1"]
                    else:
                        nb = T // (2 * m_)

                        def v(ap):
                            return ap.rearrange("p h (n s m) -> p (h n) s m", s=2, m=m_)

                        bv = v(ab[:, h0:h0 + 4, :])
                        dv = v(DD)
                        anc = bv[:, :, 0, m_ - 1].unsqueeze(2).to_broadcast([P, 4 * nb, m_])
                        tt(dv[:, :, 1, :], bv[:, :, 1, :], anc, SUB, w=(V.last(),))
                        md = tt(dv[:, :, 0, :], anc, bv[:, :, 0, :], SUB)
                        me = act(DD, DD, ACT.Exp, w=(md,))
                        tt(v(QE)[:, :, 1, :], v(aq[:, h0:h0 + 4, :])[:, :, 1, :], dv[:, :, 1, :], MUL, w=(me, qe_free, mz))
                        me = tt(v(KE)[:, :, 0, :], v(ak[:, h0:h0 + 4, :])[:, :, 0, :], dv[:, :, 0, :], MUL)
                        ql, kl = QE, KE
                    if m_ == 128:
                        b = B.get()
                        pb = B.ap(b)
                        for r in range(4):
                            m = mm(pb[:, r * 128:r * 128 + 128], kl[:, r, 0:128], ql[:, r, 128:256], inc=(r == 3), w=(me,))
                        qe_free = m
                        m = vcopy(A2, pb.rearrange("p (a b) -> p a b", a=4), w=(m,))
                        B.put(b, m)
                    else:
                        bs = [B.get(), B.get()]
                        lix = 0 if m_ == 0 else 1 + LEVELS.index(m_)
                        mask = C("lev")[:, lix * 128:lix * 128 + 128].bitcast(I32)
                        for c in range(2):
                            pb = B.ap(bs[c])
                            for r in range(4):
                                m = mm(pb[:, r * 128:r * 128 + 128], kl[:, r, c * 128:c * 128 + 128], ql[:, r, c * 128:c * 128 + 128],
                                       inc=(r == 3), w=(me,))
                        qe_free = m
                        for c in range(2):
                            pb = B.ap(bs[c])
                            V.wait(m, mz, V.last())
                            vdo(lambda e, c=c, pb=pb, mask=mask: e.copy_predicated(
                                AM[:, 4 * c:4 * c + 4, :], bc(mask, 1, [P, 4, 128]), pb.rearrange("p (a b) -> p a b", a=4)))
                            B.put(bs[c], V.last())
                    yield
                ma = V.last()
                for c in range(2):
                    b = B.get()
                    pb = B.ap(b)
                    for r in range(4):
                        hd = h0 + r
                        o = pb[:, r * 128:r * 128 + 128]
                        m = mm(o, AM[:, 4 * c + r, :], ai[:, c, hd * 128:hd * 128 + 128], start=True, stop=(c == 0), w=(ma,),
                               inc=(r == 3 and c == 0))
                        if c == 1:
                            m = mm(o, A2[:, r, :], ai[:, 0, hd * 128:hd * 128 + 128], start=False, stop=True, inc=(r == 3))
                    pv = pb.rearrange("p (h d) -> p h d", h=4)
                    sq = DD.rearrange("p a b -> p (a b)")[:, 0:512].rearrange("p (h d) -> p h d", h=4)
                    a = act(sq, pv, ACT.Square, w=(m, V.last()))
                    V.wait(a)
                    m = vdo(lambda e: e.reduce_sum(t16a[:, 0:4], sq, AX))
                    m = ts(t16a[:, 0:4], t16a[:, 0:4], 1.0 / 128, EPS, MUL, ADD, w=(m,))
                    m = act(t16a[:, 0:4], t16a[:, 0:4], ACT.Sqrt, w=(m,))
                    V.wait(m)
                    m = vdo(lambda e: e.reciprocal(t16a[:, 0:4], t16a[:, 0:4]))
                    o = scr[:, c, h0 * 128:h0 * 128 + 512].rearrange("p (h d) -> p h d", h=4)
                    m = tt(o, pv, bc(t16a[:, 0:4], 2, [P, 4, 128]), MUL, w=(m,))
                    B.put(b, m)
                    R1[f"o{hg}{c}"] = m
                    yield

        def hgrn_gate():
            for c in range(2):
                R1[f"oa{c}"] = tt(scr[:, c, 0:1024], scr[:, c, 0:1024], gsil[:, c, :], MUL, w=(R1[f"o1{c}"], R1["2ag1"]))

        bq = aq
        bk = ab
        bv_ = W_(S0 + 4096, 2, 1024)
        lf = small(2, 8)
        LU = W_(S0 + 8192, 2, 4, 128)
        assert sm_at[0] <= 1024

        def ev_feat(dst, scale):
            def ev(it, banks, last):
                n = int(it["name"][-1])
                ms = []
                for b in range(2):
                    o = dst[:, n * 4 + 2 * b:n * 4 + 2 * b + 2, :]
                    ms.append(act(o, banks[b].rearrange("p (a b) -> p a b", a=2), w=(last,), scale=scale))
                R1[it["name"]] = ms[-1]
                return ms
            return ev

        def ev_bf(it, banks, last):
            ms = []
            for tb in range(2):
                ms.append(tt(lf[:, tb, :], banks[tb][:, 0:8], C("bfox"), ADD, w=(last,)))
            l16 = lf.rearrange("p a b -> p (a b)")
            softplus(l16, l16, 16, w=(ms[-1],), neg=True)
            R1["2bf"] = V.last()
            return ms

        SX2 = W_(S0 + 9216, 1024)
        PM2 = W_(S0 + 10240, 1024)
        PT2 = W_(S0 + 11264, 1024)

        def fox():
            nonlocal SX, PM, PT
            SX, PM, PT = SX2, PM2, PT2
            R1["sx_free"] = R1["pm_free"] = R1["pt_free"] = None
            E.wait(R1["2bv1"])
            for tb in range(2):
                Kn = 128 * (tb + 1)
                for hq in range(2):
                    for q in range(2):
                        hs = [4 * hq + 2 * q, 4 * hq + 2 * q + 1]
                        if q == 0:
                            V.wait(E.last(), R1["2bf"])
                            lu = tt(LU[:, 0, :, :], bc(C("U"), 1, [P, 4, 128]), bc(lf[:, tb, 4 * hq:4 * hq + 4], 2, [P, 4, 128]), MUL)
                            if tb:
                                lu = tt(LU[:, 1, :, :], bc(C("OS")[:, 0:128], 1, [P, 4, 128]), bc(lf[:, 0, 4 * hq:4 * hq + 4], 2, [P, 4, 128]), MUL)

                        def scores(r, pb):
                            hd = hs[r]
                            mm(pb, bq[:, hd, tb * 128:tb * 128 + 128], bk[:, hd, 0:Kn], start=True, stop=False, w=(lu,))
                            if tb:
                                mm(pb[:, 0:128], LU[:, 1, 2 * q + r, :], C("OS")[:, 128:256], start=False, stop=False)
                            return mm(pb, LU[:, 0, 2 * q + r, :], C("OS")[:, 256 - Kn:256], start=False, stop=True, inc=(r == 1))

                        softmax_scores(None, 2, Kn, 1.0, scores, lambda r: zsum[:, 0, 2 * q + r:2 * q + r + 1], ())
                        yield
                        nblk = 2 * (tb + 1)
                        b = B.get()
                        pb = B.ap(b)
                        for j in range(nblk):
                            m = tp(pb[:, j * 128:j * 128 + 128], PM[:, j * 128:j * 128 + 128], inc=(j == nblk - 1), w=(R1["pm"],))
                        a = act(PT[:, 0:nblk * 128], pb[:, 0:nblk * 128], w=(m, R1.get("pt_free")))
                        B.put(b, a)
                        R1["pm_free"] = m
                        yield
                        if q == 0:
                            ob = B.get()
                            po = B.ap(ob)
                        for r in range(2):
                            for kb in range(tb + 1):
                                m = mm(po[:, (2 * q + r) * 128:(2 * q + r) * 128 + 128], PT[:, (r * (tb + 1) + kb) * 128:(r * (tb + 1) + kb) * 128 + 128],
                                       bv_[:, kb, hs[r] * 128:hs[r] * 128 + 128], start=(kb == 0), stop=(kb == tb),
                                       inc=(r == 1 and kb == tb), w=(a,))
                        R1["pt_free"] = m
                    V.wait(R1["pm"])
                    mr = vdo(lambda e: e.reciprocal(wgt[:, 0:4], zsum[:, 0, 0:4]))
                    o = scr[:, tb, 1024 + hq * 512:1024 + hq * 512 + 512].rearrange("p (h d) -> p h d", h=4)
                    m = tt(o, po.rearrange("p (h d) -> p h d", h=4), bc(wgt[:, 0:4], 2, [P, 4, 128]), MUL, w=(m, mr))
                    B.put(ob, m)
                    A.wait(m)
                    R1["fox"] = m
                    yield

        def ev_ua(it, banks, last):
            n = int(it["name"][-1])
            ms = []
            for tb in range(2):
                s_ = W[:, n * 1024 + tb * 512:n * 1024 + tb * 512 + 512]
                ms.append(tt(s_, s_, banks[tb], MUL, w=(last, R1[f"2ga{n}"])))
            return ms

        def ev_ub(it, banks, last):
            n = int(it["name"][-1])
            ms = []
            for tb in range(2):
                sa = W[:, n * 1024 + tb * 512:n * 1024 + tb * 512 + 512]
                s_ = W[:, 4096 + n * 1024 + tb * 512:4096 + n * 1024 + tb * 512 + 512]
                o = scr[:, tb, n * 512:n * 512 + 512]
                m = tt(s_, s_, banks[tb], MUL, w=(last, R1[f"2gb{n}"]))
                ms.append(m)
                R1[f"mg{n}"] = tt(o, s_, sa, ADD, w=(m, V.last(), R1["o_T"]))

            def transposes():
                for j in range(0, 4, 2):
                    bb = B.get()
                    pb = B.ap(bb)
                    for jj in range(2):
                        for tb in range(2):
                            m = tp(pb[:, jj * 256 + tb * 128:jj * 256 + tb * 128 + 128],
                                   scr[:, tb, n * 512 + (j + jj) * 128:n * 512 + (j + jj) * 128 + 128], inc=(jj == 1 and tb == 1), w=(R1[f"mg{n}"],))
                    evac_split("h", 4 * n + j, pb, m, lambda k: None, V.last())
                    B.put(bb, A.last(), V.last())

            later.append((pe_units[0] + 2, transposes))
            return ms

        def ev_acc(dst, add):
            def ev(it, banks, last):
                n = int(it["name"][-1])
                ms = []
                for tb in range(2):
                    o = dst[:, tb, n * 512:n * 512 + 512]
                    ms.append(tt(o, o, banks[tb], ADD, w=(last,)) if add else act(o, banks[tb], w=(last, E.last())))
                R1["acc"] = ms[-1]
                return ms
            return ev

        def post_norm(widx, marks):
            mb = load_bcw(widx, marks)
            junk = W_(0, 2, D)
            m = rstd(lambda tb: scr[:, tb, :], D, [*marks, V.last(), E.last()], lambda tb: junk[:, tb, :])
            for tb in range(2):
                m1 = stt(scr[:, tb, :], scr[:, tb, :], rs[:, tb:tb + 1], bcw, MUL, MUL, w=(m, mb, A.last()))
                m2 = tt(h[:, tb, :], h[:, tb, :], scr[:, tb, :], ADD, w=(m1,))
            return m2

        for tb in range(2):
            S.queue.append((lambda e, tb=tb: e.dma_start(h[:, tb, :], ins["x"][tb]).then_inc(s_x, 16), False))
        S.queue.append((lambda e: e.dma_start(cst[:, :], ins["cst"]).then_inc(s_c, 16), False))
        mx, mc = (s_x, 32), (s_c, 16)
        pump_dma()
        A.wait(mx)
        V.wait(mx)
        E.wait(mc)
        A.wait(mc)
        V.wait(mc)
        norm_to_T("x", "anw", [mx])

        run(["1k"], cp_banks(kraw, 0))
        run(["1q0", "1q1"], cp_banks(qf, 0))
        run(["1v"], ev_v)
        run(["1g"], ev_g1)
        att = attention1()
        run(["1c"], cp_banks(ckv, 0), att)
        flatten()
        run(["1mk", "1mv"], ev_cmp, att)
        run(["1x0", "1x1", "1x2"], ev_conv, att)
        side = chain(att, compressed(), ssd())
        run(["1z0", "1z1"], ev_z, side)
        for _ in side:
            pass
        ms = ssd_finish()
        to_T("x", scr, lambda k: C("snw")[:, k:k + 1] if k < 8 else None, [*ms, V.last()])
        run([f"1o{c}" for c in range(4)], ev_acc(h, True))
        fence()
        norm_to_T("x", "fnw", [R1["acc"]])
        ffn(1, True)
        flush()
        fence()

        mb = load_bcw(0, [V.last()])
        m = rstd(lambda tb: h[:, tb, :], D, [V.last(), E.last()], lambda tb: scr[:, tb, :])
        for tb in range(2):
            m2 = stt(h[:, tb, :], h[:, tb, :], rs[:, tb:tb + 1], bcw, MUL, MUL, w=(m, mb, A.last()))
        lower_bounds()
        norm_to_T("x", "nmp", [m2])
        ones256 = C("OS")[:, 0:1].to_broadcast([P, T])
        fence()
        run(["2af0", "2af1"], ev_af)
        run(["2aq0", "2aq1"], ev_feat(aq, 1.0))
        run(["2ai0", "2ai1"], ev_t1024(ai))
        side = hgrn()
        run(["2ag0", "2ag1"], ev_t1024(gsil, ACT.Silu), side)
        run([f"2ga{c}" for c in range(4)], ev_ga(0), side)
        for _ in side:
            pass
        hgrn_gate()
        fence()
        run(["2bq0", "2bq1"], ev_feat(bq, 128.0 ** -0.5))
        run(["2bk0", "2bk1"], ev_feat(bk, 1.0))
        run(["2bv0", "2bv1"], ev_t1024(bv_))
        run(["2bf"], ev_bf)
        side = fox()
        run([f"2gb{c}" for c in range(4)], ev_ga(1), side)
        for _ in side:
            pass
        to_T("x", scr, lambda k: C("hnw") if k < 8 else None, [V.last()])
        R1["o_T"] = E.last()
        for c in range(4):
            run([f"2ua{c}"], ev_ua)
            run([f"2ub{c}"], ev_ub)
        flush()
        fence()
        run([f"2o{c}" for c in range(4)], ev_acc(scr, False))
        fence()
        m = post_norm(1, [R1["acc"]])
        norm_to_T("x", "nfp", [m])
        ffn(2, False)
        flush()
        fence()
        m = post_norm(2, [V.last()])
        S.wait(m)
        for tb in range(2):
            S.queue.append((lambda e, tb=tb: e.dma_start(out[tb], h[:, tb, :]).then_inc(s_out, 16), False))
        S.wait((s_out, 32))
        assert item_at[0] == len(items) and state["dma"] == len(units)

        with nc.Block() as block:
            @block.sync
            def _(e):
                S.play(e)

            @block.scalar
            def _(e):
                A.play(e)

            @block.vector
            def _(e):
                V.play(e)

            @block.tensor
            def _(e):
                E.play(e)


def constants():
    f = np.float32
    j = np.arange(128)
    c = np.zeros((128, sum(w for _, w in _CONST)), f)

    def put(name, a):
        o, w = OFF[name]
        c[:a.shape[0], o:o + w] = a.reshape(a.shape[0], -1)

    put("ident", np.eye(128, dtype=f))
    put("U", (j[:, None] <= j[None, :]).astype(f))
    SU = (j[:, None] > j[None, :]).astype(f)
    put("OS", np.concatenate([np.ones((128, 128), f), SU], 1))
    d = j % 64
    perm = np.zeros((128, 128), f)
    for m in range(128):
        if d[m] < 8:
            perm[m + 8, m] = 1
        elif d[m] < 16:
            perm[m - 8, m] = 1
    put("perm", perm)
    put("cm", np.concatenate([np.zeros((128, 128), f), np.where(j[None, :] > j[:, None], f(NEG), f(0))], 1))
    lev = np.zeros((8, 128, 128), f)
    lev[0] = np.eye(128)
    for i, m in enumerate(LEVELS):
        s, t = j[:, None], j[None, :]
        lev[1 + i] = (s // (2 * m) == t // (2 * m)) & (s % (2 * m) < m) & (t % (2 * m) >= m)
    put("lev", lev.transpose(1, 0, 2).reshape(128, -1))
    inv = (f(1.0) / (f(500000.0) ** (np.arange(0, 16, 2, dtype=f) / f(16)))).astype(f)
    ang = (np.arange(T, dtype=f)[:, None] * inv[None, :]).astype(f)
    cos, sin = np.cos(ang).astype(f), np.sin(ang).astype(f)
    ct, st = np.ones((128, T), f), np.zeros((128, T), f)
    for m in range(128):
        if d[m] < 8:
            ct[m], st[m] = cos[:, d[m]], -sin[:, d[m]]
        elif d[m] < 16:
            ct[m], st[m] = cos[:, d[m] - 8], sin[:, d[m] - 8]
    put("cos", ct)
    put("sin", st)
    t = np.arange(T).reshape(2, 128)
    ok = (np.arange(15) * 16 + 31)[None, None, :] <= t[:, :, None]
    put("cadd", np.where(ok, f(0), f(-1e30)).transpose(1, 0, 2))
    put("cmul", ok.astype(f).transpose(1, 0, 2))
    put("bd", (np.arange(120)[:, None] // 15 == np.arange(8)[None, :]).astype(f))
    return c


def pack(w, chunks):
    k = w.shape[0]
    return np.ascontiguousarray(w.reshape(k // 256, 2, 128, chunks, CH).transpose(3, 0, 2, 1, 4)).reshape(chunks, k // 256, 128, 2 * CH)


def narrow(w):
    n = w.shape[1]
    return np.ascontiguousarray(w.reshape(16, 128, n).transpose(1, 0, 2)).reshape(1, 128, 16 * n)


def feat(v, n):
    return v.reshape(n, 128).T


def rep(v):
    return np.broadcast_to(v.reshape(1, -1), (128, v.size))


def kernel(**inputs):
    import concourse.bacc as bacc
    from concourse.bass_utils import run_bass_kernel_spmd

    a = {k: np.asarray(v) for k, v in inputs.items()}
    w = a["w_in"][0]
    z, xbc, dtr, q, kc, vc, ks, vs, kw, vw, gate = np.split(w, np.cumsum([1024, 1536, 16, 1024] + [256] * 6), axis=1)
    order = [h for i in range(2) for r in range(4) for h in (8 * i + r, 8 * i + 4 + r)]
    q = q.reshape(D, 16, 64)[:, order, :].reshape(D, 1024)
    w1 = np.concatenate([ks, kw, q, vs, vw, kc, vc, xbc, z], axis=1)
    w2 = a["w_in_2"][0]
    aq, af, ai, ag, bq, bk, bv, bf, ga, gb = np.split(w2, np.cumsum([1024] * 7 + [8, 2048]), axis=1)
    w2p = np.concatenate([af, aq, ai, ag, ga, bq, bk, bv, gb], axis=1)
    cw = a["conv_w"][0]
    cols = [constants(), feat(a["attn_norm_w"][0], 16), feat(a["ffn_norm_w"][0], 16), feat(a["ssd_norm_w"][0], 8),
            cw.reshape(4, 12, 128).transpose(2, 1, 0).reshape(128, 48), feat(a["conv_b"][0], 12)]
    for n in ("cmp_pe_k", "cmp_pe_v"):
        pe = a[n][0].T
        cols.append(np.concatenate([pe, pe], axis=0))
    cols += [feat(a["norm_mix_pre_2"][0], 16), feat(a["norm_ffn_pre_2"][0], 16), feat(a["hgrn_lb_logits_2"][0], 8),
             feat(a["hgrn_lb_logits_2"][1], 8), a["hgrn_norm_w_2"][0].reshape(128, 1), rep(a["dt_bias"][0]), rep(a["a_log"][0]),
             rep(a["d_skip"][0]), rep(a["b_fox_f_2"][0])]
    k2 = a["cmp_w2_k"][0].reshape(2, 128, 64).transpose(1, 0, 2)
    v2 = a["cmp_w2_v"][0].reshape(2, 128, 64).transpose(1, 0, 2)
    cols += [np.concatenate([k2, k2], axis=2).reshape(128, 256), v2.reshape(128, 128)]
    n = sum(c.shape[1] for c in cols)
    cols.append(np.zeros((128, NCST - n), np.float32))
    arrays = {
        "x": a["x"].reshape(2, 128, D),
        "cst": np.concatenate(cols, axis=1),
        "wb": np.stack([rep(a["final_norm_w"]), rep(a["norm_mix_post_2"][0]), rep(a["norm_ffn_post_2"][0])]),
        "w_in1": pack(w1, 10),
        "w_n1": narrow(np.concatenate([dtr, gate], axis=1)),
        "cmp1": np.stack([a[n][0].reshape(4, 4, 128, 256).transpose(0, 2, 1, 3).reshape(4, 128, 1024) for n in ("cmp_w1_k", "cmp_w1_v")]),
        "w_out1": pack(a["w_out"][0], 4),
        "gu1": np.stack([pack(a["w_gate"][0], NCH), pack(a["w_up"][0], NCH)]),
        "dn1": pack(a["w_down"][0], 4),
        "w_in2": pack(w2p, 22),
        "w_n2": narrow(bf),
        "w_up": np.stack([pack(a["w_up_a_2"][0], 4), pack(a["w_up_b_2"][0], 4)]),
        "w_o": pack(a["w_o_2"][0], 4),
        "gu2": np.stack([pack(a["w_ffn_in_2"][0][:, :FF], NCH), pack(a["w_ffn_in_2"][0][:, FF:], NCH)]),
        "dn2": pack(a["w_ffn_down_2"][0], 4),
    }
    arrays = {"in_" + k: np.ascontiguousarray(v) for k, v in arrays.items()}
    nc = bacc.Bacc("TRN2", target_bir_lowering=False, num_devices=1, dynamic_dma_scratch_size=1024)
    ins = {k[3:]: nc.dram_tensor(k, v.shape, mybir.dt.float32, kind="ExternalInput").ap() for k, v in arrays.items()}
    out = nc.dram_tensor("out_x", (2, 128, D), mybir.dt.float32, kind="ExternalOutput").ap()
    build(nc, ins, out)
    r = run_bass_kernel_spmd(nc, [arrays], core_ids=[0])
    return r.results[0]["out_x"].reshape(1, T, D)
```

```python
import numpy as np

import concourse.bass as bass
from concourse import mybir
from contextlib import ExitStack

P = 128
D = 2048
T = 256
KT = D // P
CH = 512
FF = 5632
NCH = FF // CH
GROUPS = [(0, 4), (4, 8), (8, 11)]
NRAW = 5
NSPL = 4
EPS = 1e-6
NEG = -8e30
LEVELS = [64, 32, 16, 8, 4, 2, 1]

_CONST = [("ident", 128), ("U", 128), ("OS", 256), ("perm", 128), ("cm", 256), ("lev", 1024),
          ("cos", 256), ("sin", 256), ("cadd", 30), ("cmul", 30), ("bd", 8)]
_PARAM = [("anw", 16), ("fnw", 16), ("snw", 8), ("convw", 48), ("convb", 12), ("pek", 32), ("pev", 32),
          ("nmp", 16), ("nfp", 16), ("lb0", 8), ("lb1", 8), ("hnw", 1), ("dtb", 16), ("alog", 16),
          ("dsk", 16), ("bfox", 8), ("fnl", 16), ("w2k", 256), ("w2v", 128)]
NPAR = sum(w for _, w in _PARAM)
OFF = {}
_at = 0
for _n, _w in _PARAM + _CONST:
    OFF[_n] = (_at, _w)
    _at += _w
NCST = _at


class Engine:

    def __init__(self, sem):
        self.sem, self.n, self.queue, self.seen = sem, 0, [], {}

    def do(self, fn, inc=True):
        self.n += inc
        self.queue.append((fn, inc))
        return (self.sem, self.n)

    def wait(self, *marks):
        for m in marks:
            if m is not None and self.seen.get(m[0].name, 0) < m[1]:
                self.seen[m[0].name] = m[1]
                self.queue.append((m, None))

    def last(self):
        return (self.sem, self.n) if self.n else None

    def play(self, eng):
        for fn, inc in self.queue:
            if inc is None:
                eng.wait_ge(fn[0], fn[1])
            else:
                ins = fn(eng)
                if inc:
                    ins.then_inc(self.sem, 1)


def build(nc, ins, out, tap=None):
    F = mybir.dt.float32
    R = mybir.dt.float32r
    I32 = mybir.dt.int32
    ALU = mybir.AluOpType
    ACT = mybir.ActivationFunctionType
    AX = mybir.AxisListType.X
    MUL, ADD, SUB, MAX, MIN = ALU.mult, ALU.add, ALU.subtract, ALU.max, ALU.min

    ctx = ExitStack()
    with ctx:
        def sb(name, shape, dt=F):
            return ctx.enter_context(nc.sbuf_tensor(name, shape, dt))

        def sem(name):
            return ctx.enter_context(nc.semaphore(name))

        raw = sb("raw", [P, NRAW, 1024])
        whi = sb("whi", [P, NSPL, 1024], R)
        wlo = sb("wlo", [P, NSPL, 1024], R)
        xhi = sb("xhi", [P, KT, T], R)
        xlo = sb("xlo", [P, KT, T], R)
        h = sb("h", [P, 2, D])
        scr = sb("scr", [P, 2, D])
        cst = sb("cst", [P, NCST])
        sm = sb("sm", [P, 1280])
        RB = sb("RB", [P, T])
        WN = (nc.sbuf_bytes_remaining // 4 - 64) // 2 * 2
        with nc.sbuf_tensor("W", [P, WN], F) as Wt:
            W = Wt
        hhi = sb("hhi", [P, KT, T], R)
        hlo = sb("hlo", [P, KT, T], R)
        ps = ctx.enter_context(nc.psum_tensor("ps", [P, 8, 512], F))

        def C(name, rows=P):
            o, w = OFF[name]
            return cst[0:rows, o:o + w]

        V = Engine(sem("s_dve"))
        A = Engine(sem("s_act"))
        E = Engine(sem("s_pe"))
        S = Engine(sem("s_sp"))
        s_raw = [sem(f"s_raw{i}") for i in range(NRAW)]
        s_x = sem("s_x")
        s_c = sem("s_c")
        s_bc = sem("s_bc")
        s_out = sem("s_out")
        s_k = sem("s_k")
        s_keep = sem("s_keep")

        def W_(o, *shape):
            n = int(np.prod(shape))
            ap = W[:, o:o + n]
            if len(shape) == 2:
                return ap.rearrange("p (a b) -> p a b", a=shape[0])
            if len(shape) == 3:
                return ap.rearrange("p (a b c) -> p a b c", a=shape[0], b=shape[1])
            if len(shape) == 4:
                return ap.rearrange("p (a b c d) -> p a b c d", a=shape[0], b=shape[1], c=shape[2])
            return ap

        sm_at = [0]

        def small(*shape):
            n = int(np.prod(shape))
            o = sm_at[0]
            sm_at[0] += n
            ap = sm[:, o:o + n]
            if len(shape) == 2:
                return ap.rearrange("p (a b) -> p a b", a=shape[0])
            return ap

        def bc(ap, axis, shape):
            return ap.unsqueeze(axis).to_broadcast(shape)

        def act(o, i, f=ACT.Copy, w=(), own=True, **kw):
            A.wait(*w)
            if own:
                A.wait(A.last())
            return A.do(lambda e: e.activation(o, i, f, **kw))

        def tt(o, a, b, op, w=(), own=True):
            V.wait(*w)
            if own:
                V.wait(V.last())
            return V.do(lambda e: e.tensor_tensor(o, a, b, op))

        def ts(o, a, s1, s2, op0, op1=None, w=()):
            V.wait(*w, V.last())
            if op1 is None:
                return V.do(lambda e: e.tensor_scalar(o, a, s1, None, op0))
            return V.do(lambda e: e.tensor_scalar(o, a, s1, s2, op0, op1))

        def stt(o, a, s, b, op0, op1, w=(), own=True):
            V.wait(*w, V.last() if own else None)
            return V.do(lambda e: e.scalar_tensor_tensor(out=o, in0=a, scalar=s, in1=b, op0=op0, op1=op1))

        def vdo(fn, w=()):
            V.wait(*w, V.last())
            return V.do(fn)

        def vcopy(o, a, w=()):
            V.wait(*w, V.last())
            return V.do(lambda e: e.tensor_copy(o, a))

        def mm(o, l, r, start=True, stop=True, inc=False, w=(), skip=False):
            E.wait(*w)
            return E.do(lambda e: e.matmul(o, l, r, start=start, stop=stop, skip_group_check=skip), inc)

        def tp(o, i, inc=False, w=()):
            E.wait(*w)
            k = i.shape[0]
            return E.do(lambda e: e.transpose(o, i, C("ident")[0:k, 0:k]), inc)

        class Banks:
            def __init__(self):
                self.free, self.busy, self.at = [[] for _ in range(4)], [False] * 4, 0

            def get(self):
                for _ in range(4):
                    i = self.at
                    self.at = (self.at + 1) % 4
                    if not self.busy[i]:
                        break
                else:
                    raise AssertionError("no bank")
                self.busy[i] = True
                E.wait(*self.free[i])
                return i

            def ap(self, i):
                return ps[:, 4 + i, :]

            def put(self, i, *marks):
                self.busy[i] = False
                self.free[i] = list(marks)

        B = Banks()

        def fence():
            marks = [V.last(), A.last(), E.last()]
            for e in (V, A, E):
                e.wait(*marks)

        items = []

        def item(name, src, kind, ks, ncols, opnd="x", rawonly=False):
            items.append(dict(name=name, src=src, kind=kind, ks=ks, nc=ncols, op=opnd, raw=rawonly))

        def kpairs(a, b):
            return [[k, k + 1] for k in range(a, b, 2)]

        w_in1, w_n1, cmp1, w_outd, gu1, dn1 = (ins[n] for n in ("w_in1", "w_n1", "cmp1", "w_out1", "gu1", "dn1"))
        names = ["k", "q0", "q1", "v", "c", "x0", "x1", "x2", "z0", "z1"]
        kinds = dict(k="feat", q="feat", v="tok", c="feat", x="feat", z="tok")
        for n, nm in enumerate(names):
            item("1" + nm, w_in1[n], kinds[nm[0]], kpairs(0, KT), CH)
            if nm == "v":
                item("1g", w_n1, "tok", [list(range(KT))], 64)
            if nm == "x0":
                item("1mk", cmp1[0], "cmp", [list(range(4 * u, 4 * u + 4)) for u in range(4)], 256, rawonly=True)
                item("1mv", cmp1[1], "cmp", [list(range(4 * u, 4 * u + 4)) for u in range(4)], 256, rawonly=True)
        for c in range(4):
            item(f"1oa{c}", w_outd[c][4:8], "tok", kpairs(0, 8), CH, "h")
        for c in range(4):
            item(f"1os{c}", w_outd[c][0:4], "tok", kpairs(8, 16), CH, "h")

        def ffn_items(b, gu, dn):
            for g, (c0, c1) in enumerate(GROUPS):
                for c in range(c0, c1):
                    item(f"{b}fg{c}", gu[0][c], "tok", kpairs(0, KT), CH)
                    item(f"{b}fu{c}", gu[1][c], "tok", kpairs(0, KT), CH)
                for c in range(4):
                    item(f"{b}fd{g}_{c}", dn[c][2 * c0:2 * c1], "tok", kpairs(0, 4 * (c1 - c0)), CH, "h")

        ffn_items(1, gu1, dn1)
        w_in2 = ins["w_in2"]
        names = (["af0", "af1", "aq0", "aq1", "ai0", "ai1", "ag0", "ag1", "bq0", "bq1", "bk0", "bk1", "bv0", "bv1"]
                 + [f"ga{c}" for c in range(4)] + [f"gb{c}" for c in range(4)])
        for n, nm in enumerate(names):
            item("2" + nm, w_in2[n], "feat" if nm[:2] in ("af", "aq", "bq", "bk") else "tok", kpairs(0, KT), CH)
            if nm == "bv1":
                item("2bf", ins["w_n2"], "tok", [list(range(KT))], 8)
        for c in range(4):
            item(f"2ua{c}", ins["w_up"][0][c], "tok", kpairs(0, 8), CH)
        for c in range(4):
            item(f"2ub{c}", ins["w_up"][1][c], "tok", kpairs(8, 16), CH)
        for c in range(4):
            item(f"2o{c}", ins["w_o"][c], "tok", kpairs(0, KT), CH, "h")
        ffn_items(2, ins["gu2"], ins["dn2"])

        units = []
        for it in items:
            it["first"] = len(units)
            for u, ks in enumerate(it["ks"]):
                units.append(dict(item=it, u=u, ks=ks, src=it["src"][u], n=len(ks) * it["nc"]))

        state = dict(dma=0, split=0, nraw={})

        def pump_dma(upto=10 ** 9):
            while state["dma"] < min(len(units), upto):
                j = state["dma"]
                if j >= NRAW:
                    old = units[j - NRAW]
                    if "freed" not in old:
                        return
                    S.wait(*old["freed"])
                u = units[j]
                slot = j % NRAW
                S.queue.append((lambda e, u=u, slot=slot: e.dma_start(raw[:, slot, 0:u["n"]], u["src"]).then_inc(s_raw[slot], 16), False))
                u["landed"] = (s_raw[slot], 16 * (j // NRAW + 1))
                state["dma"] += 1

        split_free = [None] * NSPL

        def pump_split(upto):
            while state["split"] <= min(upto, len(units) - 1):
                j = state["split"]
                state["split"] += 1
                u = units[j]
                if u["item"]["raw"]:
                    continue
                pump_dma()
                s = state["nraw"].setdefault("n", 0) % NSPL
                state["nraw"]["n"] += 1
                u["slot"] = s
                n, r = u["n"], j % NRAW
                hi = act(whi[:, s, 0:n], raw[:, r, 0:n], w=(u["landed"], split_free[s]), own=False)
                lo = tt(wlo[:, s, 0:n], raw[:, r, 0:n], whi[:, s, 0:n].bitcast(F), SUB, w=(hi, split_free[s]), own=False)
                u["hi"], u["lo"] = hi, lo
                split_free[s] = None
                u["freed"] = (hi, lo)
                pump_dma()

        pair_free = [[], []]
        opnd_ready = {"x": [None] * KT, "h": [None] * KT}
        opnds = {"x": (xhi, xlo), "h": (hhi, hlo)}
        later = []

        def due(n):
            for t in [t for t in later if t[0] <= n]:
                later.remove(t)
                t[1]()

        pe_units = [0]
        pair_at = [0]

        held = []

        def run_item(it, evac, defer=False):
            pair = pair_at[0] % 2
            pair_at[0] += 1
            banks = [ps[:, 2 * pair, :], ps[:, 2 * pair + 1, :]]
            hi_t, lo_t = opnds[it["op"]]
            nU = len(it["ks"])
            ncol = it["nc"]
            for ui in range(nU):
                gi = it["first"] + ui
                u = units[gi]
                pump_split(gi + NSPL - 1)
                pump_dma()
                if ui == 0:
                    E.wait(*pair_free[pair])
                if it["raw"]:
                    E.wait(u["landed"])
                    w4 = raw[:, gi % NRAW, 0:u["n"]].rearrange("p (k n) -> p k n", n=ncol)
                    kv = 0 if it["name"] == "1mk" else 1
                    for kk, k in enumerate(u["ks"]):
                        for ht in range(2):
                            last = mm(banks[0][:, ht * 60:ht * 60 + 60], w4[:, kk, ht * 128:ht * 128 + 128],
                                      flat[:, kv, k, :], start=(k == 0 and ht == 0), stop=(k == 15),
                                      inc=(kk == len(u["ks"]) - 1 and ht == 1), skip=True,
                                      w=flat_ready if kk == 0 else ())
                    u["freed"] = (last,)
                    pump_dma()
                else:
                    E.wait(u["hi"])
                    s = u["slot"]
                    wh = whi[:, s, 0:u["n"]].rearrange("p (k n) -> p k n", n=ncol)
                    wl = wlo[:, s, 0:u["n"]].rearrange("p (k n) -> p k n", n=ncol)
                    nk = len(u["ks"])
                    for kk, k in enumerate(u["ks"]):
                        E.wait(*(opnd_ready[it["op"]][k] or ()))
                        f0 = ui == 0 and kk == 0
                        l0 = ui == nU - 1 and kk == nk - 1
                        if it["kind"] == "tok":
                            for tb in range(2):
                                o = banks[tb][:, 0:ncol]
                                xh_ = hi_t[:, k, tb * 128:tb * 128 + 128]
                                xl_ = lo_t[:, k, tb * 128:tb * 128 + 128]
                                mm(o, xl_, wh[:, kk, :], start=f0, stop=False)
                                mm(o, xh_, wh[:, kk, :], start=False, stop=False)
                                last = mm(o, xh_, wl[:, kk, :], start=False, stop=l0, w=(u["lo"],),
                                          inc=(kk == nk - 1 and tb == 1))
                        else:
                            for ct in range(4):
                                o = banks[ct // 2][:, (ct % 2) * 256:(ct % 2) * 256 + 256]
                                wh_ = wh[:, kk, ct * 128:ct * 128 + 128]
                                wl_ = wl[:, kk, ct * 128:ct * 128 + 128]
                                mm(o, wh_, hi_t[:, k, :], start=(f0 and ct % 2 == 0), stop=False, skip=True)
                                mm(o, wh_, lo_t[:, k, :], start=False, stop=False, skip=True)
                                last = mm(o, wl_, hi_t[:, k, :], start=False, stop=l0, skip=True, w=(u["lo"],),
                                          inc=(kk == nk - 1 and ct == 3))
                    split_free[s] = last
                pe_units[0] += 1
                if ui == nU - 1:
                    if defer:
                        def put_off(pair=pair, banks=banks, last=last):
                            pair_free[pair] = list(evac(it, banks, last))
                        held.append(put_off)
                    else:
                        pair_free[pair] = list(evac(it, banks, last))
                due(pe_units[0])
                yield

        item_at = [0]

        def run(names, evac, side=None, ratio=1, defer=False):
            for nm in names:
                it = items[item_at[0]]
                item_at[0] += 1
                assert it["name"] == nm, (it["name"], nm)
                for _ in run_item(it, evac, defer):
                    for _ in range(ratio):
                        if side is not None:
                            next(side, None)

        def flush():
            for t in list(later):
                later.remove(t)
                t[1]()

        def both(*gens):
            gens = list(gens)
            while gens:
                for g in list(gens):
                    if next(g, gens) is gens:
                        gens.remove(g)
                yield

        def chain(*gens):
            for g in gens:
                yield from g

        junk = W_(WN - 512, 512)
        ones = C("OS")[:, 0:128]

        class Row:
            def __init__(self, width, chunks):
                self.width, self.parts, self.rs, self.m = width, small(2, chunks), small(2), None

            def add(self, tb, c, src, w):
                self.m = act(junk[:, 0:src.shape[1]], src, ACT.Square, accum_out=self.parts[:, tb, c:c + 1], w=w)

            def finish(self):
                p, r = self.parts, self.rs
                m = self.m
                if p.shape[2] > 1:
                    m = vdo(lambda e: e.reduce_sum(r, p, AX), w=(m,))
                else:
                    m = vcopy(r, p[:, :, 0], w=(m,))
                m = ts(r, r, 1.0 / self.width, EPS, MUL, ADD, w=(m,))
                m = act(r, r, ACT.Sqrt, w=(m,))
                self.m = vdo(lambda e: e.reciprocal(r, r), w=(m,))
                return self.m

        RB2 = RB[:, :].unsqueeze(1).to_broadcast([P, 2, T])

        def spread(rs, w):
            b = B.get()
            pb = B.ap(b)
            for tb in range(2):
                m = ts(rsq[:, tb, :], ones, rs[:, tb:tb + 1], None, MUL, w=w)
            for tb in range(2):
                m = mm(pb[:, tb * 128:tb * 128 + 128], rsq[:, tb, :], C("ident"), inc=(tb == 1), w=(m,))
            m = vcopy(RB[:, :], pb[:, 0:256], w=(m,))
            B.put(b, m)
            return m

        rsq = small(2, 128)

        def evac_split(dst, k, pb, m, wcols, prior):
            hi_t, lo_t = opnds[dst]
            A.wait(*prior)
            V.wait(*prior)
            if wcols is None:
                pv = pb.rearrange("p (a b) -> p a b", a=2)
                hi = act(hi_t[:, k:k + 2, :], pv, w=(m,), own=False)
                lo = tt(lo_t[:, k:k + 2, :], pv, hi_t[:, k:k + 2, :].bitcast(F), SUB, w=(hi,), own=False)
            else:
                for j in range(2):
                    hi = act(hi_t[:, k + j, :], pb[:, j * 256:j * 256 + 256], w=(m,), scale=wcols(k + j), own=False)
                for j in range(2):
                    lo = stt(lo_t[:, k + j, :], pb[:, j * 256:j * 256 + 256], wcols(k + j), hi_t[:, k + j, :].bitcast(F), MUL, SUB, w=(hi,))
            opnd_ready[dst][k] = opnd_ready[dst][k + 1] = (hi, lo)
            return (hi, lo)

        def tiles_T(dst, k, col, marks, wcols=None, prior=(), src=scr):
            b = B.get()
            pb = B.ap(b)
            for j in range(2):
                for tb in range(2):
                    m = tp(pb[:, j * 256 + tb * 128:j * 256 + tb * 128 + 128], src[:, tb, col + j * 128:col + j * 128 + 128],
                           inc=(j == 1 and tb == 1), w=marks)
            ms = evac_split(dst, k, pb, m, wcols, prior)
            B.put(b, *ms)
            return m

        G = W_(8192, 2, CH)
        Hb = W_(8192 + 1024, 2, CH)
        bcw = W_(WN - 512 - 2048, D)
        bc_n = [0]

        def load_bcw(i, marks):
            def go():
                S.wait(*marks)
                S.queue.append((lambda e: e.dma_start(bcw, ins["wb"][i]).then_inc(s_bc, 16), False))

            bc_n[0] += 1
            later.append((pe_units[0] + 4, go))
            return (s_bc, 16 * bc_n[0])

        fst = {}

        def ffn(b, acc_first, row, done, side=None, before=()):
            dst = h if b == 1 else scr

            def ev_gate(it, banks, last):
                ms = []
                for tb in range(2):
                    ms.append(act(G[:, tb, :], banks[tb], ACT.Silu, w=(last, fst.get("g_free"), row.m) + tuple(before), scale=row.rs[:, tb:tb + 1]))
                fst["g"] = ms[-1]
                return ms

            def ev_up(it, banks, last):
                c = int(it["name"][3:])
                ms = []
                for tb in range(2):
                    ms.append(stt(Hb[:, tb, :], banks[tb], row.rs[:, tb:tb + 1], G[:, tb, :], MUL, MUL, w=(last, fst["g"], fst.get("h_free")) + tuple(before)))
                fst["g_free"] = ms[-1]
                g0 = [a for a, z in GROUPS if a <= c < z][0]

                def transposes():
                    for j in range(0, 4, 2):
                        fst["h_free"] = tiles_T("h", 4 * (c - g0) + j, j * 128, (ms[-1],), prior=(fst.get("down"),), src=Hb)

                later.append((pe_units[0] + 2, transposes))
                return ms

            def ev_down(it, banks, last):
                c = int(it["name"].split("_")[1])
                g = int(it["name"][3])
                fst["down"] = last
                ms = []
                for tb in range(2):
                    o = dst[:, tb, c * CH:c * CH + CH]
                    if g == 0 and not acc_first:
                        ms.append(act(o, banks[tb], w=(last,)))
                    else:
                        ms.append(tt(o, o, banks[tb], ADD, w=(last, A.last() if g == 1 and not acc_first else None)))
                if g == 2:
                    done(c, ms[-1])
                return ms

            for g, (c0, c1) in enumerate(GROUPS):
                for c in range(c0, c1):
                    run([f"{b}fg{c}"], ev_gate, side)
                    run([f"{b}fu{c}"], ev_up)
                run([f"{b}fd{g}_{c}" for c in range(4)], ev_down)

        qf = W_(0, 8, T)
        qr = W_(2048, 8, T)
        kr = W_(4096, 4, T)
        vt = W_(5120, 2, CH)
        xT = W_(6144, 12, T)
        sz = W_(9216, 2, 1024)
        kraw = W_(11264, 4, T)
        ckv = W_(12288, 4, T)
        flat = W_(13312, 2, 16, 60)
        hid = W_(15232, 2, 2, 60)
        hrep = W_(15472, 2, 240)
        BD = W_(15952, 2, CH)
        SX = W_(16976, 512)
        PMs = [W_(17488, 512), W_(18000, 512)]
        PTs = [W_(18512, 512), W_(19024, 512)]
        RT = W_(20048, 512)
        CT = W_(20560, 4, T)
        kcT = W_(21584, 60)
        assert 21644 <= WN - 512, WN
        flat_ready = []
        gs = small(2, 48)
        dt = small(2, 16)
        aa = small(2, 16)
        zsum = small(24, 4)
        mnx = small(24, 4)
        mx16 = small(16)
        wgt = small(16)
        t16a = small(16)
        sp = [small(32) for _ in range(4)]
        ec = small(48)
        R1 = {}

        def ev_feat(dst, row, scale=None):
            def ev(it, banks, last):
                n = int(it["name"][-1]) if it["name"][-1].isdigit() else 0
                ms = []
                for b in range(2):
                    o = dst[:, n * 4 + 2 * b:n * 4 + 2 * b + 2, :]
                    pv = banks[b].rearrange("p (a b) -> p a b", a=2)
                    if scale is None:
                        ms.append(tt(o, pv, RB2, MUL, w=(last, R1["RB"])))
                    else:
                        ms.append(stt(o, pv, scale, RB2, MUL, MUL, w=(last, R1["RB"])))
                R1[it["name"]] = ms[-1]
                return ms
            return ev

        def softplus(o, x, n, w, neg=False):
            e, u, z, r = (s[:, 0:n] for s in sp)
            m = ts(u, x, -1.0, None, MUL, w=w)
            m = tt(e, x, u, MAX, w=(m,))
            m = act(e, e, ACT.Exp, scale=-1.0, w=(m,))
            m = ts(u, e, 1.0, None, ADD, w=(m,))
            l = act(r, u, ACT.Ln, w=(m,))
            m = ts(u, u, -1.0, None, ADD, w=(l,))
            m = ts(z, u, 0.0, None, ALU.is_equal, w=(m,))
            m = tt(r, r, z, ADD, w=(m,))
            m2 = tt(u, u, z, ADD, w=(m,))
            V.wait(m2)
            m = vdo(lambda e_: e_.reciprocal(u, u))
            m = tt(r, r, e, MUL, w=(m,))
            m = tt(r, r, u, MUL, w=(m,))
            if neg:
                return stt(o, x, 0.0, r, MIN, SUB, w=(m,))
            return stt(o, x, 0.0, r, MAX, ADD, w=(m,))

        def rope(src, dst, ntile, ready):
            pend = None
            for t in list(range(0, ntile, 2)) + [None]:
                if pend is not None:
                    b, m, p = pend
                    rv = RT[:, 0:512].rearrange("p (a b) -> p a b", a=2)
                    tt(dst[:, p:p + 2, :], src[:, p:p + 2, :], bc(C("cos"), 1, [P, 2, T]), MUL, w=ready)
                    m = tt(rv, B.ap(b).rearrange("p (a b) -> p a b", a=2), bc(C("sin"), 1, [P, 2, T]), MUL, w=(m,), own=False)
                    B.put(b, m)
                    R1["rope"] = tt(dst[:, p:p + 2, :], dst[:, p:p + 2, :], rv, ADD)
                if t is not None:
                    b = B.get()
                    m = mm(B.ap(b), C("perm"), src[:, t:t + 2, :].rearrange("p a b -> p (a b)"), inc=True, w=ready)
                    pend = (b, m, t)
                yield

        def attend(tasks):
            n = len(tasks)
            sx, pm_free, pt_free = None, [None, None], [None, None]
            outs = {}
            for i in range(n + 4):
                if 3 <= i < n + 3:
                    t = tasks[i - 3]
                    a = act(PTs[i % 2], B.ap(t["tb_"]), w=(t["tm"], pt_free[i % 2]), own=False)
                    B.put(t["tb_"], a)
                    t["pt"] = a
                if 1 <= i < n + 1:
                    t = tasks[i - 1]
                    Kn, nh = t["Kn"], t["nh"]
                    mk = C("cm")[:, 256 - Kn:256]
                    pb = B.ap(t["sb_"])
                    mn, zs = mnx[:, i - 1, :], zsum[:, i - 1, :]
                    V.wait(t["sm"], sx)
                    for r in range(nh):
                        V.do(lambda e, r=r, pb=pb, mn=mn, mk=mk, Kn=Kn, sc=t["scale"], SXt=SXt: e.tensor_tensor_reduce(
                            out=SXt[:, r * Kn:r * Kn + Kn], in0=pb[:, r * Kn:r * Kn + Kn], in1=mk, scale=-sc, scalar=3e38,
                            op0=ADD, op1=MIN, accum_out=mn[:, r:r + 1]))
                    B.put(t["sb_"], V.last())
                    A.wait(V.last(), pm_free[i % 2])
                    for r in range(nh):
                        sx = act(PMs[i % 2][:, r * Kn:r * Kn + Kn], SXt[:, r * Kn:r * Kn + Kn], ACT.Exp, scale=-1.0,
                                 bias=mn[:, r:r + 1], accum_out=zs[:, r:r + 1], own=False)
                    t["pm"] = sx
                if 4 <= i and "fin" in tasks[i - 4]:
                    t = tasks[i - 4]
                    t["fin"](B.ap(t["ob"]), t["pv"])
                    B.put(t["ob"], V.last())
                if 3 <= i < n + 3:
                    t = tasks[i - 3]
                    if t["new"]:
                        outs["b"] = B.get()
                    t["ob"] = outs["b"]
                    E.wait(t["pt"])
                    t["pv"] = pt_free[i % 2] = t["values"](B.ap(t["ob"]), PTs[i % 2])
                if 2 <= i < n + 2:
                    t = tasks[i - 2]
                    b = t["tb_"] = B.get()
                    pb = B.ap(b)
                    for j in range(4):
                        m = tp(pb[:, j * 128:j * 128 + 128], PMs[(i - 1) % 2][:, j * 128:j * 128 + 128], inc=(j == 3), w=(t["pm"],))
                    t["tm"] = pm_free[(i - 1) % 2] = m
                if i < n:
                    t = tasks[i]
                    t["sb_"] = B.get()
                    t["sm"] = t["scores"](B.ap(t["sb_"]))
                yield

        def att_o(tb, hh):
            return scr[:, tb, 1024 + hh * 512:1024 + hh * 512 + 512].rearrange("p (h d) -> p h d", h=8)

        def attention1():
            E.wait(R1["rope"], R1["1v"])
            tasks = []

            def task(tb, hh, br, g, r0, nh, first, lastt):
                Kn, p0 = 128 * (tb + 1), (g % 2) * 64
                nb = tb + 1

                def scores(pb):
                    for r in range(nh):
                        m = mm(pb[:, r * Kn:r * Kn + Kn], qr[p0:p0 + 64, (g // 2) * 4 + r0 + r, tb * 128:tb * 128 + 128],
                               kr[p0:p0 + 64, br * 2 + g // 2, 0:Kn], inc=(r == nh - 1))
                    return m

                def values(po, pt):
                    for r in range(nh):
                        for kb in range(nb):
                            q = r * nb + kb
                            c = (4 * (g % 2) + r0 + r) * 64
                            m = mm(po[:, c:c + 64], pt[:, q * 128:q * 128 + 128], vt[:, kb, br * 256 + g * 64:br * 256 + g * 64 + 64],
                                   start=(kb == 0), stop=(kb == nb - 1), inc=(r == nh - 1 and kb == nb - 1))
                    return m

                t = dict(Kn=Kn, nh=nh, scale=0.125, scores=scores, values=values, new=first)
                if lastt:
                    n0 = len(tasks) + 1 - 8 // nh

                    def fin(po, pv):
                        w8 = wgt[:, 0:8].rearrange("p (a b) -> p a b", b=nh)
                        z8 = zsum[:, n0:n0 + 8 // nh, 0:nh]
                        vdo(lambda e: e.reciprocal(w8, z8), w=(A.last(), R1["1g"]))
                        gv = gs[:, tb, :].rearrange("p (h b) -> p h b", b=3)[:, 8 * hh:8 * hh + 8, br + 1]
                        tt(wgt[:, 0:8], wgt[:, 0:8], gv, MUL)
                        o = att_o(tb, hh)
                        pv_ = po.rearrange("p (h d) -> p h d", h=8)
                        if br == 0:
                            tt(o, pv_, bc(wgt[:, 0:8], 2, [P, 8, 64]), MUL, w=(pv,))
                        else:
                            rt = RT[:, 0:512].rearrange("p (h d) -> p h d", h=8)
                            m = tt(rt, pv_, bc(wgt[:, 0:8], 2, [P, 8, 64]), MUL, w=(pv,))
                            tt(o, o, rt, ADD)
                    t["fin"] = fin
                tasks.append(t)

            for tb in range(2):
                nh = 4 if tb == 0 else 2
                for hh in range(2):
                    for br in range(2):
                        part = [(g, r0) for g in (2 * hh, 2 * hh + 1) for r0 in range(0, 4, nh)]
                        for x, (g, r0) in enumerate(part):
                            task(tb, hh, br, g, r0, nh, x == 0, x == len(part) - 1)
            yield from attend(tasks)

        def compressed():
            hs = [R1["1mk"], R1["1mv"]]
            b = B.get()
            pb = B.ap(b)
            w2k = C("w2k").rearrange("p (a b) -> p a b", a=2)
            w2v = C("w2v").rearrange("p (a b) -> p a b", a=2)
            for ht in range(2):
                m = mm(pb[:, 0:60], w2k[:, ht, :], hid[:, 0, ht, :], start=(ht == 0), stop=(ht == 1), inc=(ht == 1), w=hs)
            a = act(kcT, pb[:, 0:60], w=(m,))
            B.put(b, a)
            for ht in range(2):
                vcopy(hrep[:, ht, :].rearrange("p (g r i) -> p g r i", g=4, r=4),
                      hid[:, 1, ht, :].rearrange("p (g i) -> p g i", g=4).unsqueeze(2).to_broadcast([P, 4, 4, 15]), w=hs)
            mh = V.last()
            for gp in range(2):
                b = B.get()
                pb = B.ap(b)
                for ht in range(2):
                    m = mm(pb[0:120, 0:64], hrep[:, ht, gp * 120:gp * 120 + 120], w2v[:, ht, :],
                           start=(ht == 0), stop=(ht == 1), inc=(ht == 1), w=(mh,))
                m = tt(BD[0:120, gp, :].rearrange("p (c d) -> p c d", c=8), bc(pb[0:120, 0:64], 1, [120, 8, 64]),
                       bc(C("bd", 120), 2, [120, 8, 64]), MUL, w=(m,))
                B.put(b, m)
            mbd = m
            yield
            for tb in range(2):
                bs = [B.get(), B.get()]
                for par in range(2):
                    for g2 in range(2):
                        for r in range(4):
                            p0, g = par * 64, 2 * g2 + par
                            m = mm(B.ap(bs[par])[:, (4 * g2 + r) * 15:(4 * g2 + r) * 15 + 15], qf[p0:p0 + 64, g2 * 4 + r, tb * 128:tb * 128 + 128],
                                   kcT[p0:p0 + 64, g * 15:g * 15 + 15], inc=(g2 == 1 and r == 3), w=(a,))
                yield
                s = SX[:, 0:240].rearrange("p (h i) -> p h i", i=15)
                s4 = SX[:, 0:240].rearrange("p (a b c) -> p a b c", a=2, b=2)
                e = PMs[0][:, 0:240].rearrange("p (h i) -> p h i", i=15)
                cadd = C("cadd")[:, tb * 15:tb * 15 + 15]
                cmul = C("cmul")[:, tb * 15:tb * 15 + 15]
                for par in range(2):
                    ml = act(s4[:, :, par, :], B.ap(bs[par])[:, 0:120].rearrange("p (a c) -> p a c", a=2), w=(m,), scale=0.125)
                    B.put(bs[par], ml)
                m = tt(s, s, bc(cadd, 1, [P, 16, 15]), ADD, w=(ml,))
                m = vdo(lambda e_: e_.reduce_max(mx16, s, AX))
                m = tt(s, s, bc(mx16, 2, [P, 16, 15]), SUB, w=(m,))
                m = act(e, s, ACT.Exp, w=(m, E.last()))
                V.wait(m)
                m = vdo(lambda e_: e_.reduce_sum(t16a[:, 0:16], e, AX))
                V.wait(m)
                m = vdo(lambda e_: e_.reciprocal(t16a, t16a))
                gv = gs[:, tb, :].rearrange("p (h b) -> p h b", b=3)[:, :, 0]
                mw = tt(t16a, t16a, gv, MUL, w=(m, R1["1g"]))
                m = tt(e, e, bc(cmul, 1, [P, 16, 15]), MUL, w=(m,))
                yield
                b = B.get()
                pb = B.ap(b)
                for gp in range(2):
                    mt = tp(pb[0:120, gp * 128:gp * 128 + 128], PMs[0][:, gp * 120:gp * 120 + 120], inc=(gp == 1), w=(m,))
                m = act(PTs[0][0:120, 0:256], pb[0:120, 0:256], w=(mt,))
                B.put(b, m)
                yield
                for gp in range(2):
                    b = B.get()
                    pb = B.ap(b)
                    mo = mm(pb, PTs[0][0:120, gp * 128:gp * 128 + 128], BD[0:120, gp, :], inc=True, w=(m, mbd))
                    rt = RT[:, 0:512].rearrange("p (h d) -> p h d", h=8)
                    m2 = tt(rt, pb.rearrange("p (h d) -> p h d", h=8), bc(t16a[:, 8 * gp:8 * gp + 8], 2, [P, 8, 64]), MUL, w=(mo, mw))
                    B.put(b, m2)
                    tt(att_o(tb, gp), att_o(tb, gp), rt, ADD, w=(m2,))
                yield

        def flatten():
            pes = [C("pek"), C("pev")]
            for kv in range(2):
                for par in range(2):
                    p0 = par * 64
                    for jp in range(2):
                        for q in range(2):
                            for hq in range(2):
                                src = ckv[p0:p0 + 64, kv * 2 + hq, :].rearrange("p (i j) -> p i j", j=16)
                                c0 = (2 * hq + par) * 15
                                o = flat[jp * 64:jp * 64 + 64, kv, 8 * q:8 * q + 8, c0:c0 + 15]
                                i_ = src[:, q:q + 15, jp:16:2].rearrange("p i j -> p j i")
                                pe = pes[kv][p0:p0 + 64, 16 * q + jp:16 * q + 16:2].unsqueeze(2).to_broadcast([64, 8, 15])
                                m = tt(o, i_, pe, ADD, w=(R1["1c"],), own=False)
                    if kv == 1 and par == 1:
                        flat_ready.append(m)
                    yield

        def ev_cmp(it, banks, last):
            kv = 0 if it["name"] == "1mk" else 1
            m = act(hid[:, kv, :, :], banks[0][:, 0:120].rearrange("p (a b) -> p a b", a=2), ACT.Silu, w=(last,))
            R1[it["name"]] = m
            return [m]

        def ev_v(it, banks, last):
            ms = [act(vt[:, tb, :], banks[tb], w=(last, rowA.m), scale=rowA.rs[:, tb:tb + 1]) for tb in range(2)]
            R1[it["name"]] = ms[-1]
            return ms

        def ev_g1(it, banks, last):
            ms = []
            for tb in range(2):
                m = act(gs[:, tb, :], banks[tb][:, 16:64], ACT.Sigmoid, w=(last, rowA.m), scale=rowA.rs[:, tb:tb + 1])
                ms.append(stt(dt[:, tb, :], banks[tb][:, 0:16], rowA.rs[:, tb:tb + 1], C("dtb"), MUL, ADD, w=(m,)))
            d32 = dt.rearrange("p a b -> p (a b)")
            m = softplus(d32, d32, 32, w=(V.last(),))
            e = act(ec[:, 0:16], C("alog"), ACT.Exp)
            m = ts(ec[:, 0:16], ec[:, 0:16], -1.0, None, MUL, w=(e,))
            tt(aa, dt, bc(ec[:, 0:16], 1, [P, 2, 16]), MUL, w=(m,))
            R1["1g"] = V.last()
            R1["1ga"] = A.last()
            return ms

        def ev_conv(it, banks, last):
            n = int(it["name"][-1])
            ms = []
            cw = C("convw")
            for b in range(2):
                ms.append(tt(CT[:, 2 * b:2 * b + 2, :], banks[b].rearrange("p (a b) -> p a b", a=2), RB2, MUL,
                             w=(last, R1["RB"], R1.get("tap0"))))
            first = [None] * 4

            def taps(j):
                if j < 4:
                    t = n * 4 + j
                    first[j] = R1["tap0"] = act(xT[:, t, :], CT[:, j, :], ACT.Identity, scale=cw[:, t * 4 + 3:t * 4 + 4],
                                                bias=C("convb")[:, t:t + 1], w=(ms[1],), own=False)
                if j > 0:
                    t = n * 4 + j - 1
                    o = xT[:, t, :]
                    for q in range(1, 4):
                        m = stt(o[:, q:T], CT[:, j - 1, 0:T - q], cw[:, t * 4 + 3 - q:t * 4 + 4 - q], o[:, q:T], MUL, ADD, w=(first[j - 1],))
                    if j == 4:
                        R1["taps", n] = m

            for j in range(5):
                later.append((pe_units[0] + 1 + j, lambda j=j: taps(j)))
            return ms

        def ev_z(it, banks, last):
            n = int(it["name"][-1])
            ms = [act(sz[:, tb, n * 512:n * 512 + 512], banks[tb], ACT.Silu, w=(last, rowA.m), scale=rowA.rs[:, tb:tb + 1]) for tb in range(2)]
            R1[it["name"]] = ms[-1]
            return ms

        xs = W_(2048, 2, 1024)
        xd = W_(11264, 2, 1024)
        ys = W_(13312, 2, 1024)
        xe = W_(15360, 1024)
        st = W_(16384, 2, 512)
        cbm = W_(17408, 4, 128)
        UA = W_(17920, 2, 4, 128)
        EE = W_(18944, 2, 4, 128)
        MM = W_(19968, 2, 4, 128)
        Bt = W_(20992, 256)

        def attention_T():
            yield
            marks = (V.last(),)
            for k in range(0, 8, 2):
                tiles_T("h", k, 1024 + k * 128, marks, prior=marks + (E.last(), A.last()))
                yield

        def ssd():
            while ("taps", 2) not in R1:
                yield
            V.wait(E.last(), A.last())
            A.wait(E.last(), V.last())
            for t in range(0, 12, 4):
                m = act(xT[:, t:t + 4, :], xT[:, t:t + 4, :], ACT.Silu, w=(R1["taps", 2],), own=False)
            R1["1x2"] = m
            yield
            for tb in range(2):
                for q in range(2):
                    b = B.get()
                    pb = B.ap(b)
                    for j in range(4):
                        m = tp(pb[:, j * 128:j * 128 + 128], xT[:, 4 * q + j, tb * 128:tb * 128 + 128], inc=(j == 3), w=(R1["1x2"],))
                    a = act(xs[:, tb, q * 512:q * 512 + 512], pb, w=(m,))
                    B.put(b, a)
                yield
            b = B.get()
            pb = B.ap(b)
            for g in range(2):
                m = tp(pb[:, g * 128:g * 128 + 128], xT[:, 8 + g, 0:128], inc=(g == 1))
            mb = act(Bt, pb[:, 0:256], w=(m,))
            B.put(b, mb)
            for tb in range(2):
                mx = tt(xd[:, tb, :].rearrange("p (h d) -> p h d", h=16), xs[:, tb, :].rearrange("p (h d) -> p h d", h=16),
                        bc(dt[:, tb, :], 2, [P, 16, 64]), MUL, w=(a,))
            b = B.get()
            pb = B.ap(b)
            mm(pb[:, 0:16], C("OS")[:, 128:256], aa[:, 0, :], w=(R1["1g"],))
            m = mm(pb[:, 16:32], C("U"), aa[:, 1, :], inc=True)
            m = act(ec[:, 16:48], pb[:, 0:32], ACT.Exp, w=(m,))
            B.put(b, m)
            yield
            mxe = tt(xe.rearrange("p (h d) -> p h d", h=16), xd[:, 0, :].rearrange("p (h d) -> p h d", h=16),
                     bc(ec[:, 16:32], 2, [P, 16, 64]), MUL, w=(m, mx))
            for g in range(2):
                b = B.get()
                pb = B.ap(b)
                m = mm(pb, Bt[:, g * 128:g * 128 + 128], xe[:, g * 512:g * 512 + 512], inc=True, w=(mxe, mb))
                a = act(st[:, g, :], pb, w=(m,))
                B.put(b, a)
            yield
            for g in range(2):
                b = B.get()
                pb = B.ap(b)
                m = mm(pb, xT[:, 10 + g, 128:256], st[:, g, :], inc=True, w=(a,))
                m = tt(ys[:, 1, g * 512:g * 512 + 512].rearrange("p (h d) -> p h d", h=8), pb.rearrange("p (h d) -> p h d", h=8),
                       bc(ec[:, 32 + 8 * g:40 + 8 * g], 2, [P, 8, 64]), MUL, w=(m,))
                B.put(b, m)
            b = B.get()
            pb = B.ap(b)
            for c in range(2):
                for g in range(2):
                    m = mm(pb[:, (2 * c + g) * 128:(2 * c + g) * 128 + 128], xT[:, 8 + g, c * 128:c * 128 + 128],
                           xT[:, 10 + g, c * 128:c * 128 + 128], inc=(c == 1 and g == 1))
            mcb = tt(cbm, pb.rearrange("p (a b) -> p a b", a=4), bc(C("U"), 1, [P, 4, 128]), MUL, w=(m,))
            B.put(b, mcb)
            yield
            dsk = bc(C("dsk"), 2, [P, 16, 64])
            m = tt(xs[:, 1, :].rearrange("p (h d) -> p h d", h=16), xs[:, 1, :].rearrange("p (h d) -> p h d", h=16), dsk, MUL, w=(mx,))
            tt(ys[:, 1, :], ys[:, 1, :], xs[:, 1, :], ADD, w=(m,))
            my = tt(ys[:, 0, :].rearrange("p (h d) -> p h d", h=16), xs[:, 0, :].rearrange("p (h d) -> p h d", h=16), dsk, MUL)
            yield
            part = [(g, c, hq) for g in range(2) for c in range(2) for hq in range(2)]
            n = len(part)
            mu, seg, me, mk, va, obs = {}, {}, {}, {}, {}, {}
            for i in range(-1, n + 4):
                if 0 <= i < n:
                    b = B.get()
                    seg[i] = mm(B.ap(b), C("OS")[:, 128:256], UA[:, i % 2, :, :].rearrange("p a b -> p (a b)"), inc=True, w=(mu[i],))
                    me[i] = act(EE[:, i % 2, :, :], B.ap(b).rearrange("p (a b) -> p a b", a=4), ACT.Exp, w=(seg[i], mk.get(i - 2)), own=False)
                    B.put(b, me[i])
                if i >= 3 and i - 3 < n and part[i - 3][2] == 1:
                    g, c, _ = part[i - 3]
                    yv = ys[:, c, g * 512:g * 512 + 512]
                    ob = obs.pop((g, c))
                    m = tt(yv, yv, B.ap(ob), ADD, w=(va[i - 3], my))
                    B.put(ob, m)
                    o = scr[:, c, g * 512:g * 512 + 512]
                    m = tt(o, yv, sz[:, c, g * 512:g * 512 + 512], MUL, w=(m, R1[f"1z{g}"]))
                    rowS.add(c, g, o, (m,))
                    if c == 1:
                        R1["yg", g] = m
                        if g == 1:
                            rowS.finish()
                if 0 <= i - 1 < n:
                    g, c, _ = part[i - 1]
                    mk[i - 1] = tt(MM[:, (i - 1) % 2, :, :], EE[:, (i - 1) % 2, :, :], bc(cbm[:, 2 * c + g, :], 1, [P, 4, 128]), MUL,
                                   w=(me[i - 1], va.get(i - 3), mcb))
                if i + 1 < n:
                    g, c, hq = part[i + 1]
                    h0 = 8 * g + 4 * hq
                    mu[i + 1] = tt(UA[:, (i + 1) % 2, :, :], bc(C("U"), 1, [P, 4, 128]), bc(aa[:, c, h0:h0 + 4], 2, [P, 4, 128]), MUL,
                                   w=(seg.get(i - 1),))
                if 0 <= i - 2 < n:
                    g, c, hq = part[i - 2]
                    if hq == 0:
                        obs[g, c] = B.get()
                    for r in range(4):
                        hd = 8 * g + 4 * hq + r
                        va[i - 2] = mm(B.ap(obs[g, c])[:, (4 * hq + r) * 64:(4 * hq + r) * 64 + 64], MM[:, i % 2, r, :],
                                       xd[:, c, hd * 64:hd * 64 + 64], inc=(r == 3), w=(mk[i - 2], mx))
                if i in (7, 11):
                    g = i == 11
                    for k in range(4 * g, 4 * g + 4, 2):
                        tiles_T("h", 8 + k, k * 128, (R1["yg", g],), wcols=lambda kk: C("snw")[:, kk - 8:kk - 7], prior=(R1["yg", g],))
                yield

        S0 = 8192
        aq = W_(S0, 8, T)
        ab = W_(S0 + 2048, 8, T)
        ak = W_(S0 + 4096, 8, T)
        ai = W_(S0 + 6144, 2, 1024)
        AM = W_(S0 + 8192, 8, 128)
        A2 = W_(S0 + 9216, 4, 128)
        DD = W_(S0 + 9728, 4, T)
        QE = W_(S0 + 10752, 4, T)
        KE = W_(S0 + 11776, 4, T)
        assert S0 + 12800 <= WN - 512, WN
        sg = W_(0, 4, 4, CH)
        lbt = small(3, 8)

        def lower_bounds():
            l0, l1 = C("lb0"), C("lb1")
            m = tt(lbt[:, 0, :], l0, l1, MAX)
            a = tt(lbt[:, 1, :], l0, lbt[:, 0, :], SUB, w=(m,))
            b = tt(lbt[:, 2, :], l1, lbt[:, 0, :], SUB, w=(m,))
            a = act(lbt[:, 1:3, :], lbt[:, 1:3, :], ACT.Exp, w=(b,))
            m = tt(lbt[:, 2, :], lbt[:, 1, :], lbt[:, 2, :], ADD, w=(a,))
            V.wait(m)
            m = vdo(lambda e: e.reciprocal(lbt[:, 2, :], lbt[:, 2, :]))
            m = tt(lbt[:, 0, :], lbt[:, 1, :], lbt[:, 2, :], MUL, w=(m,))
            m = ts(lbt[:, 1, :], lbt[:, 0, :], -1.0, 1.0, MUL, ADD, w=(m,))
            A.wait(m)

        def ev_af(it, banks, last):
            n = int(it["name"][-1])
            ms = []
            for b in range(2):
                t = n * 4 + 2 * b
                ms.append(tt(ab[:, t:t + 2, :], banks[b].rearrange("p (a b) -> p a b", a=2), RB2, MUL, w=(last, R1["RB"])))
            t = n * 4
            act(ak[:, t:t + 4, :], ab[:, t:t + 4, :], ACT.Sigmoid, scale=-1.0, w=(ms[-1],))
            mk = act(ab[:, t:t + 4, :], ab[:, t:t + 4, :], ACT.Sigmoid)
            for t in range(n * 4, n * 4 + 4):
                ts(ak[:, t, :], ak[:, t, :], lbt[:, 1, t:t + 1], None, MUL, w=(mk,))
                act(ab[:, t, :], ab[:, t, :], ACT.Ln, scale=lbt[:, 1, t:t + 1], bias=lbt[:, 0, t:t + 1], w=(mk,))
                V.wait(A.last())
                vdo(lambda e, t=t: e.tensor_tensor_scan(ab[:, t, :], ones256, ab[:, t, :], 0.0, MUL, ADD))
            R1[it["name"]] = V.last()
            return ms

        ones256 = None

        def ev_t1024(dst, func=ACT.Copy):
            def ev(it, banks, last):
                n = int(it["name"][-1])
                ms = [act(dst[:, tb, n * 512:n * 512 + 512], banks[tb], func, w=(last, R1["rsB"]), scale=rsB[:, tb:tb + 1]) for tb in range(2)]
                R1[it["name"]] = ms[-1]
                return ms
            return ev

        def ev_ga(which):
            def ev(it, banks, last):
                n = int(it["name"][-1])
                ms = []
                for tb in range(2):
                    o = W[:, which * 4096 + n * 1024 + tb * 512:which * 4096 + n * 1024 + tb * 512 + 512]
                    ms.append(act(o, banks[tb], ACT.Sigmoid, w=(last, R1["rsB"], R1["fox"] if which else None), scale=rsB[:, tb:tb + 1]))
                R1[it["name"]] = ms[-1]
                return ms
            return ev

        rsB = small(2)
        gsil = scr[:, :, 1024:2048]

        def hgrn():
            E.wait(R1["2ai1"])
            for hg in range(2):
                h0 = 4 * hg
                vdo(lambda e: e.memset(AM, 0.0), w=(E.last(),))
                if hg == 0:
                    vdo(lambda e: e.memset(QE, 0.0))
                    vdo(lambda e: e.memset(KE, 0.0))
                seq = [0, 128] + LEVELS
                mE = None

                def decay(m_):
                    nb = T // (2 * m_)
                    bv = ab[:, h0:h0 + 4, :].rearrange("p h (n s m) -> p (h n) s m", s=2, m=m_)
                    dv = DD.rearrange("p h (n s m) -> p (h n) s m", s=2, m=m_)
                    anc = bv[:, :, 0, m_ - 1].unsqueeze(2).to_broadcast([P, 4 * nb, m_])
                    tt(dv[:, :, 1, :], bv[:, :, 1, :], anc, SUB, w=(R1["2af1"], R1["2aq1"]))
                    md = tt(dv[:, :, 0, :], anc, bv[:, :, 0, :], SUB, own=False)
                    return act(DD, DD, ACT.Exp, w=(md,))

                def factors(m_):
                    def v(ap):
                        return ap.rearrange("p h (n s m) -> p (h n) s m", s=2, m=m_)

                    tt(v(QE)[:, :, 1, :], v(aq[:, h0:h0 + 4, :])[:, :, 1, :], v(DD)[:, :, 1, :], MUL, w=(mE, E.last()))
                    return tt(v(KE)[:, :, 0, :], v(ak[:, h0:h0 + 4, :])[:, :, 0, :], v(DD)[:, :, 0, :], MUL, own=False)

                me = R1["2aq1"]
                for li, m_ in enumerate(seq):
                    ql, kl = (QE, KE) if m_ else (aq[:, h0:h0 + 4, :], ak[:, h0:h0 + 4, :])
                    if m_ == 128:
                        bs = [B.get()]
                        pb = B.ap(bs[0])
                        for r in range(4):
                            m = mm(pb[:, r * 128:r * 128 + 128], kl[:, r, 0:128], ql[:, r, 128:256], inc=(r == 3), w=(me,))
                    else:
                        bs = [B.get(), B.get()]
                        for c in range(2):
                            pb = B.ap(bs[c])
                            for r in range(4):
                                m = mm(pb[:, r * 128:r * 128 + 128], kl[:, r, c * 128:c * 128 + 128], ql[:, r, c * 128:c * 128 + 128],
                                       inc=(r == 3 and c == 1), w=(me,))
                    if li + 1 < len(seq):
                        mE = decay(seq[li + 1])
                    yield
                    if li + 1 < len(seq):
                        me = factors(seq[li + 1])
                    if m_ == 128:
                        B.put(bs[0], vcopy(A2, B.ap(bs[0]).rearrange("p (a b) -> p a b", a=4), w=(m,)))
                    else:
                        lix = 0 if m_ == 0 else 1 + LEVELS.index(m_)
                        mask = C("lev")[:, lix * 128:lix * 128 + 128].bitcast(I32)
                        for c in range(2):
                            pb = B.ap(bs[c])
                            B.put(bs[c], vdo(lambda e, c=c, pb=pb, mask=mask: e.copy_predicated(
                                AM[:, 4 * c:4 * c + 4, :], bc(mask, 1, [P, 4, 128]), pb.rearrange("p (a b) -> p a b", a=4)), w=(m,)))
                    yield
                ma = V.last()
                bs = []
                for c in range(2):
                    b = B.get()
                    bs.append(b)
                    pb = B.ap(b)
                    for r in range(4):
                        hd = h0 + r
                        o = pb[:, r * 128:r * 128 + 128]
                        m = mm(o, AM[:, 4 * c + r, :], ai[:, c, hd * 128:hd * 128 + 128], start=True, stop=(c == 0), w=(ma,),
                               inc=(r == 3 and c == 0))
                        if c == 1:
                            m = mm(o, A2[:, r, :], ai[:, 0, hd * 128:hd * 128 + 128], start=False, stop=True, inc=(r == 3))
                yield
                for c in range(2):
                    pb = B.ap(bs[c])
                    pv = pb.rearrange("p (h d) -> p h d", h=4)
                    sq = DD.rearrange("p a b -> p (a b)")[:, 512 * c:512 * c + 512].rearrange("p (h d) -> p h d", h=4)
                    t4 = t16a[:, 4 * c:4 * c + 4]
                    a = act(sq, pv, ACT.Square, w=(m, V.last()))
                    vdo(lambda e, t4=t4, sq=sq: e.reduce_sum(t4, sq, AX), w=(a,))
                    m2 = ts(t4, t4, 1.0 / 128, EPS, MUL, ADD)
                    m2 = act(t4, t4, ACT.Sqrt, w=(m2,))
                    vdo(lambda e, t4=t4: e.reciprocal(t4, t4), w=(m2,))
                    o = scr[:, c, h0 * 128:h0 * 128 + 512].rearrange("p (h d) -> p h d", h=4)
                    B.put(bs[c], tt(o, pv, bc(t4, 2, [P, 4, 128]), MUL))
                    R1[f"o{hg}{c}"] = V.last()
                    yield
            for c in range(2):
                R1["oa"] = tt(scr[:, c, 0:1024], scr[:, c, 0:1024], gsil[:, c, :], MUL, w=(R1["2ag1"],))
                yield

        bq = h[:, 0, :].rearrange("p (a b) -> p a b", a=8)
        bk = h[:, 1, :].rearrange("p (a b) -> p a b", a=8)
        bv_ = W_(6144, 2, 1024)
        lf = small(2, 8)
        LU = W_(S0 + 8192, 2, 4, 128)
        assert sm_at[0] <= 1280

        def ev_bf(it, banks, last):
            ms = []
            for tb in range(2):
                ms.append(stt(lf[:, tb, :], banks[tb][:, 0:8], rsB[:, tb:tb + 1], C("bfox"), MUL, ADD, w=(last, R1["rsB"])))
            l16 = lf.rearrange("p a b -> p (a b)")
            softplus(l16, l16, 16, w=(ms[-1],), neg=True)
            R1["2bf"] = V.last()
            return ms

        foxw = [W_(S0 + 9216 + 512 * i, 512) for i in range(5)]

        def fox():
            nonlocal SXt, PMs, PTs
            SXt, PMs, PTs = foxw[0], foxw[1:3], foxw[3:5]
            E.wait(R1["2bv1"], R1["2bk1"])
            A.wait(R1["oa"])
            V.wait(A.last())
            tasks = []

            def task(tb, h0, nh, first, lastt):
                Kn, nb = 128 * (tb + 1), tb + 1
                L0 = LU[:, 0, 0:nh, :]
                L1 = LU[:, 1, 0:nh, :]

                def scores(pb):
                    lu = tt(L0, bc(C("U"), 1, [P, nh, 128]), bc(lf[:, tb, h0:h0 + nh], 2, [P, nh, 128]), MUL, w=(E.last(), R1["2bf"]))
                    if tb:
                        lu = tt(L1, bc(ones, 1, [P, nh, 128]), bc(lf[:, 0, h0:h0 + nh], 2, [P, nh, 128]), MUL)
                    for r in range(nh):
                        o = pb[:, r * Kn:r * Kn + Kn]
                        mm(o, bq[:, h0 + r, tb * 128:tb * 128 + 128], bk[:, h0 + r, 0:Kn], start=True, stop=False)
                        if tb:
                            mm(o[:, 0:128], LU[:, 1, r, :], C("OS")[:, 128:256], start=False, stop=False, w=(lu,))
                        m = mm(o, LU[:, 0, r, :], C("OS")[:, 256 - Kn:256], start=False, stop=True, inc=(r == nh - 1), w=(lu,))
                    return m

                def values(po, pt):
                    for r in range(nh):
                        for kb in range(nb):
                            c = ((h0 + r) % 4) * 128
                            q = r * nb + kb
                            m = mm(po[:, c:c + 128], pt[:, q * 128:q * 128 + 128], bv_[:, kb, (h0 + r) * 128:(h0 + r) * 128 + 128],
                                   start=(kb == 0), stop=(kb == nb - 1), inc=(r == nh - 1 and kb == nb - 1))
                    return m

                t = dict(Kn=Kn, nh=nh, scale=1.0, scores=scores, values=values, new=first)
                if lastt:
                    n0, hq = len(tasks) + 1 - 4 // nh, h0 // 4

                    def fin(po, pv):
                        w4 = wgt[:, 0:4].rearrange("p (a b) -> p a b", b=nh)
                        z4 = zsum[:, n0:n0 + 4 // nh, 0:nh]
                        vdo(lambda e: e.reciprocal(w4, z4), w=(A.last(), R1["oa"]))
                        o = scr[:, tb, 1024 + hq * 512:1024 + hq * 512 + 512].rearrange("p (h d) -> p h d", h=4)
                        R1["fox"] = tt(o, po.rearrange("p (h d) -> p h d", h=4), bc(wgt[:, 0:4], 2, [P, 4, 128]), MUL, w=(pv,))
                    t["fin"] = fin
                tasks.append(t)

            for hq in range(2):
                task(0, 4 * hq, 4, True, True)
            for hq in range(2):
                for r in range(2):
                    task(1, 4 * hq + 2 * r, 2, r == 0, r == 1)
            yield from attend(tasks)

        def ev_ua(it, banks, last):
            n = int(it["name"][-1])
            ms = []
            for tb in range(2):
                s_ = W[:, n * 1024 + tb * 512:n * 1024 + tb * 512 + 512]
                ms.append(tt(s_, s_, banks[tb], MUL, w=(last, R1[f"2ga{n}"])))
            return ms

        def ev_ub(it, banks, last):
            n = int(it["name"][-1])
            ms = []
            for tb in range(2):
                sa = W[:, n * 1024 + tb * 512:n * 1024 + tb * 512 + 512]
                s_ = W[:, 4096 + n * 1024 + tb * 512:4096 + n * 1024 + tb * 512 + 512]
                o = scr[:, tb, n * 512:n * 512 + 512]
                m = tt(s_, s_, banks[tb], MUL, w=(last, R1[f"2gb{n}"]))
                ms.append(m)
                R1[f"mg{n}"] = tt(o, s_, sa, ADD, w=(m, R1["o_T"]))

            def transposes():
                for j in range(0, 4, 2):
                    tiles_T("h", 4 * n + j, n * 512 + j * 128, (R1[f"mg{n}"],), prior=(R1[f"mg{n}"],))

            later.append((pe_units[0] + 2, transposes))
            return ms

        def ev_acc(dst, add, row=None):
            def ev(it, banks, last):
                n = int(it["name"][-1])
                ms = []
                for tb in range(2):
                    o = dst[:, tb, n * 512:n * 512 + 512]
                    ms.append(tt(o, o, banks[tb], ADD, w=(last,)) if add else act(o, banks[tb], w=(last,)))
                    if row is not None:
                        row.add(tb, n, o, (ms[-1],))
                R1["acc"] = ms[-1]
                if add:
                    V.wait(ms[-1])
                return ms
            return ev

        def ev_os(it, banks, last):
            n = int(it["name"][-1])
            ms = []
            for tb in range(2):
                o = h[:, tb, n * 512:n * 512 + 512]
                ms.append(stt(o, banks[tb], rowS.rs[:, tb:tb + 1], o, MUL, ADD, w=(last, rowS.m)))
            chunk_T(n, ms[-1], rowF, "fnw")
            return ms

        def chunk_T(n, m, row, wname, src=h, delay=1, prior=None):
            def go():
                for tb in range(2):
                    row.add(tb, n, src[:, tb, n * 512:n * 512 + 512], (m,))
                for j in range(0, 4, 2):
                    tiles_T("x", 4 * n + j, n * 512 + j * 128, (m,), wcols=lambda k: C(wname)[:, k:k + 1] if isinstance(wname, str) else wname[:, k:k + 1],
                            prior=(prior or m,), src=src)
                if n == 3:
                    row.finish()
            if delay:
                later.append((pe_units[0] + delay, go))
            else:
                go()

        rowA, rowS, rowF, rowX, rowY, rowP, rowZ = Row(D, 4), Row(1024, 2), Row(D, 4), Row(D, 4), Row(D, 4), Row(D, 4), Row(D, 4)
        rowG = Row(D, 4)
        fwn = small(16)
        SXt = SX

        xt = scr[:, :, :].rearrange("p a b -> p (a b)").rearrange("p (k t) -> p k t", k=KT)
        n_c = [0]

        def load(sem_, o, i):
            n_c[0] += 1
            S.queue.append((lambda e: e.dma_start(o, i).then_inc(sem_, 16), False))

        s_xt = [sem(f"s_xt{i}") for i in range(4)]
        load(s_c, cst[:, 0:NPAR], ins["cst"][:, 0:NPAR])
        load(s_xt[0], xt[:, 0:4, :], ins["xT"][:, 0:4, :])
        pump_dma(1)
        load(s_xt[1], xt[:, 4:8, :], ins["xT"][:, 4:8, :])
        pump_dma(3)
        load(s_xt[2], xt[:, 8:12, :], ins["xT"][:, 8:12, :])
        pump_dma()
        load(s_xt[3], xt[:, 12:16, :], ins["xT"][:, 12:16, :])
        for tb in range(2):
            load(s_x, h[:, tb, :], ins["x"][tb])
        load(s_k, cst[:, NPAR:], ins["cst"][:, NPAR:])
        A.wait((s_c, 16))
        V.wait((s_c, 16))

        def x_tiles(q):
            for k in range(4 * q, 4 * q + 4):
                w = C("anw")[:, k:k + 1]
                hi = act(xhi[:, k, :], xt[:, k, :], w=((s_xt[q], 16),), scale=w, own=False)
                lo = stt(xlo[:, k, :], xt[:, k, :], w, xhi[:, k, :].bitcast(F), MUL, SUB, w=(hi, (s_xt[q], 16)))
                opnd_ready["x"][k] = (hi, lo)

        def start_side():
            yield
            x_tiles(1)
            yield
            x_tiles(2)
            yield
            x_tiles(3)
            for _ in range(6):
                yield
            for tb in range(2):
                for c in range(4):
                    rowA.add(tb, c, h[:, tb, c * 512:c * 512 + 512], ((s_x, 32),))
                yield
            rowA.finish()
            E.wait((s_k, 16))
            V.wait((s_k, 16))
            A.wait((s_k, 16))
            R1["RB"] = spread(rowA.rs, (rowA.m,))
            held.pop()()
            yield

        x_tiles(0)
        side = start_side()
        next(side)
        run(["1k"], ev_feat(kraw, None), side, defer=True)
        run(["1q0"], ev_feat(qf, None), side)
        for _ in side:
            pass
        assert not held
        run(["1q1"], ev_feat(qf, None), rope(kraw, kr, 4, (R1["1k"],)))
        run(["1v"], ev_v, rope(qf, qr, 8, (R1["1q1"],)))
        run(["1g"], ev_g1)
        att = attention1()
        run(["1c"], ev_feat(ckv, None), att)
        side = both(att, flatten())
        run(["1x0"], ev_conv, side)
        run(["1mk", "1mv"], ev_cmp, att)

        def second():
            yield from att
            yield from compressed()
            yield from attention_T()
            yield from ssd()

        side = second()
        run(["1x1", "1x2"], ev_conv, side)
        run(["1z0", "1z1"], ev_z, side)
        while opnd_ready["h"][7] is None:
            next(side)
        run([f"1oa{c}" for c in range(4)], ev_acc(h, True), side)
        for _ in side:
            pass
        before = (V.last(), A.last(), E.last())
        run([f"1os{c}" for c in range(4)], ev_os)
        mb = load_bcw(0, before)

        def done1(c, m):
            chunk_T(c, m, rowX, fwn)

        A.wait(tt(fwn, C("fnl"), C("nmp"), MUL))
        ffn(1, True, rowF, done1, before=before)
        lower_bounds()

        def x2():
            yield
            V.wait(mb)
            for tb in range(2):
                for c in range(4):
                    o = h[:, tb, c * 512:c * 512 + 512]
                    m = stt(o, o, rowX.rs[:, tb:tb + 1], bcw[:, c * 512:c * 512 + 512], MUL, MUL, w=(rowX.m, E.last()))
                    rowZ.add(tb, c, o, (m,))
                    if c % 2:
                        yield
            m = rowZ.finish()
            R1["rsB"] = tt(rsB, rowZ.rs, rowX.rs, MUL)
            while not held:
                yield
            R1["RB"] = spread(rsB, (R1["rsB"],))
            held.pop()()
            yield
            S.wait(m)
            S.queue.append((lambda e: e.dma_start(keep, h[:, :, :].rearrange("p a b -> p (a b)")).then_inc(s_keep, 16), False))

        keep = nc.dram_tensor("keep", (P, 2 * D), F, kind="Internal").ap()
        ones256 = C("OS")[:, 0:1].to_broadcast([P, T])
        side = x2()
        run(["2af0"], ev_af, side, defer=True)
        run(["2af1"], ev_af, side)
        for _ in side:
            pass
        run(["2aq0", "2aq1"], ev_feat(aq, None))
        run(["2ai0", "2ai1"], ev_t1024(ai))
        V.wait((s_keep, 16))
        side = hgrn()
        run(["2ag0", "2ag1"], ev_t1024(gsil, ACT.Silu), side)
        run(["2bq0", "2bq1"], ev_feat(bq, None, 128.0 ** -0.5), side)
        run(["2bk0", "2bk1"], ev_feat(bk, None), side)
        run(["2bv0", "2bv1"], ev_t1024(bv_), side)
        run(["2bf"], ev_bf, side)
        side = chain(side, fox())
        run([f"2ga{c}" for c in range(4)], ev_ga(0), side)
        run([f"2gb{c}" for c in range(4)], ev_ga(1), side)
        for _ in side:
            pass
        xdone = E.last()
        m = V.last()
        for k in range(0, 8, 2):
            tiles_T("x", k, k * 128, (R1["oa"],), wcols=lambda kk: C("hnw"), prior=(xdone,))
        for k in range(8, 16, 2):
            R1["o_T"] = tiles_T("x", k, k * 128, (R1["fox"],), prior=(xdone,))
        S.wait(R1["o_T"])
        S.queue.append((lambda e: e.dma_start(h[:, :, :].rearrange("p a b -> p (a b)"), keep).then_inc(s_keep, 16), False))
        mb = load_bcw(1, [V.last(), A.last(), E.last()])
        run([f"2ua{c}" for c in range(4)], ev_ua)
        run([f"2ub{c}" for c in range(4)], ev_ub)
        before = (V.last(), A.last(), E.last())

        def ev_o(it, banks, last):
            c = int(it["name"][-1])
            ms = []
            for tb in range(2):
                rowY.add(tb, c, banks[tb], (last,))
                ms.append(tt(scr[:, tb, c * 512:c * 512 + 512], banks[tb], bcw[:, c * 512:c * 512 + 512], MUL, w=(rowY.m, mb)))
            return ms

        run([f"2o{c}" for c in range(4)], ev_o)
        mb2 = load_bcw(2, [V.last()])
        V.wait((s_keep, 32))
        rowY.finish()

        def post(c, row, tb):
            y, o = scr[:, tb, c * 512:c * 512 + 512], h[:, tb, c * 512:c * 512 + 512]
            return stt(o, y, row.rs[:, tb:tb + 1], o, MUL, ADD, w=(row.m,), own=False)

        prior = E.last()

        def posts():
            for c in range(4):
                post(c, rowY, 0)
                chunk_T(c, post(c, rowY, 1), rowP, "nfp", delay=0, prior=prior)
                yield
                if c:
                    yield

        def done2(c, m):
            for tb in range(2):
                y = scr[:, tb, c * 512:c * 512 + 512]
                rowG.add(tb, c, y, (m,))
                m = tt(y, y, bcw[:, c * 512:c * 512 + 512], MUL, w=(rowG.m, mb2))

        side = posts()
        next(side)
        ffn(2, False, rowP, done2, side=side, before=before)
        flush()
        rowG.finish()
        for c in range(4):
            for tb in range(2):
                S.wait(post(c, rowG, tb))
                S.queue.append((lambda e, tb=tb, c=c: e.dma_start(out[tb][:, c * 512:c * 512 + 512], h[:, tb, c * 512:c * 512 + 512]).then_inc(s_out, 16), False))
        S.wait((s_out, 16 * 8))
        assert item_at[0] == len(items) and state["dma"] == len(units)

        with nc.Block() as block:
            @block.sync
            def _(e):
                S.play(e)

            @block.scalar
            def _(e):
                A.play(e)

            @block.vector
            def _(e):
                V.play(e)

            @block.tensor
            def _(e):
                E.play(e)


def constants():
    f = np.float32
    j = np.arange(128)
    c = np.zeros((128, NCST - NPAR), f)

    def put(name, a):
        o, w = OFF[name]
        c[:a.shape[0], o - NPAR:o - NPAR + w] = a.reshape(a.shape[0], -1)

    put("ident", np.eye(128, dtype=f))
    put("U", (j[:, None] <= j[None, :]).astype(f))
    SU = (j[:, None] > j[None, :]).astype(f)
    put("OS", np.concatenate([np.ones((128, 128), f), SU], 1))
    d = j % 64
    perm = np.zeros((128, 128), f)
    for m in range(128):
        if d[m] < 8:
            perm[m + 8, m] = 1
        elif d[m] < 16:
            perm[m - 8, m] = 1
    put("perm", perm)
    put("cm", np.concatenate([np.zeros((128, 128), f), np.where(j[None, :] > j[:, None], f(NEG), f(0))], 1))
    lev = np.zeros((8, 128, 128), f)
    lev[0] = np.eye(128)
    for i, m in enumerate(LEVELS):
        s, t = j[:, None], j[None, :]
        lev[1 + i] = (s // (2 * m) == t // (2 * m)) & (s % (2 * m) < m) & (t % (2 * m) >= m)
    put("lev", lev.transpose(1, 0, 2).reshape(128, -1))
    inv = (f(1.0) / (f(500000.0) ** (np.arange(0, 16, 2, dtype=f) / f(16)))).astype(f)
    ang = (np.arange(T, dtype=f)[:, None] * inv[None, :]).astype(f)
    cos, sin = np.cos(ang).astype(f), np.sin(ang).astype(f)
    ct, st = np.ones((128, T), f), np.zeros((128, T), f)
    for m in range(128):
        if d[m] < 8:
            ct[m], st[m] = cos[:, d[m]], -sin[:, d[m]]
        elif d[m] < 16:
            ct[m], st[m] = cos[:, d[m] - 8], sin[:, d[m] - 8]
    put("cos", ct)
    put("sin", st)
    t = np.arange(T).reshape(2, 128)
    ok = (np.arange(15) * 16 + 31)[None, None, :] <= t[:, :, None]
    put("cadd", np.where(ok, f(0), f(-1e30)).transpose(1, 0, 2))
    put("cmul", ok.astype(f).transpose(1, 0, 2))
    put("bd", (np.arange(120)[:, None] // 15 == np.arange(8)[None, :]).astype(f))
    return c


def pack(w, chunks):
    k = w.shape[0]
    return np.ascontiguousarray(w.reshape(k // 256, 2, 128, chunks, CH).transpose(3, 0, 2, 1, 4)).reshape(chunks, k // 256, 128, 2 * CH)


def narrow(w):
    n = w.shape[1]
    return np.ascontiguousarray(w.reshape(16, 128, n).transpose(1, 0, 2)).reshape(1, 128, 16 * n)


def feat(v, n):
    return v.reshape(n, 128).T


def rep(v):
    return np.broadcast_to(v.reshape(1, -1), (128, v.size))


def kernel(**inputs):
    import concourse.bacc as bacc
    from concourse.bass_utils import run_bass_kernel_spmd

    a = {k: np.asarray(v) for k, v in inputs.items()}
    w = a["w_in"][0]
    z, xbc, dtr, q, kc, vc, ks, vs, kw, vw, gate = np.split(w, np.cumsum([1024, 1536, 16, 1024] + [256] * 6), axis=1)
    order = [h for i in range(2) for r in range(4) for h in (8 * i + r, 8 * i + 4 + r)]
    q = q.reshape(D, 16, 64)[:, order, :].reshape(D, 1024)
    w1 = np.concatenate([ks, kw, q, vs, vw, kc, vc, xbc, z], axis=1)
    w2 = a["w_in_2"][0]
    aq, af, ai, ag, bq, bk, bv, bf, ga, gb = np.split(w2, np.cumsum([1024] * 7 + [8, 2048]), axis=1)
    w2p = np.concatenate([af, aq, ai, ag, bq, bk, bv, ga, gb], axis=1)
    cw = a["conv_w"][0]
    cols = [feat(a["attn_norm_w"][0], 16), feat(a["ffn_norm_w"][0], 16), feat(a["ssd_norm_w"][0], 8),
            cw.reshape(4, 12, 128).transpose(2, 1, 0).reshape(128, 48), feat(a["conv_b"][0], 12)]
    for n in ("cmp_pe_k", "cmp_pe_v"):
        pe = a[n][0].T
        cols.append(np.concatenate([pe, pe], axis=0))
    cols += [feat(a["norm_mix_pre_2"][0], 16), feat(a["norm_ffn_pre_2"][0], 16), feat(a["hgrn_lb_logits_2"][0], 8),
             feat(a["hgrn_lb_logits_2"][1], 8), a["hgrn_norm_w_2"][0].reshape(128, 1), rep(a["dt_bias"][0]), rep(a["a_log"][0]),
             rep(a["d_skip"][0]), rep(a["b_fox_f_2"][0]), feat(a["final_norm_w"], 16)]
    k2 = a["cmp_w2_k"][0].reshape(2, 128, 64).transpose(1, 0, 2)
    v2 = a["cmp_w2_v"][0].reshape(2, 128, 64).transpose(1, 0, 2)
    cols += [np.concatenate([k2, k2], axis=2).reshape(128, 256), v2.reshape(128, 128)]
    cols.append(constants())
    arrays = {
        "x": a["x"].reshape(2, 128, D),
        "xT": a["x"].reshape(T, KT, 128).transpose(2, 1, 0),
        "cst": np.concatenate(cols, axis=1),
        "wb": np.stack([rep(a["final_norm_w"]), rep(a["norm_mix_post_2"][0]), rep(a["norm_ffn_post_2"][0])]),
        "w_in1": pack(w1, 10),
        "w_n1": narrow(np.concatenate([dtr, gate], axis=1)),
        "cmp1": np.stack([a[n][0].reshape(4, 4, 128, 256).transpose(0, 2, 1, 3).reshape(4, 128, 1024) for n in ("cmp_w1_k", "cmp_w1_v")]),
        "w_out1": pack(a["w_out"][0], 4),
        "gu1": np.stack([pack(a["w_gate"][0], NCH), pack(a["w_up"][0], NCH)]),
        "dn1": pack(a["w_down"][0], 4),
        "w_in2": pack(w2p, 22),
        "w_n2": narrow(bf),
        "w_up": np.stack([pack(a["w_up_a_2"][0], 4), pack(a["w_up_b_2"][0], 4)]),
        "w_o": pack(a["w_o_2"][0], 4),
        "gu2": np.stack([pack(a["w_ffn_in_2"][0][:, :FF], NCH), pack(a["w_ffn_in_2"][0][:, FF:], NCH)]),
        "dn2": pack(a["w_ffn_down_2"][0], 4),
    }
    arrays = {"in_" + k: np.ascontiguousarray(v) for k, v in arrays.items()}
    nc = bacc.Bacc("TRN2", target_bir_lowering=False, num_devices=1, dynamic_dma_scratch_size=1024)
    ins = {k[3:]: nc.dram_tensor(k, v.shape, mybir.dt.float32, kind="ExternalInput").ap() for k, v in arrays.items()}
    out = nc.dram_tensor("out_x", (2, 128, D), mybir.dt.float32, kind="ExternalOutput").ap()
    build(nc, ins, out)
    r = run_bass_kernel_spmd(nc, [arrays], core_ids=[0])
    return r.results[0]["out_x"].reshape(1, T, D)
```

```python
import numpy as np

import concourse.bass as bass
from concourse import mybir
from contextlib import ExitStack

P = 128
D = 2048
T = 256
KT = D // P
CH = 512
FF = 5632
NCH = FF // CH
GROUPS = [(0, 4), (4, 8), (8, 11)]
NRAW = 5
NSPL = 4
EPS = 1e-6
NEG = -8e30
LEVELS = [64, 32, 16, 8, 4, 2, 1]

_CONST = [("w2k", 256), ("w2v", 128), ("ident", 128), ("U", 128), ("OS", 256), ("perm", 128), ("cm", 256), ("lev", 1024),
          ("cos", 256), ("sin", 256), ("cadd", 30), ("cmul", 30), ("bd", 8)]
_PARAM = [("anw", 16), ("fnw", 16), ("snw", 8), ("convw", 48), ("convb", 12), ("pek", 32), ("pev", 32),
          ("nmp", 16), ("nfp", 16), ("lb0", 8), ("lb1", 8), ("hnw", 1), ("dtb", 16), ("alog", 16),
          ("dsk", 16), ("bfox", 8), ("fnl", 16)]
NPAR = sum(w for _, w in _PARAM)
OFF = {}
_at = 0
for _n, _w in _PARAM + _CONST:
    OFF[_n] = (_at, _w)
    _at += _w
NCST = _at


class Engine:

    def __init__(self, sem):
        self.sem, self.n, self.queue, self.seen = sem, 0, [], {}

    def do(self, fn, inc=True):
        self.n += inc
        self.queue.append((fn, inc))
        return (self.sem, self.n)

    def wait(self, *marks):
        for m in marks:
            if m is not None and self.seen.get(m[0].name, 0) < m[1]:
                self.seen[m[0].name] = m[1]
                self.queue.append((m, None))

    def last(self):
        return (self.sem, self.n) if self.n else None

    def play(self, eng):
        for fn, inc in self.queue:
            if inc is None:
                eng.wait_ge(fn[0], fn[1])
            else:
                ins = fn(eng)
                if inc:
                    ins.then_inc(self.sem, 1)


def build(nc, ins, out):
    F = mybir.dt.float32
    R = mybir.dt.float32r
    I32 = mybir.dt.int32
    ALU = mybir.AluOpType
    ACT = mybir.ActivationFunctionType
    AX = mybir.AxisListType.X
    MUL, ADD, SUB, MAX, MIN = ALU.mult, ALU.add, ALU.subtract, ALU.max, ALU.min

    ctx = ExitStack()
    with ctx:
        def sb(name, shape, dt=F):
            return ctx.enter_context(nc.sbuf_tensor(name, shape, dt))

        def sem(name):
            return ctx.enter_context(nc.semaphore(name))

        raw = sb("raw", [P, NRAW, 1024])
        whi = sb("whi", [P, NSPL, 1024], R)
        wlo = sb("wlo", [P, NSPL, 1024], R)
        xhi = sb("xhi", [P, KT, T], R)
        xlo = sb("xlo", [P, KT, T], R)
        h = sb("h", [P, 2, D])
        scr = sb("scr", [P, 2, D])
        cst = sb("cst", [P, NCST])
        sm = sb("sm", [P, 1280])
        RB = sb("RB", [P, T])
        thin = sb("thin", [64, T])
        WN = (nc.sbuf_bytes_remaining // 4 - 64) // 2 * 2
        with nc.sbuf_tensor("W", [P, WN], F) as Wt:
            W = Wt
        hhi = sb("hhi", [P, KT, T], R)
        hlo = sb("hlo", [P, KT, T], R)
        ps = ctx.enter_context(nc.psum_tensor("ps", [P, 8, 512], F))

        def C(name, rows=P):
            o, w = OFF[name]
            return cst[0:rows, o:o + w]

        V = Engine(sem("s_dve"))
        A = Engine(sem("s_act"))
        E = Engine(sem("s_pe"))
        S = Engine(sem("s_sp"))
        s_raw = [sem(f"s_raw{i}") for i in range(NRAW)]
        s_x = sem("s_x")
        s_c = sem("s_c")
        s_bc = sem("s_bc")
        s_out = sem("s_out")
        s_k = sem("s_k")
        s_keep = sem("s_keep")

        def W_(o, *shape):
            n = int(np.prod(shape))
            ap = W[:, o:o + n]
            if len(shape) == 2:
                return ap.rearrange("p (a b) -> p a b", a=shape[0])
            if len(shape) == 3:
                return ap.rearrange("p (a b c) -> p a b c", a=shape[0], b=shape[1])
            if len(shape) == 4:
                return ap.rearrange("p (a b c d) -> p a b c d", a=shape[0], b=shape[1], c=shape[2])
            return ap

        sm_at = [0]

        def small(*shape):
            n = int(np.prod(shape))
            o = sm_at[0]
            sm_at[0] += n
            ap = sm[:, o:o + n]
            if len(shape) == 2:
                return ap.rearrange("p (a b) -> p a b", a=shape[0])
            return ap

        def bc(ap, axis, shape):
            return ap.unsqueeze(axis).to_broadcast(shape)

        def act(o, i, f=ACT.Copy, w=(), own=True, **kw):
            A.wait(*w)
            if own:
                A.wait(A.last())
            return A.do(lambda e: e.activation(o, i, f, **kw))

        def tt(o, a, b, op, w=(), own=True):
            V.wait(*w)
            if own:
                V.wait(V.last())
            return V.do(lambda e: e.tensor_tensor(o, a, b, op))

        def ts(o, a, s1, s2, op0, op1=None, w=()):
            V.wait(*w, V.last())
            if op1 is None:
                return V.do(lambda e: e.tensor_scalar(o, a, s1, None, op0))
            return V.do(lambda e: e.tensor_scalar(o, a, s1, s2, op0, op1))

        def stt(o, a, s, b, op0, op1, w=(), own=True):
            V.wait(*w, V.last() if own else None)
            return V.do(lambda e: e.scalar_tensor_tensor(out=o, in0=a, scalar=s, in1=b, op0=op0, op1=op1))

        def vdo(fn, w=()):
            V.wait(*w, V.last())
            return V.do(fn)

        def vcopy(o, a, w=()):
            V.wait(*w, V.last())
            return V.do(lambda e: e.tensor_copy(o, a))

        def mm(o, l, r, start=True, stop=True, inc=False, w=(), skip=False):
            E.wait(*w)
            return E.do(lambda e: e.matmul(o, l, r, start=start, stop=stop, skip_group_check=skip), inc)

        def tp(o, i, inc=False, w=()):
            E.wait(*w)
            k = i.shape[0]
            return E.do(lambda e: e.transpose(o, i, C("ident")[0:k, 0:k]), inc)

        class Banks:
            def __init__(self):
                self.free, self.idle = [[] for _ in range(4)], [0, 1, 2, 3]

            def get(self):
                i = self.idle.pop(0)
                E.wait(*self.free[i])
                return i

            def ap(self, i):
                return ps[:, 4 + i, :]

            def put(self, i, *marks):
                self.idle.append(i)
                self.free[i] = list(marks)

        B = Banks()

        items = []

        def item(name, src, kind, ks, ncols, opnd="x", rawonly=False):
            items.append(dict(name=name, src=src, kind=kind, ks=ks, nc=ncols, op=opnd, raw=rawonly))

        def kpairs(a, b):
            return [[k, k + 1] for k in range(a, b, 2)]

        w_in1, w_n1, cmp1, w_outd, gu1, dn1 = (ins[n] for n in ("w_in1", "w_n1", "cmp1", "w_out1", "gu1", "dn1"))
        names = ["k", "q0", "q1", "v", "c", "x0", "x1", "x2", "z0", "z1"]
        kinds = dict(k="feat", q="feat", v="tok", c="feat", x="feat", z="tok")
        for n, nm in enumerate(names):
            item("1" + nm, w_in1[n], kinds[nm[0]], kpairs(0, KT), CH)
            if nm == "v":
                item("1g", w_n1, "thin", [list(range(KT))], 64)
            if nm == "x0":
                item("1mk", cmp1[0], "cmp", [list(range(4 * u, 4 * u + 4)) for u in range(4)], 256, rawonly=True)
                item("1mv", cmp1[1], "cmp", [list(range(4 * u, 4 * u + 4)) for u in range(4)], 256, rawonly=True)
        for c in range(4):
            item(f"1oa{c}", w_outd[c][4:8], "tok", kpairs(0, 8), CH, "h")
        for c in range(4):
            item(f"1os{c}", w_outd[c][0:4], "tok", kpairs(8, 16), CH, "h")

        def ffn_items(b, gu, dn):
            for g, (c0, c1) in enumerate(GROUPS):
                for c in range(c0, c1):
                    item(f"{b}fg{c}", gu[0][c], "tok", kpairs(0, KT), CH)
                    item(f"{b}fu{c}", gu[1][c], "tok", kpairs(0, KT), CH)
                for c in range(4):
                    item(f"{b}fd{g}_{c}", dn[c][2 * c0:2 * c1], "tok", kpairs(0, 4 * (c1 - c0)), CH, "h")

        ffn_items(1, gu1, dn1)
        w_in2 = ins["w_in2"]
        names = (["af0", "af1", "aq0", "aq1", "ai0", "ai1", "ag0", "ag1", "bq0", "bq1", "bk0", "bk1", "bv0", "bv1"]
                 + [f"ga{c}" for c in range(4)] + [f"gb{c}" for c in range(4)])
        for n, nm in enumerate(names):
            item("2" + nm, w_in2[n], "feat" if nm[:2] in ("af", "aq", "bq", "bk") else "tok", kpairs(0, KT), CH)
            if nm == "bv1":
                item("2bf", ins["w_n2"], "thin", [list(range(KT))], 8)
        for c in range(4):
            item(f"2ua{c}", ins["w_up"][0][c], "tok", kpairs(0, 8), CH)
        for c in range(4):
            item(f"2ub{c}", ins["w_up"][1][c], "tok", kpairs(8, 16), CH)
        for c in range(4):
            item(f"2o{c}", ins["w_o"][c], "tok", kpairs(0, KT), CH, "h")
        ffn_items(2, ins["gu2"], ins["dn2"])

        units = []
        for it in items:
            it["first"] = len(units)
            for u, ks in enumerate(it["ks"]):
                units.append(dict(item=it, u=u, ks=ks, src=it["src"][u], n=len(ks) * it["nc"]))

        state = dict(dma=0, split=0, cut=0)

        def pump_dma(upto=10 ** 9):
            while state["dma"] < min(len(units), upto):
                j = state["dma"]
                if j >= NRAW:
                    old = units[j - NRAW]
                    if "freed" not in old:
                        return
                    S.wait(*old["freed"])
                u = units[j]
                slot = j % NRAW
                S.queue.append((lambda e, u=u, slot=slot: e.dma_start(raw[:, slot, 0:u["n"]], u["src"]).then_inc(s_raw[slot], 16), False))
                u["landed"] = (s_raw[slot], 16 * (j // NRAW + 1))
                state["dma"] += 1

        split_free = [None] * NSPL

        def pump_split(upto):
            while state["split"] <= min(upto, len(units) - 1):
                j = state["split"]
                state["split"] += 1
                u = units[j]
                if u["item"]["raw"]:
                    continue
                pump_dma()
                s = state["cut"] % NSPL
                state["cut"] += 1
                u["slot"] = s
                n, r = u["n"], j % NRAW
                hi = act(whi[:, s, 0:n], raw[:, r, 0:n], w=(u["landed"], split_free[s]), own=False)
                lo = tt(wlo[:, s, 0:n], raw[:, r, 0:n], whi[:, s, 0:n].bitcast(F), SUB, w=(hi, split_free[s]), own=False)
                u["hi"], u["lo"] = hi, lo
                split_free[s] = None
                u["freed"] = (hi, lo)
                pump_dma()

        pair_free = [[], []]
        opnd_ready = {"x": [None] * KT, "h": [None] * KT}
        opnds = {"x": (xhi, xlo), "h": (hhi, hlo)}
        later = []

        def due(n):
            for t in [t for t in later if t[0] <= n]:
                later.remove(t)
                t[1]()

        pe_units = [0]
        pair_at = [0]

        held = []

        def run_item(it, evac, defer=False):
            pair = pair_at[0] % 2
            pair_at[0] += 1
            banks = [ps[:, 2 * pair, :], ps[:, 2 * pair + 1, :]]
            hi_t, lo_t = opnds[it["op"]]
            nU = len(it["ks"])
            ncol = it["nc"]
            for ui in range(nU):
                gi = it["first"] + ui
                u = units[gi]
                pump_split(gi + NSPL - 1)
                pump_dma()
                if ui == 0:
                    E.wait(*pair_free[pair])
                if it["raw"]:
                    E.wait(u["landed"])
                    w4 = raw[:, gi % NRAW, 0:u["n"]].rearrange("p (k n) -> p k n", n=ncol)
                    kv = 0 if it["name"] == "1mk" else 1
                    for kk, k in enumerate(u["ks"]):
                        last = mm(banks[0][0:60, 0:256], flat[:, kv, k, :], w4[:, kk, :], start=(k == 0), stop=(k == 15),
                                  inc=(kk == len(u["ks"]) - 1), w=flat_ready if kk == 0 else ())
                    u["freed"] = (last,)
                    pump_dma()
                else:
                    E.wait(u["hi"])
                    s = u["slot"]
                    wh = whi[:, s, 0:u["n"]].rearrange("p (k n) -> p k n", n=ncol)
                    wl = wlo[:, s, 0:u["n"]].rearrange("p (k n) -> p k n", n=ncol)
                    nk = len(u["ks"])
                    for kk, k in enumerate(u["ks"]):
                        E.wait(*(opnd_ready[it["op"]][k] or ()))
                        f0 = ui == 0 and kk == 0
                        l0 = ui == nU - 1 and kk == nk - 1
                        if it["kind"] == "thin":
                            o = banks[0][0:ncol, 0:T]
                            mm(o, wh[:, kk, :], hi_t[:, k, :], start=f0, stop=False)
                            mm(o, wh[:, kk, :], lo_t[:, k, :], start=False, stop=False)
                            last = mm(o, wl[:, kk, :], hi_t[:, k, :], start=False, stop=l0, inc=(kk == nk - 1), w=(u["lo"],))
                        elif it["kind"] == "tok":
                            for tb in range(2):
                                o = banks[tb][:, 0:ncol]
                                xh_ = hi_t[:, k, tb * 128:tb * 128 + 128]
                                xl_ = lo_t[:, k, tb * 128:tb * 128 + 128]
                                mm(o, xl_, wh[:, kk, :], start=f0, stop=False)
                                mm(o, xh_, wh[:, kk, :], start=False, stop=False)
                                last = mm(o, xh_, wl[:, kk, :], start=False, stop=l0, w=(u["lo"],),
                                          inc=(kk == nk - 1 and tb == 1))
                        else:
                            for ct in range(4):
                                o = banks[ct // 2][:, (ct % 2) * 256:(ct % 2) * 256 + 256]
                                wh_ = wh[:, kk, ct * 128:ct * 128 + 128]
                                wl_ = wl[:, kk, ct * 128:ct * 128 + 128]
                                mm(o, wh_, hi_t[:, k, :], start=(f0 and ct % 2 == 0), stop=False, skip=True)
                                mm(o, wh_, lo_t[:, k, :], start=False, stop=False, skip=True)
                                last = mm(o, wl_, hi_t[:, k, :], start=False, stop=l0, skip=True, w=(u["lo"],),
                                          inc=(kk == nk - 1 and ct == 3))
                    split_free[s] = last
                pe_units[0] += 1
                if ui == nU - 1:
                    if defer:
                        def put_off(pair=pair, banks=banks, last=last):
                            pair_free[pair] = list(evac(it, banks, last))

                        held.append(put_off)
                    else:
                        pair_free[pair] = list(evac(it, banks, last))
                due(pe_units[0])
                yield

        item_at = [0]

        def run(names, evac, side=None, defer=False):
            for nm in names:
                it = items[item_at[0]]
                item_at[0] += 1
                assert it["name"] == nm, (it["name"], nm)
                for _ in run_item(it, evac, defer):
                    if side is not None:
                        next(side, None)

        def flush():
            for t in list(later):
                later.remove(t)
                t[1]()

        def both(*gens):
            gens = list(gens)
            while gens:
                for g in list(gens):
                    if next(g, gens) is gens:
                        gens.remove(g)
                yield

        def chain(*gens):
            for g in gens:
                yield from g

        junk = W_(WN - 512, 512)
        ones = C("OS")[:, 0:128]

        class Row:
            def __init__(self, width, chunks):
                self.width, self.parts, self.rs, self.m = width, small(2, chunks), small(2), None

            def add(self, tb, c, src, w):
                self.m = act(junk[:, 0:src.shape[1]], src, ACT.Square, accum_out=self.parts[:, tb, c:c + 1], w=w)

            def finish(self):
                p, r = self.parts, self.rs
                m = self.m
                if p.shape[2] > 1:
                    m = vdo(lambda e: e.reduce_sum(r, p, AX), w=(m,))
                else:
                    m = vcopy(r, p[:, :, 0], w=(m,))
                m = ts(r, r, 1.0 / self.width, EPS, MUL, ADD, w=(m,))
                m = act(r, r, ACT.Sqrt, w=(m,))
                self.m = vdo(lambda e: e.reciprocal(r, r), w=(m,))
                return self.m

        def warm(src, w=()):
            act(junk[:, 1:2], src, ACT.Sqrt, w=w)

        RB2 = RB[:, :].unsqueeze(1).to_broadcast([P, 2, T])

        def spread(rs, w):
            for tb in range(2):
                m = ts(rsq[:, tb, :], ones, rs[:, tb:tb + 1], None, MUL, w=w)
            yield
            yield
            b = B.get()
            pb = B.ap(b)
            for tb in range(2):
                m = mm(pb[:, tb * 128:tb * 128 + 128], rsq[:, tb, :], C("ident"), inc=(tb == 1), w=(m,))
            R1["RB"] = vcopy(RB[:, :], pb[:, 0:256], w=(m,))
            B.put(b, R1["RB"])
            held.pop()()

        rsq = small(2, 128)

        def evac_split(dst, k, pb, m, wcols, prior):
            hi_t, lo_t = opnds[dst]
            A.wait(*prior)
            V.wait(*prior)
            if wcols is None:
                pv = pb.rearrange("p (a b) -> p a b", a=2)
                hi = act(hi_t[:, k:k + 2, :], pv, w=(m,), own=False)
                lo = tt(lo_t[:, k:k + 2, :], pv, hi_t[:, k:k + 2, :].bitcast(F), SUB, w=(hi,), own=False)
            else:
                for j in range(2):
                    hi = act(hi_t[:, k + j, :], pb[:, j * 256:j * 256 + 256], w=(m,), scale=wcols(k + j), own=False)
                for j in range(2):
                    lo = stt(lo_t[:, k + j, :], pb[:, j * 256:j * 256 + 256], wcols(k + j), hi_t[:, k + j, :].bitcast(F), MUL, SUB, w=(hi,))
            opnd_ready[dst][k] = opnd_ready[dst][k + 1] = (hi, lo)
            return (hi, lo)

        def tiles_T(dst, k, col, marks, wcols=None, prior=(), src=scr):
            b = B.get()
            pb = B.ap(b)
            for j in range(2):
                for tb in range(2):
                    m = tp(pb[:, j * 256 + tb * 128:j * 256 + tb * 128 + 128], src[:, tb, col + j * 128:col + j * 128 + 128],
                           inc=(j == 1 and tb == 1), w=marks)
            ms = evac_split(dst, k, pb, m, wcols, prior)
            B.put(b, *ms)
            return m

        G = W_(8192, 2, CH)
        Hb = W_(8192 + 1024, 2, CH)
        bcw = W_(WN - 512 - 2048, D)
        bc_n = [0]

        def load_bcw(i, marks):
            def go():
                S.wait(*marks)
                S.queue.append((lambda e: e.dma_start(bcw, ins["wb"][i]).then_inc(s_bc, 16), False))

            bc_n[0] += 1
            later.append((pe_units[0] + 4, go))
            return (s_bc, 16 * bc_n[0])

        fst = {}

        def ffn(b, acc_first, row, done, side=None, before=()):
            dst = h if b == 1 else scr

            def ev_gate(it, banks, last):
                ms = []
                for tb in range(2):
                    ms.append(act(G[:, tb, :], banks[tb], ACT.Silu, w=(last, fst.get("g_free"), row.m) + tuple(before), scale=row.rs[:, tb:tb + 1]))
                fst["g"] = ms[-1]
                return ms

            def ev_up(it, banks, last):
                c = int(it["name"][3:])
                ms = []
                for tb in range(2):
                    ms.append(stt(Hb[:, tb, :], banks[tb], row.rs[:, tb:tb + 1], G[:, tb, :], MUL, MUL, w=(last, fst["g"], fst.get("h_free")) + tuple(before)))
                fst["g_free"] = ms[-1]
                g0 = [a for a, z in GROUPS if a <= c < z][0]

                def transposes():
                    for j in range(0, 4, 2):
                        fst["h_free"] = tiles_T("h", 4 * (c - g0) + j, j * 128, (ms[-1],), prior=(fst.get("down"),), src=Hb)

                later.append((pe_units[0] + 2, transposes))
                return ms

            def ev_down(it, banks, last):
                c = int(it["name"].split("_")[1])
                g = int(it["name"][3])
                fst["down"] = last
                ms = []
                for tb in range(2):
                    o = dst[:, tb, c * CH:c * CH + CH]
                    if g == 0 and not acc_first:
                        ms.append(act(o, banks[tb], w=(last,)))
                    else:
                        ms.append(tt(o, o, banks[tb], ADD, w=(last, A.last() if g == 1 and not acc_first else None)))
                if g == 2:
                    done(c, ms[-1])
                return ms

            for g, (c0, c1) in enumerate(GROUPS):
                for c in range(c0, c1):
                    run([f"{b}fg{c}"], ev_gate, side)
                    run([f"{b}fu{c}"], ev_up)
                if g == 2:
                    warm(ones[:, 0:1])
                run([f"{b}fd{g}_{c}" for c in range(4)], ev_down)

        qf = W_(0, 8, T)
        qr = W_(2048, 8, T)
        kr = W_(4096, 4, T)
        vt = W_(5120, 2, CH)
        xT = W_(6144, 12, T)
        sz = W_(9216, 2, 1024)
        kraw = W_(11264, 4, T)
        ckv = W_(12288, 4, T)
        flat = W_(13312, 2, 16, 60)
        hid = W_(15232, 2, 2, 60)
        hrep = W_(15472, 2, 240)
        BD = W_(15952, 2, CH)
        SX = W_(16976, 512)
        SXs = [SX, W_(15952, 512)]
        PMs = [W_(17488, 512), W_(18000, 512)]
        PTs = [W_(18512, 512), W_(19024, 512)]
        RT = W_(20048, 512)
        hidT = W_(19536, 2, 256)
        CT = W_(20560, 4, T)
        kcT = W_(21584, 60)
        assert 21644 <= WN - 512, WN
        flat_ready = []
        gs = small(2, 48)
        dt = small(2, 16)
        aa = small(2, 16)
        zsum = small(24, 4)
        mnx = small(24, 4)
        mx16 = small(16)
        wgt = small(16)
        t16a = small(16)
        sp = [small(32) for _ in range(4)]
        ec = small(48)
        R1 = {}

        def ev_feat(dst, scale=None):
            def ev(it, banks, last):
                n = int(it["name"][-1]) if it["name"][-1].isdigit() else 0
                ms = []
                for b in range(2):
                    o = dst[:, n * 4 + 2 * b:n * 4 + 2 * b + 2, :]
                    pv = banks[b].rearrange("p (a b) -> p a b", a=2)
                    if scale is None:
                        ms.append(tt(o, pv, RB2, MUL, w=(last, R1["RB"])))
                    else:
                        ms.append(stt(o, pv, scale, RB2, MUL, MUL, w=(last, R1["RB"])))
                R1[it["name"]] = ms[-1]
                return ms
            return ev

        def softplus(o, x, n, w, neg, then):
            e, u, z, r = (s[:, 0:n] for s in sp)

            def first():
                m = ts(u, x, -1.0, None, MUL, w=w)
                m = tt(e, x, u, MAX, w=(m,))
                act(e, e, ACT.Exp, scale=-1.0, w=(m,))

            def second():
                m = ts(u, e, 1.0, None, ADD, w=(A.last(),))
                R1["ln"] = act(r, u, ACT.Ln, w=(m,))

            def third():
                m = ts(u, u, -1.0, None, ADD, w=(R1["ln"],))
                m = ts(z, u, 0.0, None, ALU.is_equal)
                m = tt(r, r, z, ADD)
                m = tt(u, u, z, ADD)
                vdo(lambda e_: e_.reciprocal(u, u))
                m = tt(r, r, e, MUL)
                m = tt(r, r, u, MUL)
                if neg:
                    m = stt(o, x, 0.0, r, MIN, SUB)
                else:
                    m = stt(o, x, 0.0, r, MAX, ADD)
                then(m)

            for i, f in enumerate((first, second, third)):
                later.append((pe_units[0] + 1 + i, f))

        def rope(src, dst, ntile, ready):
            pend = None
            for t in list(range(0, ntile, 2)) + [None]:
                if pend is not None:
                    b, m, p = pend
                    rv = RT[:, 0:512].rearrange("p (a b) -> p a b", a=2)
                    tt(dst[:, p:p + 2, :], src[:, p:p + 2, :], bc(C("cos"), 1, [P, 2, T]), MUL, w=ready)
                    m = tt(rv, B.ap(b).rearrange("p (a b) -> p a b", a=2), bc(C("sin"), 1, [P, 2, T]), MUL, w=(m,), own=False)
                    B.put(b, m)
                    R1["rope"] = tt(dst[:, p:p + 2, :], dst[:, p:p + 2, :], rv, ADD)
                if t is not None:
                    b = B.get()
                    m = mm(B.ap(b), C("perm"), src[:, t:t + 2, :].rearrange("p a b -> p (a b)"), inc=True, w=ready)
                    pend = (b, m, t)
                yield

        def attend(tasks):
            n = len(tasks)
            sx_free, pm_free, pt_free = [None, None], [None, None], [None, None]
            outs = {}
            if "prep" in tasks[0]:
                tasks[0]["prep"](E.last())
                yield
            for i in range(n + 5):
                if 4 <= i < n + 4:
                    j = i - 4
                    t = tasks[j]
                    t["pt"] = act(PTs[j % 2], B.ap(t["tb_"]), w=(t["tm"], pt_free[j % 2]), own=False)
                    B.put(t["tb_"], t["pt"])
                if 2 <= i < n + 2:
                    j = i - 2
                    t = tasks[j]
                    Kn, mn, zs = t["Kn"], mnx[:, j, :], zsum[:, j, :]
                    A.wait(t["sx"], pm_free[j % 2])
                    for r in range(t["nh"]):
                        m = act(PMs[j % 2][:, r * Kn:r * Kn + Kn], SXs[j % 2][:, r * Kn:r * Kn + Kn], ACT.Exp, scale=-1.0,
                                bias=mn[:, r:r + 1], accum_out=zs[:, r:r + 1], own=False)
                    t["pm"] = sx_free[j % 2] = m
                if 1 <= i < n + 1:
                    j = i - 1
                    t = tasks[j]
                    Kn, mn, pb, sx = t["Kn"], mnx[:, j, :], B.ap(t["sb_"]), SXs[j % 2]
                    mk = C("cm")[:, 256 - Kn:256]
                    V.wait(t["sm"], sx_free[j % 2])
                    for r in range(t["nh"]):
                        t["sx"] = V.do(lambda e, r=r, pb=pb, mn=mn, mk=mk, Kn=Kn, sc=t["scale"], sx=sx: e.tensor_tensor_reduce(
                            out=sx[:, r * Kn:r * Kn + Kn], in0=pb[:, r * Kn:r * Kn + Kn], in1=mk, scale=-sc, scalar=3e38,
                            op0=ADD, op1=MIN, accum_out=mn[:, r:r + 1]))
                    B.put(t["sb_"], t["sx"])
                if 5 <= i and "fin" in tasks[i - 5]:
                    t = tasks[i - 5]
                    t["fin"](B.ap(t["ob"]), t["pv"], t["pm"])
                    B.put(t["ob"], V.last())
                if 4 <= i < n + 4:
                    j = i - 4
                    t = tasks[j]
                    if t["new"]:
                        outs["b"] = B.get()
                    t["ob"] = outs["b"]
                    E.wait(t["pt"])
                    t["pv"] = pt_free[j % 2] = t["values"](B.ap(t["ob"]), PTs[j % 2])
                if 3 <= i < n + 3:
                    j = i - 3
                    t = tasks[j]
                    b = t["tb_"] = B.get()
                    pb = B.ap(b)
                    for q in range(4):
                        m = tp(pb[:, q * 128:q * 128 + 128], PMs[j % 2][:, q * 128:q * 128 + 128], inc=(q == 3), w=(t["pm"],))
                    t["tm"] = pm_free[j % 2] = m
                if i < n:
                    t = tasks[i]
                    t["sb_"] = B.get()
                    t["sm"] = t["scores"](B.ap(t["sb_"]))
                if i + 1 < n and "prep" in tasks[i + 1]:
                    tasks[i + 1]["prep"](tasks[i - 1]["sm"] if i else None)
                yield

        def att_o(tb, hh):
            return scr[:, tb, 1024 + hh * 512:1024 + hh * 512 + 512].rearrange("p (h d) -> p h d", h=8)

        def attention1():
            E.wait(R1["rope"], R1["1v"])
            tasks = []

            def task(tb, hh, br, g, r0, nh, first, lastt):
                Kn, p0 = 128 * (tb + 1), (g % 2) * 64
                nb = tb + 1

                def scores(pb):
                    for r in range(nh):
                        m = mm(pb[:, r * Kn:r * Kn + Kn], qr[p0:p0 + 64, (g // 2) * 4 + r0 + r, tb * 128:tb * 128 + 128],
                               kr[p0:p0 + 64, br * 2 + g // 2, 0:Kn], inc=(r == nh - 1))
                    return m

                def values(po, pt):
                    for r in range(nh):
                        for kb in range(nb):
                            q = r * nb + kb
                            c = (4 * (g % 2) + r0 + r) * 64
                            m = mm(po[:, c:c + 64], pt[:, q * 128:q * 128 + 128], vt[:, kb, br * 256 + g * 64:br * 256 + g * 64 + 64],
                                   start=(kb == 0), stop=(kb == nb - 1), inc=(r == nh - 1 and kb == nb - 1))
                    return m

                t = dict(Kn=Kn, nh=nh, scale=0.125, scores=scores, values=values, new=first)
                if lastt:
                    n0 = len(tasks) + 1 - 8 // nh

                    def fin(po, pv, pm):
                        w8 = wgt[:, 0:8].rearrange("p (a b) -> p a b", b=nh)
                        z8 = zsum[:, n0:n0 + 8 // nh, 0:nh]
                        vdo(lambda e: e.reciprocal(w8, z8), w=(pm, R1["1g"]))
                        gv = gs[:, tb, :].rearrange("p (h b) -> p h b", b=3)[:, 8 * hh:8 * hh + 8, br + 1]
                        tt(wgt[:, 0:8], wgt[:, 0:8], gv, MUL)
                        o = att_o(tb, hh)
                        pv_ = po.rearrange("p (h d) -> p h d", h=8)
                        if br == 0:
                            tt(o, pv_, bc(wgt[:, 0:8], 2, [P, 8, 64]), MUL, w=(pv,))
                        else:
                            rt = RT[:, 0:512].rearrange("p (h d) -> p h d", h=8)
                            m = tt(rt, pv_, bc(wgt[:, 0:8], 2, [P, 8, 64]), MUL, w=(pv,))
                            tt(o, o, rt, ADD)
                    t["fin"] = fin
                tasks.append(t)

            for tb in range(2):
                nh = 4 if tb == 0 else 2
                for hh in range(2):
                    for br in range(2):
                        part = [(g, r0) for g in (2 * hh, 2 * hh + 1) for r0 in range(0, 4, nh)]
                        for x, (g, r0) in enumerate(part):
                            task(tb, hh, br, g, r0, nh, x == 0, x == len(part) - 1)
            yield from attend(tasks)

        def compressed():
            V.wait(A.last())
            hs = [act(hid, hid, ACT.Silu, w=(R1["1mk"], R1["1mv"]))]
            yield
            b = B.get()
            pb = B.ap(b)
            w2k = C("w2k").rearrange("p (a b) -> p a b", a=2)
            w2v = C("w2v").rearrange("p (a b) -> p a b", a=2)
            for ht in range(2):
                m = mm(pb[:, 0:60], w2k[:, ht, :], hid[:, 0, ht, :], start=(ht == 0), stop=(ht == 1), inc=(ht == 1), w=hs)
            a = act(kcT, pb[:, 0:60], w=(m,))
            B.put(b, a)
            for ht in range(2):
                vcopy(hrep[:, ht, :].rearrange("p (g r i) -> p g r i", g=4, r=4),
                      hid[:, 1, ht, :].rearrange("p (g i) -> p g i", g=4).unsqueeze(2).to_broadcast([P, 4, 4, 15]), w=hs)
            mh = V.last()
            for gp in range(2):
                b = B.get()
                pb = B.ap(b)
                for ht in range(2):
                    m = mm(pb[0:120, 0:64], hrep[:, ht, gp * 120:gp * 120 + 120], w2v[:, ht, :],
                           start=(ht == 0), stop=(ht == 1), inc=(ht == 1), w=(mh,))
                m = tt(BD[0:120, gp, :].rearrange("p (c d) -> p c d", c=8), bc(pb[0:120, 0:64], 1, [120, 8, 64]),
                       bc(C("bd", 120), 2, [120, 8, 64]), MUL, w=(m,))
                B.put(b, m)
            mbd = m
            mt = E.last()
            yield
            for tb in range(2):
                bs = [B.get(), B.get()]
                for par in range(2):
                    for g2 in range(2):
                        for r in range(4):
                            p0, g = par * 64, 2 * g2 + par
                            m = mm(B.ap(bs[par])[:, (4 * g2 + r) * 15:(4 * g2 + r) * 15 + 15], qf[p0:p0 + 64, g2 * 4 + r, tb * 128:tb * 128 + 128],
                                   kcT[p0:p0 + 64, g * 15:g * 15 + 15], inc=(g2 == 1 and r == 3), w=(a,))
                yield
                s = SX[:, 0:240].rearrange("p (h i) -> p h i", i=15)
                s4 = SX[:, 0:240].rearrange("p (a b c) -> p a b c", a=2, b=2)
                e = PMs[0][:, 0:240].rearrange("p (h i) -> p h i", i=15)
                cadd = C("cadd")[:, tb * 15:tb * 15 + 15]
                cmul = C("cmul")[:, tb * 15:tb * 15 + 15]
                for par in range(2):
                    ml = act(s4[:, :, par, :], B.ap(bs[par])[:, 0:120].rearrange("p (a c) -> p a c", a=2), w=(m,), scale=0.125)
                    B.put(bs[par], ml)
                m = tt(s, s, bc(cadd, 1, [P, 16, 15]), ADD, w=(ml,))
                m = vdo(lambda e_: e_.reduce_max(mx16, s, AX))
                m = tt(s, s, bc(mx16, 2, [P, 16, 15]), SUB, w=(m,))
                m = act(e, s, ACT.Exp, w=(m, mt))
                V.wait(m)
                m = vdo(lambda e_: e_.reduce_sum(t16a[:, 0:16], e, AX))
                V.wait(m)
                m = vdo(lambda e_: e_.reciprocal(t16a, t16a))
                gv = gs[:, tb, :].rearrange("p (h b) -> p h b", b=3)[:, :, 0]
                mw = tt(t16a, t16a, gv, MUL, w=(m, R1["1g"]))
                m = tt(e, e, bc(cmul, 1, [P, 16, 15]), MUL, w=(m,))
                yield
                b = B.get()
                pb = B.ap(b)
                for gp in range(2):
                    mt = tp(pb[0:120, gp * 128:gp * 128 + 128], PMs[0][:, gp * 120:gp * 120 + 120], inc=(gp == 1), w=(m,))
                m = act(PTs[0][0:120, 0:256], pb[0:120, 0:256], w=(mt,))
                B.put(b, m)
                yield
                for gp in range(2):
                    b = B.get()
                    pb = B.ap(b)
                    mo = mm(pb, PTs[0][0:120, gp * 128:gp * 128 + 128], BD[0:120, gp, :], inc=True, w=(m, mbd))
                    rt = RT[:, 0:512].rearrange("p (h d) -> p h d", h=8)
                    m2 = tt(rt, pb.rearrange("p (h d) -> p h d", h=8), bc(t16a[:, 8 * gp:8 * gp + 8], 2, [P, 8, 64]), MUL, w=(mo, mw))
                    B.put(b, m2)
                    tt(att_o(tb, gp), att_o(tb, gp), rt, ADD, w=(m2,))
                yield

        def flatten():
            pes = [C("pek"), C("pev")]
            for kv in range(2):
                for par in range(2):
                    p0 = par * 64
                    for jp in range(2):
                        for q in range(2):
                            for hq in range(2):
                                src = ckv[p0:p0 + 64, kv * 2 + hq, :].rearrange("p (i j) -> p i j", j=16)
                                c0 = (2 * hq + par) * 15
                                o = flat[jp * 64:jp * 64 + 64, kv, 8 * q:8 * q + 8, c0:c0 + 15]
                                i_ = src[:, q:q + 15, jp:16:2].rearrange("p i j -> p j i")
                                pe = pes[kv][p0:p0 + 64, 16 * q + jp:16 * q + 16:2].unsqueeze(2).to_broadcast([64, 8, 15])
                                m = tt(o, i_, pe, ADD, w=(R1["1c"],), own=False)
                    if kv == 1 and par == 1:
                        flat_ready.append(m)
                    yield

        def ev_cmp(it, banks, last):
            kv = 0 if it["name"] == "1mk" else 1
            m = act(hidT[0:60, kv, :], banks[0][0:60, 0:256], w=(last,))

            def transposes():
                b = B.get()
                pb = B.ap(b)
                for ht in range(2):
                    mt = tp(pb[:, ht * 60:ht * 60 + 60], hidT[0:60, kv, ht * 128:ht * 128 + 128], inc=(ht == 1), w=(m,))
                R1[it["name"]] = a = act(hid[:, kv, :, :], pb[:, 0:120].rearrange("p (a b) -> p a b", a=2), w=(mt,))
                B.put(b, a)

            later.append((pe_units[0] + 2, transposes))
            return [m]

        def ev_v(it, banks, last):
            ms = [act(vt[:, tb, :], banks[tb], w=(last, rowA.m), scale=rowA.rs[:, tb:tb + 1]) for tb in range(2)]
            R1[it["name"]] = ms[-1]
            return ms

        def ev_thin(then):
            def ev(it, banks, last):
                n = it["nc"]
                m = act(thin[0:n, :], banks[0][0:n, 0:T], w=(last,))

                def go():
                    b = B.get()
                    pb = B.ap(b)
                    for tb in range(2):
                        mt = tp(pb[:, tb * 64:tb * 64 + n], thin[0:n, tb * 128:tb * 128 + 128], inc=(tb == 1), w=(m,))
                    B.put(b, *then(it, [pb[:, 0:64], pb[:, 64:128]], mt))

                later.append((pe_units[0] + 2, go))
                return [m]
            return ev

        def ev_g1(it, banks, last):
            ms = []
            for tb in range(2):
                m = act(gs[:, tb, :], banks[tb][:, 16:64], ACT.Sigmoid, w=(last, rowA.m), scale=rowA.rs[:, tb:tb + 1])
            for tb in range(2):
                ms.append(stt(dt[:, tb, :], banks[tb][:, 0:16], rowA.rs[:, tb:tb + 1], C("dtb"), MUL, ADD, w=(m,)))
            d32 = dt.rearrange("p a b -> p (a b)")
            R1["1g"] = V.last()

            def then(m):
                e = act(ec[:, 0:16], C("alog"), ACT.Exp)
                m = ts(ec[:, 0:16], ec[:, 0:16], -1.0, None, MUL, w=(e,))
                R1["dt"] = tt(aa, dt, bc(ec[:, 0:16], 1, [P, 2, 16]), MUL, w=(m,))

            softplus(d32, d32, 32, (V.last(),), False, then)
            return ms

        def ev_conv(it, banks, last):
            n = int(it["name"][-1])
            ms = []
            cw = C("convw")
            for b in range(2):
                ms.append(tt(CT[:, 2 * b:2 * b + 2, :], banks[b].rearrange("p (a b) -> p a b", a=2), RB2, MUL,
                             w=(last, R1["RB"], R1.get("tap0"))))
            first = [None] * 4

            def taps(j):
                if j < 4:
                    t = n * 4 + j
                    first[j] = R1["tap0"] = act(xT[:, t, :], CT[:, j, :], ACT.Identity, scale=cw[:, t * 4 + 3:t * 4 + 4],
                                                bias=C("convb")[:, t:t + 1], w=(ms[1],), own=False)
                if j > 0:
                    t = n * 4 + j - 1
                    o = xT[:, t, :]
                    for q in range(1, 4):
                        m = stt(o[:, q:T], CT[:, j - 1, 0:T - q], cw[:, t * 4 + 3 - q:t * 4 + 4 - q], o[:, q:T], MUL, ADD, w=(first[j - 1],))
                    if j == 4:
                        R1["taps", n] = m

            for j in range(5):
                later.append((pe_units[0] + 1 + j, lambda j=j: taps(j)))
            return ms

        def ev_z(it, banks, last):
            n = int(it["name"][-1])
            ms = [act(sz[:, tb, n * 512:n * 512 + 512], banks[tb], ACT.Silu, w=(last, rowA.m), scale=rowA.rs[:, tb:tb + 1]) for tb in range(2)]
            R1[it["name"]] = ms[-1]
            return ms

        xs = W_(2048, 2, 1024)
        xd = W_(11264, 2, 1024)
        ys = W_(13312, 2, 1024)
        xe = W_(15360, 1024)
        st = W_(16384, 2, 512)
        cbm = W_(17408, 4, 128)
        UA = W_(17920, 2, 4, 128)
        EE = W_(18944, 2, 4, 128)
        MM = W_(19968, 2, 4, 128)
        Bt = W_(20992, 256)

        def attention_T():
            R1["attended"] = marks = (V.last(), A.last(), E.last())
            yield
            for k in range(0, 8, 2):
                tiles_T("h", k, 1024 + k * 128, marks, prior=marks)
                yield

        def ssd():
            while ("taps", 2) not in R1:
                yield
            V.wait(*R1["attended"])
            A.wait(*R1["attended"])
            for t in range(0, 12, 4):
                m = act(xT[:, t:t + 4, :], xT[:, t:t + 4, :], ACT.Silu, w=(R1["taps", 2],), own=False)
            R1["1x2"] = m
            yield
            yield
            for tb in range(2):
                for q in range(2):
                    b = B.get()
                    pb = B.ap(b)
                    for j in range(4):
                        m = tp(pb[:, j * 128:j * 128 + 128], xT[:, 4 * q + j, tb * 128:tb * 128 + 128], inc=(j == 3), w=(R1["1x2"],))
                    a = act(xs[:, tb, q * 512:q * 512 + 512], pb, w=(m,))
                    B.put(b, a)
                yield
            b = B.get()
            pb = B.ap(b)
            for g in range(2):
                m = tp(pb[:, g * 128:g * 128 + 128], xT[:, 8 + g, 0:128], inc=(g == 1))
            mb = act(Bt, pb[:, 0:256], w=(m,))
            B.put(b, mb)
            for tb in range(2):
                mx = tt(xd[:, tb, :].rearrange("p (h d) -> p h d", h=16), xs[:, tb, :].rearrange("p (h d) -> p h d", h=16),
                        bc(dt[:, tb, :], 2, [P, 16, 64]), MUL, w=(a,))
            b = B.get()
            pb = B.ap(b)
            mm(pb[:, 0:16], C("OS")[:, 128:256], aa[:, 0, :], w=(R1["dt"],))
            m = mm(pb[:, 16:32], C("U"), aa[:, 1, :], inc=True)
            m = act(ec[:, 16:48], pb[:, 0:32], ACT.Exp, w=(m,))
            B.put(b, m)
            yield
            mxe = tt(xe.rearrange("p (h d) -> p h d", h=16), xd[:, 0, :].rearrange("p (h d) -> p h d", h=16),
                     bc(ec[:, 16:32], 2, [P, 16, 64]), MUL, w=(m, mx))
            yield
            for g in range(2):
                b = B.get()
                pb = B.ap(b)
                m = mm(pb, Bt[:, g * 128:g * 128 + 128], xe[:, g * 512:g * 512 + 512], inc=True, w=(mxe, mb))
                a = act(st[:, g, :], pb, w=(m,))
                B.put(b, a)
            yield
            for g in range(2):
                b = B.get()
                pb = B.ap(b)
                m = mm(pb, xT[:, 10 + g, 128:256], st[:, g, :], inc=True, w=(a,))
                m = tt(ys[:, 1, g * 512:g * 512 + 512].rearrange("p (h d) -> p h d", h=8), pb.rearrange("p (h d) -> p h d", h=8),
                       bc(ec[:, 32 + 8 * g:40 + 8 * g], 2, [P, 8, 64]), MUL, w=(m,))
                B.put(b, m)
            b = B.get()
            pb = B.ap(b)
            for c in range(2):
                for g in range(2):
                    m = mm(pb[:, (2 * c + g) * 128:(2 * c + g) * 128 + 128], xT[:, 8 + g, c * 128:c * 128 + 128],
                           xT[:, 10 + g, c * 128:c * 128 + 128], inc=(c == 1 and g == 1))
            mcb = tt(cbm, pb.rearrange("p (a b) -> p a b", a=4), bc(C("U"), 1, [P, 4, 128]), MUL, w=(m,))
            B.put(b, mcb)
            yield
            dsk = bc(C("dsk"), 2, [P, 16, 64])
            m = tt(xs[:, 1, :].rearrange("p (h d) -> p h d", h=16), xs[:, 1, :].rearrange("p (h d) -> p h d", h=16), dsk, MUL, w=(mx,))
            tt(ys[:, 1, :], ys[:, 1, :], xs[:, 1, :], ADD, w=(m,))
            my = tt(ys[:, 0, :].rearrange("p (h d) -> p h d", h=16), xs[:, 0, :].rearrange("p (h d) -> p h d", h=16), dsk, MUL)
            yield
            part = [(g, c, hq) for g in range(2) for c in range(2) for hq in range(2)]
            n = len(part)
            mu, seg, me, mk, va, obs, segb = {}, {}, {}, {}, {}, {}, {}
            for i in range(-1, n + 5):
                if 0 <= i - 1 < n:
                    j = i - 1
                    b = segb[j]
                    me[j] = act(EE[:, j % 2, :, :], B.ap(b).rearrange("p (a b) -> p a b", a=4), ACT.Exp, w=(seg[j], mk.get(j - 2)), own=False)
                    B.put(b, me[j])
                if 0 <= i < n:
                    b = B.get()
                    segb[i] = b
                    seg[i] = mm(B.ap(b), C("OS")[:, 128:256], UA[:, i % 2, :, :].rearrange("p a b -> p (a b)"), inc=True, w=(mu[i],))
                if i >= 4 and i - 4 < n and part[i - 4][2] == 1:
                    g, c, _ = part[i - 4]
                    yv = ys[:, c, g * 512:g * 512 + 512]
                    ob = obs.pop((g, c))
                    m = tt(yv, yv, B.ap(ob), ADD, w=(va[i - 4], my))
                    B.put(ob, m)
                    o = scr[:, c, g * 512:g * 512 + 512]
                    m = tt(o, yv, sz[:, c, g * 512:g * 512 + 512], MUL, w=(m, R1[f"1z{g}"]))
                    rowS.add(c, g, o, (m,))
                    if c == 1:
                        R1["yg", g] = m
                        if g == 1:
                            rowS.finish()
                if 0 <= i - 2 < n:
                    j = i - 2
                    g, c, _ = part[j]
                    mk[j] = tt(MM[:, j % 2, :, :], EE[:, j % 2, :, :], bc(cbm[:, 2 * c + g, :], 1, [P, 4, 128]), MUL,
                               w=(me[j], va.get(j - 2), mcb))
                if i + 1 < n:
                    g, c, hq = part[i + 1]
                    h0 = 8 * g + 4 * hq
                    mu[i + 1] = tt(UA[:, (i + 1) % 2, :, :], bc(C("U"), 1, [P, 4, 128]), bc(aa[:, c, h0:h0 + 4], 2, [P, 4, 128]), MUL,
                                   w=(seg.get(i - 1),))
                if 0 <= i - 3 < n:
                    j = i - 3
                    g, c, hq = part[j]
                    if hq == 0:
                        obs[g, c] = B.get()
                    for r in range(4):
                        hd = 8 * g + 4 * hq + r
                        va[j] = mm(B.ap(obs[g, c])[:, (4 * hq + r) * 64:(4 * hq + r) * 64 + 64], MM[:, j % 2, r, :],
                                       xd[:, c, hd * 64:hd * 64 + 64], inc=(r == 3), w=(mk[j], mx))
                if i in (8, 12):
                    g = i == 12
                    for k in range(4 * g, 4 * g + 4, 2):
                        tiles_T("h", 8 + k, k * 128, (R1["yg", g],), wcols=lambda kk: C("snw")[:, kk - 8:kk - 7], prior=(R1["yg", g],))
                yield

        S0 = 8192
        aq = W_(S0, 8, T)
        ab = W_(S0 + 2048, 8, T)
        ak = W_(S0 + 4096, 8, T)
        ai = W_(S0 + 6144, 2, 1024)
        AM = W_(S0 + 8192, 8, 128)
        A2 = W_(S0 + 9216, 4, 128)
        DD = W_(S0 + 9728, 4, T)
        QE = W_(S0 + 10752, 4, T)
        KE = W_(S0 + 11776, 4, T)
        assert S0 + 12800 <= WN - 512, WN
        sg = W_(0, 4, 4, CH)
        ones256 = C("OS")[:, 0:1].to_broadcast([P, T])
        lbt = small(3, 8)

        def lower_bounds():
            l0, l1 = C("lb0"), C("lb1")
            m = tt(lbt[:, 0, :], l0, l1, MAX)
            a = tt(lbt[:, 1, :], l0, lbt[:, 0, :], SUB, w=(m,))
            b = tt(lbt[:, 2, :], l1, lbt[:, 0, :], SUB, w=(m,))
            a = act(lbt[:, 1:3, :], lbt[:, 1:3, :], ACT.Exp, w=(b,))
            m = tt(lbt[:, 2, :], lbt[:, 1, :], lbt[:, 2, :], ADD, w=(a,))
            V.wait(m)
            m = vdo(lambda e: e.reciprocal(lbt[:, 2, :], lbt[:, 2, :]))
            m = tt(lbt[:, 0, :], lbt[:, 1, :], lbt[:, 2, :], MUL, w=(m,))
            m = ts(lbt[:, 1, :], lbt[:, 0, :], -1.0, 1.0, MUL, ADD, w=(m,))
            A.wait(m)

        def ev_af(it, banks, last):
            n = int(it["name"][-1])
            ms = []
            for b in range(2):
                t = n * 4 + 2 * b
                ms.append(tt(ab[:, t:t + 2, :], banks[b].rearrange("p (a b) -> p a b", a=2), RB2, MUL, w=(last, R1["RB"])))
            t = n * 4
            R1[it["name"]] = None

            def first():
                act(ak[:, t:t + 4, :], ab[:, t:t + 4, :], ACT.Sigmoid, scale=-1.0, w=(ms[-1],), own=False)
                R1["sg"] = act(ab[:, t:t + 4, :], ab[:, t:t + 4, :], ACT.Sigmoid)

            def second():
                for q in range(t, t + 4):
                    R1["lnf", q] = act(ab[:, q, :], ab[:, q, :], ACT.Ln, scale=lbt[:, 1, q:q + 1], bias=lbt[:, 0, q:q + 1], w=(R1["sg"],), own=False)
                for q in range(t, t + 4):
                    ts(ak[:, q, :], ak[:, q, :], lbt[:, 1, q:q + 1], None, MUL, w=(R1["sg"],))

            def scans(q0):
                def go():
                    for q in (q0, q0 + 1):
                        V.wait(R1["lnf", q])
                        R1[it["name"]] = vdo(lambda e, q=q: e.tensor_tensor_scan(ab[:, q, :], ones256, ab[:, q, :], 0.0, MUL, ADD))
                return go

            for i, f in enumerate((first, second, scans(t), scans(t + 2))):
                later.append((pe_units[0] + 1 + i, f))
            return ms

        def ev_t1024(dst, func=ACT.Copy):
            def ev(it, banks, last):
                n = int(it["name"][-1])
                ms = [act(dst[:, tb, n * 512:n * 512 + 512], banks[tb], func, w=(last, R1["rsB"]), scale=rsB[:, tb:tb + 1]) for tb in range(2)]
                R1[it["name"]] = ms[-1]
                return ms
            return ev

        def ev_ga(which):
            def ev(it, banks, last):
                n = int(it["name"][-1])
                ms = []
                for tb in range(2):
                    o = W[:, which * 4096 + n * 1024 + tb * 512:which * 4096 + n * 1024 + tb * 512 + 512]
                    ms.append(act(o, banks[tb], ACT.Sigmoid, w=(last, R1["rsB"], R1["fox"] if which else None), scale=rsB[:, tb:tb + 1]))
                R1[it["name"]] = ms[-1]
                return ms
            return ev

        rsB = small(2)
        gsil = scr[:, :, 1024:2048]

        def hgrn():
            E.wait(R1["2ai1"])
            for hg in range(2):
                h0 = 4 * hg
                vdo(lambda e: e.memset(AM, 0.0), w=(E.last() if hg == 0 else m,))
                seq = [0, 128] + LEVELS
                mE = None

                def decay(m_):
                    nb = T // (2 * m_)
                    bv = ab[:, h0:h0 + 4, :].rearrange("p h (n s m) -> p (h n) s m", s=2, m=m_)
                    dv = DD.rearrange("p h (n s m) -> p (h n) s m", s=2, m=m_)
                    anc = bv[:, :, 0, m_ - 1].unsqueeze(2).to_broadcast([P, 4 * nb, m_])
                    tt(dv[:, :, 1, :], bv[:, :, 1, :], anc, SUB, w=(R1["2af1"], R1["2aq1"]))
                    md = tt(dv[:, :, 0, :], anc, bv[:, :, 0, :], SUB, own=False) if m_ > 1 else V.last()
                    return md

                def factors(m_, mp):
                    def v(ap):
                        return ap.rearrange("p h (n s m) -> p (h n) s m", s=2, m=m_)

                    mq = tt(v(QE)[:, :, 1, :], v(aq[:, h0:h0 + 4, :])[:, :, 1, :], v(DD)[:, :, 1, :], MUL, w=(mE, mp))
                    if m_ == 1:
                        return mq
                    return tt(v(KE)[:, :, 0, :], v(ak[:, h0:h0 + 4, :])[:, :, 0, :], v(DD)[:, :, 0, :], MUL, own=False)

                me = R1["2aq1"]
                for li, m_ in enumerate(seq):
                    ql = QE if m_ else aq[:, h0:h0 + 4, :]
                    kl = KE if m_ > 1 else ak[:, h0:h0 + 4, :]
                    if m_ == 128:
                        bs = [B.get()]
                        pb = B.ap(bs[0])
                        for r in range(4):
                            m = mm(pb[:, r * 128:r * 128 + 128], kl[:, r, 0:128], ql[:, r, 128:256], inc=(r == 3), w=(me,))
                    else:
                        bs = [B.get(), B.get()]
                        for c in range(2):
                            pb = B.ap(bs[c])
                            for r in range(4):
                                m = mm(pb[:, r * 128:r * 128 + 128], kl[:, r, c * 128:c * 128 + 128], ql[:, r, c * 128:c * 128 + 128],
                                       inc=(r == 3 and c == 1), w=(me,))
                    if li + 1 < len(seq):
                        md = decay(seq[li + 1])
                    yield
                    if li + 1 < len(seq):
                        mE = act(DD, DD, ACT.Exp, w=(md,))
                    if m_ == 128:
                        B.put(bs[0], vcopy(A2, B.ap(bs[0]).rearrange("p (a b) -> p a b", a=4), w=(m,)))
                    else:
                        lix = 0 if m_ == 0 else 1 + LEVELS.index(m_)
                        mask = C("lev")[:, lix * 128:lix * 128 + 128].bitcast(I32)
                        for c in range(2):
                            pb = B.ap(bs[c])
                            B.put(bs[c], vdo(lambda e, c=c, pb=pb, mask=mask: e.copy_predicated(
                                AM[:, 4 * c:4 * c + 4, :], bc(mask, 1, [P, 4, 128]), pb.rearrange("p (a b) -> p a b", a=4)), w=(m,)))
                    yield
                    if li + 1 < len(seq):
                        me = factors(seq[li + 1], m)
                        yield
                ma = V.last()
                bs = []
                for c in range(2):
                    b = B.get()
                    bs.append(b)
                    pb = B.ap(b)
                    for r in range(4):
                        hd = h0 + r
                        o = pb[:, r * 128:r * 128 + 128]
                        m = mm(o, AM[:, 4 * c + r, :], ai[:, c, hd * 128:hd * 128 + 128], start=True, stop=(c == 0), w=(ma,),
                               inc=(r == 3 and c == 0))
                        if c == 1:
                            m = mm(o, A2[:, r, :], ai[:, 0, hd * 128:hd * 128 + 128], start=False, stop=True, inc=(r == 3))
                yield
                for c in range(2):
                    pb = B.ap(bs[c])
                    pv = pb.rearrange("p (h d) -> p h d", h=4)
                    sq = DD.rearrange("p a b -> p (a b)")[:, 512 * c:512 * c + 512].rearrange("p (h d) -> p h d", h=4)
                    t4 = t16a[:, 4 * c:4 * c + 4]
                    a = act(sq, pv, ACT.Square, w=(m, V.last()))
                    vdo(lambda e, t4=t4, sq=sq: e.reduce_sum(t4, sq, AX), w=(a,))
                    m2 = ts(t4, t4, 1.0 / 128, EPS, MUL, ADD)
                    m2 = act(t4, t4, ACT.Sqrt, w=(m2,))
                    vdo(lambda e, t4=t4: e.reciprocal(t4, t4), w=(m2,))
                    o = scr[:, c, h0 * 128:h0 * 128 + 512].rearrange("p (h d) -> p h d", h=4)
                    B.put(bs[c], tt(o, pv, bc(t4, 2, [P, 4, 128]), MUL))
                    R1[f"o{hg}{c}"] = V.last()
                    yield
            for c in range(2):
                R1["oa"] = tt(scr[:, c, 0:1024], scr[:, c, 0:1024], gsil[:, c, :], MUL, w=(R1["2ag1"],))
                yield

        bq = h[:, 0, :].rearrange("p (a b) -> p a b", a=8)
        bk = h[:, 1, :].rearrange("p (a b) -> p a b", a=8)
        bv_ = W_(6144, 2, 1024)
        lf = small(2, 8)
        LUs = [W_(S0 + 8192 + 1024 * i, 2, 4, 128) for i in range(2)]
        assert sm_at[0] <= 1280

        def ev_bf(it, banks, last):
            ms = []
            for tb in range(2):
                ms.append(stt(lf[:, tb, :], banks[tb][:, 0:8], rsB[:, tb:tb + 1], C("bfox"), MUL, ADD, w=(last, R1["rsB"])))
            l16 = lf.rearrange("p a b -> p (a b)")
            softplus(l16, l16, 16, (ms[-1],), True, lambda m: R1.update({"2bf": m}))
            return ms

        foxw = [W_(S0 + 10240 + 512 * i, 512) for i in range(6)]

        def fox():
            nonlocal SXs, PMs, PTs
            while "2bf" not in R1:
                yield
            SXs, PMs, PTs = foxw[0:2], foxw[2:4], foxw[4:6]
            E.wait(R1["2bv1"], R1["2bk1"])
            A.wait(R1["oa"])
            V.wait(A.last())
            tasks = []

            def task(tb, h0, nh, first, lastt):
                Kn, nb = 128 * (tb + 1), tb + 1
                LU = LUs[len(tasks) % 2]
                L0 = LU[:, 0, 0:nh, :]
                L1 = LU[:, 1, 0:nh, :]
                lu = []

                def prep(free):
                    m = tt(L0, bc(C("U"), 1, [P, nh, 128]), bc(lf[:, tb, h0:h0 + nh], 2, [P, nh, 128]), MUL, w=(free, R1["2bf"]))
                    if tb:
                        m = tt(L1, bc(ones, 1, [P, nh, 128]), bc(lf[:, 0, h0:h0 + nh], 2, [P, nh, 128]), MUL)
                    lu.append(m)

                def scores(pb):
                    for r in range(nh):
                        o = pb[:, r * Kn:r * Kn + Kn]
                        mm(o, bq[:, h0 + r, tb * 128:tb * 128 + 128], bk[:, h0 + r, 0:Kn], start=True, stop=False)
                        if tb:
                            mm(o[:, 0:128], LU[:, 1, r, :], C("OS")[:, 128:256], start=False, stop=False, w=lu)
                        m = mm(o, LU[:, 0, r, :], C("OS")[:, 256 - Kn:256], start=False, stop=True, inc=(r == nh - 1), w=lu)
                    return m

                def values(po, pt):
                    for r in range(nh):
                        for kb in range(nb):
                            c = ((h0 + r) % 4) * 128
                            q = r * nb + kb
                            m = mm(po[:, c:c + 128], pt[:, q * 128:q * 128 + 128], bv_[:, kb, (h0 + r) * 128:(h0 + r) * 128 + 128],
                                   start=(kb == 0), stop=(kb == nb - 1), inc=(r == nh - 1 and kb == nb - 1))
                    return m

                t = dict(Kn=Kn, nh=nh, scale=1.0, prep=prep, scores=scores, values=values, new=first)
                if lastt:
                    n0, hq = len(tasks) + 1 - 4 // nh, h0 // 4

                    def fin(po, pv, pm):
                        w4 = wgt[:, 0:4].rearrange("p (a b) -> p a b", b=nh)
                        z4 = zsum[:, n0:n0 + 4 // nh, 0:nh]
                        vdo(lambda e: e.reciprocal(w4, z4), w=(pm, R1["oa"]))
                        o = scr[:, tb, 1024 + hq * 512:1024 + hq * 512 + 512].rearrange("p (h d) -> p h d", h=4)
                        R1["fox"] = tt(o, po.rearrange("p (h d) -> p h d", h=4), bc(wgt[:, 0:4], 2, [P, 4, 128]), MUL, w=(pv,))
                    t["fin"] = fin
                tasks.append(t)

            for hq in range(2):
                task(0, 4 * hq, 4, True, True)
            for hq in range(2):
                for r in range(2):
                    task(1, 4 * hq + 2 * r, 2, r == 0, r == 1)
            yield from attend(tasks)

        def ev_ua(it, banks, last):
            n = int(it["name"][-1])
            ms = []
            for tb in range(2):
                s_ = W[:, n * 1024 + tb * 512:n * 1024 + tb * 512 + 512]
                ms.append(tt(s_, s_, banks[tb], MUL, w=(last, R1[f"2ga{n}"])))
            return ms

        def ev_ub(it, banks, last):
            n = int(it["name"][-1])
            ms = []
            for tb in range(2):
                sa = W[:, n * 1024 + tb * 512:n * 1024 + tb * 512 + 512]
                s_ = W[:, 4096 + n * 1024 + tb * 512:4096 + n * 1024 + tb * 512 + 512]
                o = scr[:, tb, n * 512:n * 512 + 512]
                m = tt(s_, s_, banks[tb], MUL, w=(last, R1[f"2gb{n}"]))
                ms.append(m)
                R1[f"mg{n}"] = tt(o, s_, sa, ADD, w=(m, R1["o_T"]))

            def transposes():
                for j in range(0, 4, 2):
                    tiles_T("h", 4 * n + j, n * 512 + j * 128, (R1[f"mg{n}"],), prior=(R1[f"mg{n}"],))

            later.append((pe_units[0] + 2, transposes))
            return ms

        def ev_acc(dst, add, row=None):
            def ev(it, banks, last):
                n = int(it["name"][-1])
                ms = []
                for tb in range(2):
                    o = dst[:, tb, n * 512:n * 512 + 512]
                    ms.append(tt(o, o, banks[tb], ADD, w=(last,)) if add else act(o, banks[tb], w=(last,)))
                    if row is not None:
                        row.add(tb, n, o, (ms[-1],))
                R1["acc"] = ms[-1]
                if add:
                    V.wait(ms[-1])
                return ms
            return ev

        def ev_os(it, banks, last):
            n = int(it["name"][-1])
            ms = []
            for tb in range(2):
                o = h[:, tb, n * 512:n * 512 + 512]
                ms.append(stt(o, banks[tb], rowS.rs[:, tb:tb + 1], o, MUL, ADD, w=(last, rowS.m)))
            chunk_T(n, ms[-1], rowF, "fnw")
            return ms

        def chunk_T(n, m, row, wname, src=h, delay=1, prior=None):
            wcol = C(wname) if isinstance(wname, str) else wname

            def go():
                for j in range(0, 4, 2):
                    tiles_T("x", 4 * n + j, n * 512 + j * 128, (m,), wcols=lambda k: wcol[:, k:k + 1], prior=(prior or m,), src=src)
                for tb in range(2):
                    row.add(tb, n, src[:, tb, n * 512:n * 512 + 512], (m,))
                if n == 3:
                    row.finish()
            if delay:
                later.append((pe_units[0] + delay, go))
            else:
                go()

        rowA, rowS, rowF, rowX, rowY, rowP, rowZ = Row(D, 4), Row(1024, 2), Row(D, 4), Row(D, 4), Row(D, 4), Row(D, 4), Row(D, 4)
        rowG = Row(D, 4)
        fwn = small(16)

        xt = scr[:, :, :].rearrange("p a b -> p (a b)").rearrange("p (k t) -> p k t", k=KT)
        def load(sem_, o, i):
            S.queue.append((lambda e: e.dma_start(o, i).then_inc(sem_, 16), False))

        pieces = [(0, 2), (2, 4), (4, 8), (8, 12), (12, 16)]
        s_xt = [sem(f"s_xt{i}") for i in range(5)]

        def load_xt(i):
            a, z = pieces[i]
            load(s_xt[i], xt[:, a:z, :], ins["xT"][:, a:z, :])

        vdo(lambda e: e.memset(junk[:, 0:1], 1.0))
        warm(junk[:, 0:1], (V.last(),))
        load(s_c, cst[:, 0:NPAR], ins["cst"][:, 0:NPAR])
        load_xt(0)
        pump_dma(1)
        load_xt(1)
        pump_dma(2)
        load_xt(2)
        pump_dma(4)
        load_xt(3)
        pump_dma(5)
        load_xt(4)
        A.wait((s_c, 16))
        V.wait((s_c, 16))

        def x_tiles(q):
            for k in range(*pieces[q]):
                w = C("anw")[:, k:k + 1]
                hi = act(xhi[:, k, :], xt[:, k, :], w=((s_xt[q], 16),), scale=w, own=False)
                lo = stt(xlo[:, k, :], xt[:, k, :], w, xhi[:, k, :].bitcast(F), MUL, SUB, w=(hi, (s_xt[q], 16)), own=False)
                opnd_ready["x"][k] = (hi, lo)

        def start_side():
            yield
            x_tiles(2)
            yield
            x_tiles(3)
            yield
            for tb in range(2):
                load(s_x, h[:, tb, :], ins["x"][tb])
            x_tiles(4)
            yield
            load(s_k, cst[:, NPAR:], ins["cst"][:, NPAR:])
            for _ in range(2):
                yield
            for tb in range(2):
                for c in range(4):
                    rowA.add(tb, c, h[:, tb, c * 512:c * 512 + 512], ((s_x, 32),))
                    if c % 2:
                        yield
            rowA.finish()
            yield
            E.wait((s_k, 16))
            V.wait((s_k, 16))
            A.wait((s_k, 16))
            yield from spread(rowA.rs, (rowA.m,))
            yield

        x_tiles(0)
        pump_split(0)
        x_tiles(1)
        side = start_side()
        next(side)
        run(["1k"], ev_feat(kraw), side, defer=True)
        run(["1q0"], ev_feat(qf), side)
        for _ in side:
            pass
        assert not held
        run(["1q1"], ev_feat(qf), rope(kraw, kr, 4, (R1["1k"],)))
        run(["1v"], ev_v, rope(qf, qr, 8, (R1["1q1"],)))
        run(["1g"], ev_thin(ev_g1))
        att = attention1()
        run(["1c"], ev_feat(ckv), att)
        side = both(att, flatten())
        run(["1x0"], ev_conv, side)
        run(["1mk", "1mv"], ev_cmp, att)

        def second():
            yield from att
            yield from compressed()
            yield from attention_T()
            yield from ssd()

        side = second()
        run(["1x1", "1x2"], ev_conv, side)
        run(["1z0", "1z1"], ev_z, side)
        while opnd_ready["h"][7] is None:
            next(side)
        run([f"1oa{c}" for c in range(4)], ev_acc(h, True), side)
        before = (V.last(), A.last(), E.last())
        run([f"1os{c}" for c in range(4)], ev_os)
        mb = load_bcw(0, before)

        def done1(c, m):
            chunk_T(c, m, rowX, fwn)

        A.wait(tt(fwn, C("fnl"), C("nmp"), MUL))
        ffn(1, True, rowF, done1, before=before)
        lower_bounds()

        def x2():
            yield
            V.wait(mb)
            free = E.last()
            before = ()
            for tb in range(2):
                for c in range(4):
                    if before:
                        rowZ.add(*before)
                    o = h[:, tb, c * 512:c * 512 + 512]
                    m = stt(o, o, rowX.rs[:, tb:tb + 1], bcw[:, c * 512:c * 512 + 512], MUL, MUL, w=(rowX.m, free))
                    before = (tb, c, o, (m,))
                    yield
            rowZ.add(*before)
            yield
            m = rowZ.finish()
            R1["rsB"] = tt(rsB, rowZ.rs, rowX.rs, MUL)
            while not held:
                yield
            yield from spread(rsB, (R1["rsB"],))
            yield
            S.wait(m)
            S.queue.append((lambda e: e.dma_start(keep, h[:, :, :].rearrange("p a b -> p (a b)")).then_inc(s_keep, 16), False))

        keep = nc.dram_tensor("keep", (P, 2 * D), F, kind="Internal").ap()
        side = x2()
        run(["2af0"], ev_af, side, defer=True)
        run(["2af1"], ev_af, side)
        for _ in side:
            pass
        run(["2aq0", "2aq1"], ev_feat(aq))
        run(["2ai0", "2ai1"], ev_t1024(ai))
        V.wait((s_keep, 16))
        side = hgrn()
        run(["2ag0", "2ag1"], ev_t1024(gsil, ACT.Silu), side)
        run(["2bq0", "2bq1"], ev_feat(bq, 128.0 ** -0.5), side)
        run(["2bk0", "2bk1"], ev_feat(bk), side)
        run(["2bv0", "2bv1"], ev_t1024(bv_), side)
        run(["2bf"], ev_thin(ev_bf), side)
        side = chain(side, fox())
        run([f"2ga{c}" for c in range(4)], ev_ga(0), side)
        run([f"2gb{c}" for c in range(4)], ev_ga(1), side)
        xdone = E.last()

        def o_tiles():
            for k in range(0, 16, 2):
                if k < 8:
                    tiles_T("x", k, k * 128, (R1["oa"],), wcols=lambda kk: C("hnw"), prior=(xdone,))
                else:
                    R1["o_T"] = tiles_T("x", k, k * 128, (R1["fox"],), prior=(xdone,))
                if k:
                    yield
            S.wait(R1["o_T"])
            S.queue.append((lambda e: e.dma_start(h[:, :, :].rearrange("p a b -> p (a b)"), keep).then_inc(s_keep, 16), False))
            yield

        side = o_tiles()
        next(side)
        mb = load_bcw(1, [V.last(), A.last(), E.last()])
        run([f"2ua{c}" for c in range(4)], ev_ua, side)
        run([f"2ub{c}" for c in range(4)], ev_ub)
        before = (V.last(), A.last(), E.last())

        def ev_o(it, banks, last):
            c = int(it["name"][-1])
            ms = []
            for tb in range(2):
                rowY.add(tb, c, banks[tb], (last,))
            sq = rowY.m
            if c == 3:
                V.wait((s_keep, 32))
                rowY.finish()
                for tb in range(2):
                    R1["post0"] = post(0, rowY, tb)
            for tb in range(2):
                ms.append(tt(scr[:, tb, c * 512:c * 512 + 512], banks[tb], bcw[:, c * 512:c * 512 + 512], MUL, w=(sq, mb)))
            return ms

        def post(c, row, tb):
            y, o = scr[:, tb, c * 512:c * 512 + 512], h[:, tb, c * 512:c * 512 + 512]
            return stt(o, y, row.rs[:, tb:tb + 1], o, MUL, ADD, w=(row.m,), own=False)

        run(["2o0", "2o1"], ev_o)
        warm(ones[:, 0:1])
        run(["2o2", "2o3"], ev_o)
        mb2 = load_bcw(2, [V.last()])

        prior = E.last()

        def posts():
            m = R1["post0"]
            for c in range(4):
                chunk_T(c, m, rowP, "nfp", delay=0, prior=prior)
                if c < 3:
                    post(c + 1, rowY, 0)
                    m = post(c + 1, rowY, 1)
                yield
                if c:
                    yield

        def done2(c, m):
            for tb in range(2):
                rowG.add(tb, c, scr[:, tb, c * 512:c * 512 + 512], (m,))
            sq = rowG.m
            if c == 3:
                rowG.finish()
                for q in range(3):
                    send(q)
            for tb in range(2):
                y = scr[:, tb, c * 512:c * 512 + 512]
                tt(y, y, bcw[:, c * 512:c * 512 + 512], MUL, w=(sq, mb2))
            if c == 3:
                V.wait(V.last())
                send(3)

        def send(c):
            for tb in range(2):
                S.wait(post(c, rowG, tb))
                S.queue.append((lambda e, tb=tb: e.dma_start(out[tb][:, c * 512:c * 512 + 512], h[:, tb, c * 512:c * 512 + 512]).then_inc(s_out, 16), False))

        side = posts()
        next(side)
        ffn(2, False, rowP, done2, side=side, before=before)
        S.wait((s_out, 16 * 8))
        assert item_at[0] == len(items) and state["dma"] == len(units)

        with nc.Block() as block:
            @block.sync
            def _(e):
                S.play(e)

            @block.scalar
            def _(e):
                A.play(e)

            @block.vector
            def _(e):
                V.play(e)

            @block.tensor
            def _(e):
                E.play(e)


def constants():
    f = np.float32
    j = np.arange(128)
    c0 = OFF["ident"][0]
    c = np.zeros((128, NCST - c0), f)

    def put(name, a):
        o, w = OFF[name]
        c[:a.shape[0], o - c0:o - c0 + w] = a.reshape(a.shape[0], -1)

    put("ident", np.eye(128, dtype=f))
    put("U", (j[:, None] <= j[None, :]).astype(f))
    SU = (j[:, None] > j[None, :]).astype(f)
    put("OS", np.concatenate([np.ones((128, 128), f), SU], 1))
    d = j % 64
    perm = np.zeros((128, 128), f)
    for m in range(128):
        if d[m] < 8:
            perm[m + 8, m] = 1
        elif d[m] < 16:
            perm[m - 8, m] = 1
    put("perm", perm)
    put("cm", np.concatenate([np.zeros((128, 128), f), np.where(j[None, :] > j[:, None], f(NEG), f(0))], 1))
    lev = np.zeros((8, 128, 128), f)
    lev[0] = np.eye(128)
    for i, m in enumerate(LEVELS):
        s, t = j[:, None], j[None, :]
        lev[1 + i] = (s // (2 * m) == t // (2 * m)) & (s % (2 * m) < m) & (t % (2 * m) >= m)
    put("lev", lev.transpose(1, 0, 2).reshape(128, -1))
    inv = (f(1.0) / (f(500000.0) ** (np.arange(0, 16, 2, dtype=f) / f(16)))).astype(f)
    ang = (np.arange(T, dtype=f)[:, None] * inv[None, :]).astype(f)
    cos, sin = np.cos(ang).astype(f), np.sin(ang).astype(f)
    ct, st = np.ones((128, T), f), np.zeros((128, T), f)
    for m in range(128):
        if d[m] < 8:
            ct[m], st[m] = cos[:, d[m]], -sin[:, d[m]]
        elif d[m] < 16:
            ct[m], st[m] = cos[:, d[m] - 8], sin[:, d[m] - 8]
    put("cos", ct)
    put("sin", st)
    t = np.arange(T).reshape(2, 128)
    ok = (np.arange(15) * 16 + 31)[None, None, :] <= t[:, :, None]
    put("cadd", np.where(ok, f(0), f(-1e30)).transpose(1, 0, 2))
    put("cmul", ok.astype(f).transpose(1, 0, 2))
    put("bd", (np.arange(120)[:, None] // 15 == np.arange(8)[None, :]).astype(f))
    return c


def pack(w, chunks):
    k = w.shape[0]
    return np.ascontiguousarray(w.reshape(k // 256, 2, 128, chunks, CH).transpose(3, 0, 2, 1, 4)).reshape(chunks, k // 256, 128, 2 * CH)


def narrow(w):
    n = w.shape[1]
    return np.ascontiguousarray(w.reshape(16, 128, n).transpose(1, 0, 2)).reshape(1, 128, 16 * n)


def feat(v, n):
    return v.reshape(n, 128).T


def rep(v):
    return np.broadcast_to(v.reshape(1, -1), (128, v.size))


def kernel(**inputs):
    import concourse.bacc as bacc
    from concourse.bass_utils import run_bass_kernel_spmd

    a = {k: np.asarray(v) for k, v in inputs.items()}
    w = a["w_in"][0]
    z, xbc, dtr, q, kc, vc, ks, vs, kw, vw, gate = np.split(w, np.cumsum([1024, 1536, 16, 1024] + [256] * 6), axis=1)
    order = [h for i in range(2) for r in range(4) for h in (8 * i + r, 8 * i + 4 + r)]
    q = q.reshape(D, 16, 64)[:, order, :].reshape(D, 1024)
    w1 = np.concatenate([ks, kw, q, vs, vw, kc, vc, xbc, z], axis=1)
    w2 = a["w_in_2"][0]
    aq, af, ai, ag, bq, bk, bv, bf, ga, gb = np.split(w2, np.cumsum([1024] * 7 + [8, 2048]), axis=1)
    w2p = np.concatenate([af, aq, ai, ag, bq, bk, bv, ga, gb], axis=1)
    cw = a["conv_w"][0]
    cols = [feat(a["attn_norm_w"][0], 16), feat(a["ffn_norm_w"][0], 16), feat(a["ssd_norm_w"][0], 8),
            cw.reshape(4, 12, 128).transpose(2, 1, 0).reshape(128, 48), feat(a["conv_b"][0], 12)]
    for n in ("cmp_pe_k", "cmp_pe_v"):
        pe = a[n][0].T
        cols.append(np.concatenate([pe, pe], axis=0))
    cols += [feat(a["norm_mix_pre_2"][0], 16), feat(a["norm_ffn_pre_2"][0], 16), feat(a["hgrn_lb_logits_2"][0], 8),
             feat(a["hgrn_lb_logits_2"][1], 8), a["hgrn_norm_w_2"][0].reshape(128, 1), rep(a["dt_bias"][0]), rep(a["a_log"][0]),
             rep(a["d_skip"][0]), rep(a["b_fox_f_2"][0]), feat(a["final_norm_w"], 16)]
    npar = sum(c.shape[1] for c in cols)
    assert npar == NPAR
    k2 = a["cmp_w2_k"][0].reshape(2, 128, 64).transpose(1, 0, 2)
    v2 = a["cmp_w2_v"][0].reshape(2, 128, 64).transpose(1, 0, 2)
    cols += [np.concatenate([k2, k2], axis=2).reshape(128, 256), v2.reshape(128, 128)]
    cols.append(constants())
    arrays = {
        "x": a["x"].reshape(2, 128, D),
        "xT": a["x"].reshape(T, KT, 128).transpose(2, 1, 0),
        "cst": np.concatenate(cols, axis=1),
        "wb": np.stack([rep(a["final_norm_w"]), rep(a["norm_mix_post_2"][0]), rep(a["norm_ffn_post_2"][0])]),
        "w_in1": pack(w1, 10),
        "w_n1": narrow(np.concatenate([dtr, gate], axis=1)),
        "cmp1": np.stack([a[n][0].reshape(4, 4, 128, 256).transpose(0, 2, 1, 3).reshape(4, 128, 1024) for n in ("cmp_w1_k", "cmp_w1_v")]),
        "w_out1": pack(a["w_out"][0], 4),
        "gu1": np.stack([pack(a["w_gate"][0], NCH), pack(a["w_up"][0], NCH)]),
        "dn1": pack(a["w_down"][0], 4),
        "w_in2": pack(w2p, 22),
        "w_n2": narrow(bf),
        "w_up": np.stack([pack(a["w_up_a_2"][0], 4), pack(a["w_up_b_2"][0], 4)]),
        "w_o": pack(a["w_o_2"][0], 4),
        "gu2": np.stack([pack(a["w_ffn_in_2"][0][:, :FF], NCH), pack(a["w_ffn_in_2"][0][:, FF:], NCH)]),
        "dn2": pack(a["w_ffn_down_2"][0], 4),
    }
    arrays = {"in_" + k: np.ascontiguousarray(v) for k, v in arrays.items()}
    nc = bacc.Bacc("TRN2", target_bir_lowering=False, num_devices=1, dynamic_dma_scratch_size=1024)
    ins = {k[3:]: nc.dram_tensor(k, v.shape, mybir.dt.float32, kind="ExternalInput").ap() for k, v in arrays.items()}
    out = nc.dram_tensor("out_x", (2, 128, D), mybir.dt.float32, kind="ExternalOutput").ap()
    build(nc, ins, out)
    r = run_bass_kernel_spmd(nc, [arrays], core_ids=[0])
    return r.results[0]["out_x"].reshape(1, T, D)
```
